# Optimizing a Trainium2 kernel written in Bass

```python
import jax, jax.numpy as jnp
from jax import lax
import numpy as np

D_MODEL = 1024
BATCH = 1
SEQ = 256
DEPTH = 2

EPS = 1e-6
NEG_INF = -1e30
ROPE_BASE = 10000.0
MEM_LEN = 256
N_BRANCH = 3

RET_HEADS = 4
RET_QK_DIM = 128
RET_V_DIM = 128
RET_CHUNK = 128

MLA_HEADS = 8
MLA_NOPE_DIM = 64
MLA_ROPE_DIM = 32
MLA_V_DIM = 64
MLA_Q_RANK = 256
MLA_KV_RANK = 128
MLA_BLOCK = 128

SWA_HEADS = 8
SWA_KV_HEADS = 2
SWA_HEAD_DIM = 64
SWA_WINDOW = 128

REL_BUCKETS = 32
REL_MAX_DIST = 128

XA_HEADS = 4
XA_HEAD_DIM = 128

PEER_HEADS = 8
PEER_N_KEYS = 128
PEER_N_EXPERTS = PEER_N_KEYS * PEER_N_KEYS
PEER_D_KEY = 128
PEER_TOPK = 16
PEER_TOKEN_BLOCK = 128

IN_SPLITS = (
    RET_HEADS * RET_QK_DIM, RET_HEADS * RET_QK_DIM, RET_HEADS * RET_V_DIM, RET_HEADS * RET_V_DIM,
    MLA_Q_RANK, MLA_KV_RANK, MLA_ROPE_DIM,
    SWA_HEADS * SWA_HEAD_DIM, SWA_KV_HEADS * SWA_HEAD_DIM, SWA_KV_HEADS * SWA_HEAD_DIM,
    N_BRANCH * D_MODEL,
)
W_IN_COLS = sum(IN_SPLITS)

kernel_name = "hybrid_ret_mla_swa_peer_trunk"

def rms_norm(x, g=None):
    x32 = x.astype(jnp.float32)
    y = x32 * lax.rsqrt(jnp.mean(x32 * x32, axis=-1, keepdims=True) + EPS)
    if g is not None:
        y = y * g.astype(jnp.float32)
    return y.astype(x.dtype)

def rope(t, positions):
    half = t.shape[-1] // 2
    inv_freq = jnp.power(ROPE_BASE, -jnp.arange(half, dtype=jnp.float32) / half)
    ang = positions.astype(jnp.float32)[:, None] * inv_freq[None, :]
    cos = jnp.cos(ang)[None, :, None, :]
    sin = jnp.sin(ang)[None, :, None, :]
    t32 = t.astype(jnp.float32)
    t1, t2 = t32[..., :half], t32[..., half:]
    return jnp.concatenate([t1 * cos - t2 * sin, t2 * cos + t1 * sin], axis=-1).astype(t.dtype)

def retention(q, k, v, g, positions):
    out_dtype = q.dtype
    B, S, H, dk = q.shape
    dv = v.shape[-1]
    C = RET_CHUNK
    NC = S // C
    q = rope(q, positions).astype(jnp.float32)
    k = rope(k, positions).astype(jnp.float32) * (dk ** -0.5)
    v = v.astype(jnp.float32)
    log_gamma = jnp.log(1.0 - jnp.exp2(-5.0 - jnp.arange(H, dtype=jnp.float32)))
    qc = q.reshape(B, NC, C, H, dk)
    kc = k.reshape(B, NC, C, H, dk)
    vc = v.reshape(B, NC, C, H, dv)
    idx = jnp.arange(C, dtype=jnp.float32)
    diff = idx[:, None] - idx[None, :]
    intra_decay = jnp.where(diff >= 0, jnp.exp(log_gamma[:, None, None] * jnp.maximum(diff, 0.0)), 0.0)
    scores = jnp.einsum('bnihd,bnjhd->bnhij', qc, kc) * intra_decay
    inner = jnp.einsum('bnhij,bnjhe->bnihe', scores, vc)
    key_w = jnp.exp(log_gamma[None, :] * (C - 1.0 - idx)[:, None])
    chunk_kv = jnp.einsum('bnjhd,jh,bnjhe->nbhde', kc, key_w, vc)
    chunk_decay = jnp.exp(log_gamma * C)[None, :, None, None]

    def step(state, kv):
        return chunk_decay * state + kv, state

    _, prev_state = lax.scan(step, jnp.zeros((B, H, dk, dv), jnp.float32), chunk_kv)
    query_w = jnp.exp(log_gamma[None, :] * (idx + 1.0)[:, None])
    cross = jnp.einsum('bnihd,nbhde->bnihe', qc, prev_state) * query_w[None, None, :, :, None]
    y = rms_norm(inner + cross)
    y = y * jax.nn.silu(g.astype(jnp.float32)).reshape(B, NC, C, H, dv)
    return y.reshape(B, S, H * dv).astype(out_dtype)

def mla(qa, kva, kr, q_norm_g, w_qb, kv_norm_g, w_kvb, positions):
    B, S, _ = qa.shape
    H, NOPE, R, V, BLK = MLA_HEADS, MLA_NOPE_DIM, MLA_ROPE_DIM, MLA_V_DIM, MLA_BLOCK
    q = (rms_norm(qa, q_norm_g) @ w_qb).reshape(B, S, H, NOPE + R)
    q_nope = q[..., :NOPE]
    q_rope = rope(q[..., NOPE:], positions)
    kv = (rms_norm(kva, kv_norm_g) @ w_kvb).reshape(B, S, H, NOPE + V)
    k_nope, v = kv[..., :NOPE], kv[..., NOPE:]
    k_rope = rope(kr[:, :, None, :], positions)[:, :, 0, :]
    scale = (NOPE + R) ** -0.5
    nb = S // BLK
    qn_b = q_nope.reshape(B, nb, BLK, H, NOPE).transpose(1, 0, 2, 3, 4)
    qr_b = q_rope.reshape(B, nb, BLK, H, R).transpose(1, 0, 2, 3, 4)
    key_pos = jnp.arange(S)

    def block(args):
        qn, qr, b = args
        s = jnp.einsum('bqhd,bkhd->bhqk', qn, k_nope) + jnp.einsum('bqhr,bkr->bhqk', qr, k_rope)
        s = s.astype(jnp.float32) * scale
        qpos = b * BLK + jnp.arange(BLK)
        causal = key_pos[None, :] <= qpos[:, None]
        p = jax.nn.softmax(jnp.where(causal, s, NEG_INF), axis=-1)
        return jnp.einsum('bhqk,bkhe->bqhe', p.astype(v.dtype), v)

    out = lax.map(block, (qn_b, qr_b, jnp.arange(nb)))
    return out.transpose(1, 0, 2, 3, 4).reshape(B, S, H * V)

def t5_causal_buckets(rel):
    n = np.maximum(rel, 0)
    max_exact = REL_BUCKETS // 2
    large = max_exact + (np.log(np.maximum(n, 1) / max_exact) / np.log(REL_MAX_DIST / max_exact)
                         * (REL_BUCKETS - max_exact)).astype(np.int32)
    large = np.minimum(large, REL_BUCKETS - 1)
    return np.where(n < max_exact, n, large).astype(np.int32)

def sliding_window_attention(q, k, v, sinks, rel_bias):
    B, S, Hq, d = q.shape
    Hkv = k.shape[2]
    G = Hq // Hkv
    W = SWA_WINDOW
    nb = S // W
    qb = q.reshape(B, nb, W, Hkv, G, d)

    def band(t):
        tb = t.reshape(B, nb, W, Hkv, d)
        prev = jnp.pad(tb, ((0, 0), (1, 0), (0, 0), (0, 0), (0, 0)))[:, :-1]
        return jnp.concatenate([prev, tb], axis=2)

    kb, vb = band(k), band(v)
    s = jnp.einsum('bnqhgd,bnkhd->bnhgqk', qb, kb).astype(jnp.float32) * (d ** -0.5)
    qi = np.arange(W)[:, None] + W
    kj = np.arange(2 * W)[None, :]
    rel = qi - kj
    bias = rel_bias[t5_causal_buckets(rel)]
    bias = bias.transpose(2, 0, 1).reshape(Hkv, G, W, 2 * W).astype(jnp.float32)
    in_window = (rel >= 0) & (rel < W)
    first_block = in_window & (kj >= W)
    valid = jnp.where((jnp.arange(nb) == 0)[:, None, None], first_block, in_window)
    s = jnp.where(valid[None, :, None, None], s + bias, NEG_INF)
    sink = sinks.astype(jnp.float32).reshape(Hkv, G)[None, None, :, :, None, None]
    m = jnp.maximum(jnp.max(s, axis=-1, keepdims=True), sink)
    e = jnp.exp(s - m)
    p = e / (jnp.sum(e, axis=-1, keepdims=True) + jnp.exp(sink - m))
    out = jnp.einsum('bnhgqk,bnkhd->bnqhgd', p.astype(v.dtype), vb)
    return out.reshape(B, S, Hq * d)

def memory_cross_attention(h, mem_n, w_q, w_kv, w_o):
    B, S, _ = h.shape
    M = mem_n.shape[1]
    q = (h @ w_q).reshape(B, S, XA_HEADS, XA_HEAD_DIM)
    kv = (mem_n @ w_kv).reshape(B, M, 2, XA_HEADS, XA_HEAD_DIM)
    k, v = kv[:, :, 0], kv[:, :, 1]
    s = jnp.einsum('bqhd,bkhd->bhqk', q, k).astype(jnp.float32) * (XA_HEAD_DIM ** -0.5)
    p = jax.nn.softmax(s, axis=-1)
    o = jnp.einsum('bhqk,bkhd->bqhd', p.astype(v.dtype), v).reshape(B, S, XA_HEADS * XA_HEAD_DIM)
    return o @ w_o

def peer_ffn(h, w_query, sub_keys, expert_u, expert_v):
    B, S, D = h.shape
    T = B * S
    H, K, NK, Tb = PEER_HEADS, PEER_TOPK, PEER_N_KEYS, PEER_TOKEN_BLOCK
    hf = h.reshape(T, D)
    q = (hf @ w_query).reshape(T, H, 2, PEER_D_KEY // 2)
    s = jnp.einsum('thpc,hpnc->thpn', q, sub_keys).astype(jnp.float32)
    top_s, top_i = lax.top_k(s, K)
    cand_s = (top_s[:, :, 0, :, None] + top_s[:, :, 1, None, :]).reshape(T, H, K * K)
    cand_i = (top_i[:, :, 0, :, None] * NK + top_i[:, :, 1, None, :]).reshape(T, H, K * K)
    best_s, best_pos = lax.top_k(cand_s, K)
    expert_idx = jnp.take_along_axis(cand_i, best_pos, axis=-1)
    gates = jax.nn.softmax(best_s, axis=-1)
    nt = T // Tb

    def block(args):
        xc, ic, gc = args
        u_sel = expert_u[ic]
        a = jnp.einsum('td,thkd->thk', xc, u_sel).astype(jnp.float32)
        act = (jax.nn.gelu(a, approximate=False) * gc).astype(xc.dtype)
        v_sel = expert_v[ic]
        return jnp.einsum('thk,thkd->td', act, v_sel)

    out = lax.map(block, (hf.reshape(nt, Tb, D), expert_idx.reshape(nt, Tb, H, K), gates.reshape(nt, Tb, H, K)))
    return out.reshape(B, S, D)

def setup_inputs(seed: int = 0) -> dict:
    key = jax.random.key(seed)
    ks = jax.random.split(key, 32)
    f32 = jnp.float32
    L, D = DEPTH, D_MODEL

    def nrm(k, shape, scale):
        return jax.random.normal(k, shape, f32) * scale

    def gain(k, shape):
        return 1.0 + 0.02 * jax.random.normal(k, shape, f32)

    ret_w = RET_HEADS * RET_V_DIM
    mla_w = MLA_HEADS * MLA_V_DIM
    swa_w = SWA_HEADS * SWA_HEAD_DIM
    xa_w = XA_HEADS * XA_HEAD_DIM
    return {
        "x": nrm(ks[0], (BATCH, SEQ, D), 1.0),
        "mem": nrm(ks[1], (BATCH, MEM_LEN, D), 1.0),
        "rel_bias": nrm(ks[2], (REL_BUCKETS, SWA_HEADS), 0.5),
        "g_mix": gain(ks[3], (L, D)),
        "w_in": nrm(ks[4], (L, D, W_IN_COLS), D ** -0.5),
        "mla_q_norm": gain(ks[5], (L, MLA_Q_RANK)),
        "w_mla_qb": nrm(ks[6], (L, MLA_Q_RANK, MLA_HEADS * (MLA_NOPE_DIM + MLA_ROPE_DIM)), MLA_Q_RANK ** -0.5),
        "mla_kv_norm": gain(ks[7], (L, MLA_KV_RANK)),
        "w_mla_kvb": nrm(ks[8], (L, MLA_KV_RANK, MLA_HEADS * (MLA_NOPE_DIM + MLA_V_DIM)), MLA_KV_RANK ** -0.5),
        "swa_sinks": nrm(ks[9], (L, SWA_HEADS), 0.5),
        "w_branch_ret": nrm(ks[10], (L, ret_w, D), ret_w ** -0.5),
        "w_branch_mla": nrm(ks[11], (L, mla_w, D), mla_w ** -0.5),
        "w_branch_swa": nrm(ks[12], (L, swa_w, D), swa_w ** -0.5),
        "w_out": nrm(ks[13], (L, D, D), 0.5 * D ** -0.5),
        "g_xattn": gain(ks[14], (L, D)),
        "g_mem": gain(ks[15], (L, D)),
        "w_xq": nrm(ks[16], (L, D, xa_w), D ** -0.5),
        "w_xkv": nrm(ks[17], (L, D, 2 * xa_w), D ** -0.5),
        "w_xo": nrm(ks[18], (L, xa_w, D), 0.5 * xa_w ** -0.5),
        "g_ffn": gain(ks[19], (L, D)),
        "w_peer_query": nrm(ks[20], (L, D, PEER_HEADS * PEER_D_KEY), D ** -0.5),
        "peer_sub_keys": nrm(ks[21], (L, PEER_HEADS, 2, PEER_N_KEYS, PEER_D_KEY // 2), (PEER_D_KEY // 2) ** -0.5),
        "peer_u": nrm(ks[22], (L, PEER_N_EXPERTS, D), D ** -0.5),
        "peer_v": nrm(ks[23], (L, PEER_N_EXPERTS, D), 0.5 * PEER_HEADS ** -0.5),
        "g_final": gain(ks[24], (D,)),
    }

def reference(x, mem, rel_bias, g_mix, w_in, mla_q_norm, w_mla_qb, mla_kv_norm, w_mla_kvb,
              swa_sinks, w_branch_ret, w_branch_mla, w_branch_swa, w_out,
              g_xattn, g_mem, w_xq, w_xkv, w_xo,
              g_ffn, w_peer_query, peer_sub_keys, peer_u, peer_v, g_final):
    B, S, D = x.shape
    positions = jnp.arange(S)
    split_points = [int(p) for p in np.cumsum(IN_SPLITS)[:-1]]
    for l in range(DEPTH):
        h = rms_norm(x, g_mix[l])
        z = h @ w_in[l]
        rq, rk, rv, rg, qa, kva, kr, sq, sk, sv, gate_logits = jnp.split(z, split_points, axis=-1)
        y_ret = retention(rq.reshape(B, S, RET_HEADS, RET_QK_DIM), rk.reshape(B, S, RET_HEADS, RET_QK_DIM),
                          rv.reshape(B, S, RET_HEADS, RET_V_DIM), rg.reshape(B, S, RET_HEADS, RET_V_DIM), positions)
        y_mla = mla(qa, kva, kr, mla_q_norm[l], w_mla_qb[l], mla_kv_norm[l], w_mla_kvb[l], positions)
        y_swa = sliding_window_attention(sq.reshape(B, S, SWA_HEADS, SWA_HEAD_DIM),
                                         sk.reshape(B, S, SWA_KV_HEADS, SWA_HEAD_DIM),
                                         sv.reshape(B, S, SWA_KV_HEADS, SWA_HEAD_DIM),
                                         swa_sinks[l], rel_bias)
        gates = jax.nn.sigmoid(gate_logits.astype(jnp.float32)).astype(x.dtype).reshape(B, S, N_BRANCH, D)
        merged = (gates[:, :, 0] * (y_ret @ w_branch_ret[l])
                  + gates[:, :, 1] * (y_mla @ w_branch_mla[l])
                  + gates[:, :, 2] * (y_swa @ w_branch_swa[l]))
        x = x + merged @ w_out[l]
        x = x + memory_cross_attention(rms_norm(x, g_xattn[l]), rms_norm(mem, g_mem[l]), w_xq[l], w_xkv[l], w_xo[l])
        x = x + peer_ffn(rms_norm(x, g_ffn[l]), w_peer_query[l], peer_sub_keys[l], peer_u[l], peer_v[l])
    return rms_norm(x, g_final)


_drawn_inputs = setup_inputs


def setup_inputs(seed=0):
    import zlib

    import numpy as np

    out = dict(_drawn_inputs(seed))
    spreads = {}
    factors = {'g_mix': 3.362,
     'mla_q_norm': 8.0,
     'mla_kv_norm': 7.947,
     'swa_sinks': 8.0,
     'g_xattn': 8.0,
     'g_mem': 7.87,
     'g_ffn': 2.821,
     'g_final': 2.853}
    for name, (base, spread) in spreads.items():
        noise = np.random.default_rng([zlib.crc32(name.encode()), seed]).standard_normal(out[name].shape)
        drawn = base * np.exp(spread * noise) if base else spread * noise
        out[name] = __import__('jax').numpy.asarray(drawn.astype(out[name].dtype))
    for name, factor in factors.items():
        out[name] = (out[name] * factor).astype(out[name].dtype)
    return out
```

```python
from contextlib import ExitStack

import numpy as np
import concourse.bass as bass
from concourse import mybir

F32 = mybir.dt.float32
F32R = mybir.dt.float32r
U32 = mybir.dt.uint32
ALU = mybir.AluOpType
ACT = mybir.ActivationFunctionType
AXX = mybir.AxisListType.X

P = 128
D = 1024
DC = D // P
SEQ = 256
NT = SEQ // P
DEPTH = 2
EPS = 1e-6
NEG = -1e30
RH = 4
MH, NOPE, ROPE, MV = 8, 64, 32, 64
MQK = NOPE + ROPE
QR, KVR = 256, 128
SH, SKV, SD = 8, 2, 64
XH, XD = 4, 128
PH, TOPK, NK = 8, 16, 128
SLOTS = 4

TILES = {}


def _tiles():
    n = 0
    for name, count in (("rq", 4), ("rk", 4), ("rv", 4), ("sv", 1), ("qa", 2), ("kva", 1), ("kr", 1),
                        ("sq", 4), ("sk", 1), ("rg", 4), ("bias", 2), ("qb", 2), ("kvb", 1),
                        ("gate", 24), ("branch", 12), ("wo", 8), ("xk", 4), ("xv", 4), ("xq", 4),
                        ("xo", 4), ("pq", 8), ("keys", 1)):
        for i in range(count):
            TILES[name, i] = n
            n += 1
    return n


MIX_TILES = _tiles()
assert MIX_TILES % SLOTS == 0 and NK % SLOTS == 0
ROUNDS = (MIX_TILES + 2 * NK) // SLOTS
U_ROUND0 = MIX_TILES // SLOTS
V_ROUND0 = U_ROUND0 + NK // SLOTS
U_ROUNDS = NK // SLOTS

JOBS, JOB_ORDER = {}, []


def _jobs():
    def job(*name):
        JOBS[name] = len(JOB_ORDER)
        JOB_ORDER.append(name)

    for n in ("x0", "mem"):
        for t in range(NT):
            for half in range(2):
                job(n, t, half)
    ropes = [("rq", i) for i in range(4)] + [("rk", i) for i in range(4)]
    for i, r in enumerate(ropes):
        job(*r)
        if i:
            job("rot", *ropes[i - 1])
    job("rv", 0)
    job("rot", *ropes[-1])
    for i in range(1, 4):
        job("rv", i)
    for n in (("sv", 0), ("qa", 0), ("qa", 1), ("kva", 0), ("kr", 0), ("sq", 0), ("rot", "kr", 0), ("sq", 1),
              ("sq", 2), ("sq", 3), ("tqa", 0), ("tkv", 0), ("sk", 0), ("rg", 0), ("rg", 1), ("rg", 2), ("rg", 3)):
        job(*n)
    for h in range(MH):
        job("qb", h)
        job("kn", h)
        if h:
            job("rot", "qb", h - 1)
    job("mv", 0)
    job("rot", "qb", MH - 1)
    job("mv", 1)
    job("ty", 0)
    job("ty", 1)


def _late_jobs():
    def job(*name):
        JOBS[name] = len(JOB_ORDER)
        JOB_ORDER.append(name)

    for cg in range(4):
        for br in range(3):
            for m in range(2):
                job("branch", cg, br, m)
    for n in ("wo", "xk", "xv"):
        for i in range(4):
            job(n, i)
    for t in range(NT):
        for half in range(2):
            job("x1", t, half)
    for i in range(4):
        job("xq", i)


UNITS = [("swa", t, h) for t in range(NT) for h in range(SH)] + [("mla", t, h) for t in range(NT) for h in range(MH)]
MIX_UNITS = len(UNITS)
UNITS += [("xa", t, h) for t in range(NT) for h in range(XH)]
GROUPS = []
for _v, (_k, _t, _h) in enumerate(UNITS):
    if not GROUPS or GROUPS[-1][:2] != [_k, _t]:
        GROUPS.append([_k, _t, _v, _v])
    GROUPS[-1][3] = _v
LAG = 2
END_AT = {g[3] + LAG: n for n, g in enumerate(GROUPS)}
GATES = 3 * DC


def gates_at(step):
    return range(step * GATES // MIX_UNITS, (step + 1) * GATES // MIX_UNITS)


def mix_steps():
    return range(MIX_UNITS + LAG)


def xa_steps():
    return range(MIX_UNITS, len(UNITS) + LAG)


def _unit_jobs():
    def job(*name):
        JOBS[name] = len(JOB_ORDER)
        JOB_ORDER.append(name)

    for step in mix_steps():
        for g in gates_at(step) if step < MIX_UNITS else ():
            job("gate", g)
        if step - 1 in END_AT:
            job("ty", 2 + END_AT[step - 1])
    job("ty", 2 + 3)


def _xa_jobs():
    def job(*name):
        JOBS[name] = len(JOB_ORDER)
        JOB_ORDER.append(name)

    for step in xa_steps():
        if step - 1 in END_AT and END_AT[step - 1] >= 4:
            job("ty", 2 + END_AT[step - 1])
    job("ty", 2 + 5)
    for i in range(4):
        job("xo", i)
    for t in range(NT):
        for half in range(2):
            job("x2", t, half)
    for i in range(8):
        job("pq", i)
    for t in range(NT):
        for pair in range(PH // 2):
            for half in range(2):
                job("ps", t, pair, half)


_jobs()
_unit_jobs()
_late_jobs()
_xa_jobs()
ROPES = [("rq", i) for i in range(4)] + [("rk", i) for i in range(4)] + [("kr", 0)] + [("qb", h) for h in range(MH)]
NROPE = len(ROPES)
TILE_ENDS = {n: TILES[n] for n in JOB_ORDER if n in TILES and n[0] in
             ("rq", "rk", "rv", "sv", "qa", "kva", "kr", "sq", "sk", "rg", "gate", "xk", "xv", "xq", "pq")}
TILE_ENDS |= {("qb", 3): TILES["qb", 0], ("qb", 7): TILES["qb", 1], ("mv", 1): TILES["kvb", 0],
              ("wo", 3): TILES["wo", 7], ("xo", 3): TILES["xo", 3], ("ps", NT - 1, PH // 2 - 1, 1): TILES["keys", 0]}
TILE_ENDS |= {("branch", cg, br, 1): TILES["branch", cg * 3 + br] for cg in range(4) for br in range(3)}
PLAIN_JOBS = {n: k for k, n in enumerate(n for n in JOB_ORDER if n not in TILE_ENDS)}
GATE_OF = (0, 2, 1)
TURN_ROUND = 24
LEAST = -3.0e38
NJOBS = len(JOB_ORDER)
JOB_BANKS = 4
BANK_JOBS = [len(range(b, NJOBS, JOB_BANKS)) for b in range(JOB_BANKS)]

G_MIX, G_XA, G_MEM, G_FFN, G_Q, G_KV, SINKS = 0, 8, 16, 24, 32, 34, 35
NVEC = 43
C_ID, C_PERM, C_PERM96, C_IOTA = 0, 128, 256, 352
NCONST = 480
T_COS, T_SIN, T_COSM, T_SINM, T_DECAY, T_CAUSAL, T_WINDOW = 0, 256, 512, 768, 1024, 2048, 2304
NTAB = 2560


class Signal:

    def __init__(self, sem, per_layer, by=1, base=0):
        self.sem, self.per_layer, self.by, self.base = sem, per_layer, by, base

    def after(self, layer, events):
        return self.sem, (layer * self.per_layer + events) * self.by + self.base


def trunk(nc, mix_w, u_t, v_t, vecs, consts, tables, g_final, x_in, mem_in, out):
    ctx = ExitStack()
    with ctx:
        def sb(name, shape, dt=F32):
            return ctx.enter_context(nc.sbuf_tensor(name, shape, dt))

        def sig(name, per_layer=1, by=1, base=0):
            return Signal(ctx.enter_context(nc.semaphore(name)), per_layer, by, base)

        arena = sb("arena", [P, NK * SEQ])
        ring = sb("ring", [P, SLOTS, D])
        hi = sb("table_hi", [P, 2, D], F32R)
        lo = sb("table_lo", [P, 2, D], F32R)
        h_hi = sb("h_hi", [P, DC, SEQ], F32R)
        h_lo = sb("h_lo", [P, DC, SEQ], F32R)
        w_hi = sb("w_hi", [P, 2, SEQ], F32R)
        w_lo = sb("w_lo", [P, 2, SEQ], F32R)
        x = sb("x", [P, NT, D])
        hT = sb("hT", [P, DC, SEQ])
        chosen = sb("chosen", [P, 3, NT, P])
        cst = sb("cst", [P, NCONST])
        vec = sb("vec", [P, NVEC])
        stat = sb("stat", [P, 64])
        negmax = sb("negmax", [P, len(UNITS)])
        sums = sb("sums", [P, len(UNITS)])
        sinkexp = sb("sinkexp", [P, 2, 8])
        rden = sb("rden", [P, 2, 8])
        negsink = sb("negsink", [P, 8])[:, :]
        rowm = sb("rowm", [P, 2])
        rsum = sb("rsum", [P, 8])[:, :]
        i1col = sb("i1col", [P, 8])

        flat = arena[:, :]
        where = [0]

        def part(n, *dims):
            a = flat[:, where[0]:where[0] + n]
            where[0] += n
            if len(dims) == 2:
                return a.rearrange("p (a b) -> p a b", a=dims[0])
            if len(dims) == 3:
                return a.rearrange("p (a b c) -> p a b c", a=dims[0], b=dims[1])
            return a

        gates = part(3 * DC * SEQ, 3 * DC, SEQ)
        xn = flat[:, 0:2 * D].rearrange("p (t d) -> p t d", t=NT)
        junk = flat[:, 2 * D:3 * D].rearrange("p (t d) -> p t d", t=NT)
        rsq = flat[:, 0:D].rearrange("p (t d) -> p t d", t=NT)
        gfin = flat[:, 3 * D:4 * D]
        mem = part(2 * D, NT, D)
        merged = mem.rearrange("p t d -> p (t d)").rearrange("p (c s) -> p c s", c=DC)
        memT = part(2 * D, DC, SEQ)
        raw = part(2 * SEQ, 2, SEQ)
        cosx = part(2 * SEQ, 2, SEQ)
        sinx = part(2 * SEQ, 2, SEQ)
        at_q = where[0]
        rq = part(4 * SEQ, 4, SEQ)
        rk = part(4 * SEQ, 4, SEQ)
        mq = flat[0:MQK, at_q:at_q + MH * SEQ].rearrange("p (h s) -> p h s", h=MH)
        at_v = where[0]
        rv = part(NT * 512, NT, 512)
        mv = flat[:, at_v:at_v + NT * 512].rearrange("p (t s) -> p t s", t=NT)
        rgs = part(NT * 512, NT, 512)
        sgm = part(SEQ, NT, P)
        qk = part(NT * 384, NT, 384)
        qanT = part(2 * SEQ, 2, SEQ)
        kvanT = part(SEQ)
        krr = part(SEQ)
        mk = part(MH * SEQ, MH, SEQ)
        at_sw = where[0]
        swq = part(4 * SEQ, 4, SEQ)
        swk = part(2 * SEQ, 2, SEQ)
        sv = part(NT * P, NT, P)
        yT = part(3 * 4 * SEQ, 12, SEQ)
        ytok = part(NT * 512, NT, 512)
        tab = part(NTAB)
        bias = part(8 * SEQ, 8, SEQ)
        sm = part(2 * SEQ, 2, SEQ)
        prob = part(2 * SEQ, 2, SEQ)
        probT = part(2 * SEQ, 2, SEQ)
        retT = part(2 * 384, 2, 384)
        assert where[0] <= NK * SEQ, where[0]
        xk = flat[:, at_q:at_q + 4 * SEQ].rearrange("p (h s) -> p h s", h=4)
        xq = flat[:, at_q + 4 * SEQ:at_q + 8 * SEQ].rearrange("p (h s) -> p h s", h=4)
        xv = flat[:, at_v:at_v + NT * 512].rearrange("p (t s) -> p t s", t=NT)
        FREE_ROUNDS = 18
        where[0] = FREE_ROUNDS * SLOTS * SEQ
        pq = part(8 * SEQ, 8, SEQ)
        sc = part(NT * PH * 2 * NK, NT * PH * 2, NK)
        cand = part(PH * 256, PH, 256)
        onehot = part(PH * 256, PH * TOPK, TOPK)
        top = part(NT * PH * 2 * TOPK, NT * PH * 2, TOPK)
        topf = part(NT * PH * 2 * TOPK, NT * PH * 2, TOPK)
        topi = part(NT * PH * 2 * TOPK, NT * PH * 2, TOPK).bitcast(U32)
        best = part(NT * PH * TOPK, NT * PH, TOPK)
        besti = part(NT * PH * TOPK, NT * PH, TOPK).bitcast(U32)
        posi = part(2 * NT * PH * TOPK, 2, NT * PH * TOPK).bitcast(U32)
        posf = part(2 * NT * PH * TOPK, 2 * NT, PH * TOPK)
        bestmax = part(NT * PH).unsqueeze(2)
        bestsum = part(NT * PH)
        assert where[0] <= NK * SEQ, where[0]
        hflat = hT[:, :, :].rearrange("p c s -> p (c s)")
        chosenT = hflat[:, 0:3 * SEQ].rearrange("p (a s) -> p a s", a=3)
        oh1 = hflat[:, 768:768 + 512].rearrange("p (a b) -> p a b", a=4)
        oh2 = hflat[:, 1280:1280 + 512].rearrange("p (a b) -> p a b", a=4)
        pre = arena[:, :].rearrange("p (g s) -> p g s", g=NK)

        ident = cst[:, C_ID:C_ID + P]
        perm = cst[:, C_PERM:C_PERM + P]
        perm96 = cst[0:MQK, C_PERM96:C_PERM96 + MQK]
        iota = cst[:, C_IOTA:C_IOTA + P]
        cos, sin = tab[:, T_COS:T_COS + SEQ], tab[:, T_SIN:T_SIN + SEQ]
        cosm, sinm = tab[0:MQK, T_COSM:T_COSM + SEQ], tab[0:MQK, T_SINM:T_SINM + SEQ]
        decay = tab[:, T_DECAY:T_DECAY + 4 * SEQ].rearrange("p (h s) -> p h s", h=4)
        causal = tab[:, T_CAUSAL:T_CAUSAL + SEQ]
        window = tab[:, T_WINDOW:T_WINDOW + SEQ]

        bank = [ctx.enter_context(nc.psum_tensor(f"bank{b}", [P, 512], F32))[:, :] for b in range(8)]


        slot_full = [sig(f"slot_full{s}", ROUNDS, 16) for s in range(SLOTS)]
        slot_done = [sig(f"slot_done{s}", ROUNDS, base=1) for s in range(SLOTS)]
        job_full = sig("job_full", len(PLAIN_JOBS))
        job_stored = [sig(f"job_stored{b}", BANK_JOBS[b], base=1) for b in range(JOB_BANKS)]
        x_loaded = sig("x_loaded")
        cst_loaded = sig("cst_loaded")
        vec_loaded = sig("vec_loaded", 1, 16)
        tab_loaded = sig("tab_loaded", 1, 16)
        mem_loaded = sig("mem_loaded", 1, 16)
        squares = sig("squares", 8)
        meansq = sig("meansq", 4)
        root = sig("root", 4)
        rstd = sig("rstd", 4)
        normed = sig("normed", 8)
        raw_cos = sig("raw_cos", NROPE)
        roped = sig("roped", NROPE)
        kr_spread = sig("kr_spread")
        qk_sq = sig("qk_sq", 4)
        qk_ms = sig("qk_ms", 2)
        qk_root = sig("qk_root")
        qk_rstd = sig("qk_rstd")
        qk_normed = sig("qk_normed", 4)
        gate_sig = sig("gate_sig", 4)
        bias_ready = sig("bias_ready")
        score_full = sig("score_full", RH + len(UNITS))
        ret_scores = sig("ret_scores", RH)
        ret_full = sig("ret_full", RH)
        ret_stored = sig("ret_stored", RH)
        ret_sq = sig("ret_sq", NT)
        ret_sum = sig("ret_sum", NT)
        ret_ms = sig("ret_ms")
        ret_root = sig("ret_root")
        ret_rstd = sig("ret_rstd")
        ret_scaled = sig("ret_scaled", NT)
        ytok_ready = sig("ytok_ready", NT + len(GROUPS))
        masked = sig("masked", MIX_UNITS)
        rowmax = sig("rowmax", SH * NT)
        negmax_ready = sig("negmax_ready", len(UNITS))
        prob_ready = sig("prob_ready", len(UNITS))
        probT_full = sig("probT_full", len(UNITS))
        probT_ready = sig("probT_ready", len(UNITS))
        pv_done = sig("pv_done", len(UNITS))
        sink_shift = sig("sink_shift", NT)
        sink_exp = sig("sink_exp", NT)
        den_ready = sig("den_ready", NT)
        rden_ready = sig("rden_ready", len(GROUPS))
        gated = sig("gated", 16)
        peer_added = sig("peer_added", 4, base=1)
        sink_negated, best_top = sig("sink_negated"), sig("best_top")
        xa_max = sig("xa_max", XH * NT)
        settled = sig("settled")
        h_split = sig("h_split", 2)
        top1, top_idx1, top_cut, top2, top_idx2, top_float = (
            sig(n) for n in ("top1", "top_idx1", "top_cut", "top2", "top_idx2", "top_float"))
        cand_ready, best1, best_idx1, best_cut, best2, best_idx2 = (
            sig(n, NT) for n in ("cand_ready", "best1", "best_idx1", "best_cut", "best2", "best_idx2"))
        pos_split, pos_float = sig("pos_split"), sig("pos_float")
        onehot_ready, picked, index_ready = (sig(n, 2 * NT) for n in ("onehot_ready", "picked", "index_ready"))
        best_shift, best_exp, best_sum, best_rsum, choice_made = (
            sig(n) for n in ("best_shift", "best_exp", "best_sum", "best_rsum", "choice_made"))
        choice_turned = sig("choice_turned", 3)
        choiceT_ready = sig("choiceT_ready", 3)
        high_ready = [sig(f"high_ready{b}", NK) for b in range(2)]
        pair_used = [sig(f"pair_used{b}", NK, base=1) for b in range(2)]
        pre_stored = [sig(f"pre_stored{b}", NK // 4, base=1) for b in range(4)]
        i1_copied = sig("i1_copied", SEQ // 8)
        oh1_ready = [sig(f"oh1_ready{s}", SEQ // 4, base=1) for s in range(4)]
        oh2_ready = [sig(f"oh2_ready{s}", SEQ // 4) for s in range(4)]
        oh_used = [sig(f"oh_used{s}", SEQ // 4, base=1) for s in range(4)]
        spread_used = [sig(f"spread_used{b}", SEQ // 8, base=1) for b in range(2)]
        w_high = [sig(f"w_high{b}", NK // 2) for b in range(2)]
        w_low = [sig(f"w_low{b}", NK // 2) for b in range(2)]
        f_sq, f_ms, f_root, f_rstd, f_scaled, f_ready, gf_loaded, stored = (
            sig(n) for n in ("f_sq", "f_ms", "f_root", "f_rstd", "f_scaled", "f_ready", "gf_loaded", "stored"))

        def settle(eng):
            eng.sem_inc(settled.sem, 1)

        def start(eng, *signals):
            for signal in signals:
                eng.sem_inc(signal.sem, 1)

        def tile(name, i=0):
            return ring[:, TILES[name, i] % SLOTS, :]

        def loaded(layer, name, i=0):
            n = TILES[name, i]
            return slot_full[n % SLOTS].after(layer, n // SLOTS + 1)

        def bank_of(*name):
            return bank[JOBS[name] % JOB_BANKS]

        def bank_free(layer, *name):
            k = JOBS[name]
            return job_stored[k % JOB_BANKS].after(layer, k // JOB_BANKS)

        def ends(*name):
            if name in TILE_ENDS:
                return slot_done[TILE_ENDS[name] % SLOTS].sem, 1
            return job_full.sem, 1

        def full(layer, *name):
            if name in TILE_ENDS:
                n = TILE_ENDS[name]
                return slot_done[n % SLOTS].after(layer, n // SLOTS + 1)
            return job_full.after(layer, PLAIN_JOBS[name] + 1)

        def stores(*name):
            return job_stored[JOBS[name] % JOB_BANKS].sem, 1

        def in_sbuf(layer, *name):
            k = JOBS[name]
            return job_stored[k % JOB_BANKS].after(layer, k // JOB_BANKS + 1)

        block = ctx.enter_context(nc.Block())

        @block.sync
        def _(sp):
            start(sp, *slot_done, *job_stored, peer_added, *pair_used, *pre_stored, oh1_ready[3], *oh_used, *spread_used)
            for s in range(3):
                start(sp, oh1_ready[s])
            sp.dma_start(cst[:, :], consts).then_inc(cst_loaded.sem, 16)
            sp.dma_start(x[:, :, :], x_in).then_inc(x_loaded.sem, 16)
            with sp.Fori(0, DEPTH) as layer:
                with sp.Fori(0, U_ROUND0) as r:
                    for s in range(SLOTS):
                        sp.wait_ge(*slot_done[s].after(layer, r))
                        sp.dma_start(ring[:, s, :], mix_w[layer, r * SLOTS + s]).then_inc(slot_full[s].sem, 16)
                for table, first in ((u_t, U_ROUND0), (v_t, V_ROUND0)):
                    with sp.Fori(0, U_ROUNDS) as r:
                        for s in range(SLOTS):
                            sp.wait_ge(*slot_done[s].after(layer, r + first))
                            sp.dma_start(ring[:, s, :], table[layer, r * SLOTS + s]).then_inc(slot_full[s].sem, 16)
            sp.wait_ge(f_ready.sem, 1)
            sp.dma_start(out, xn).then_inc(stored.sem, 16)
            sp.wait_ge(stored.sem, 16)

        @block.gpsimd
        def _(pool):
            pool.wait_ge(cst_loaded.sem, 16)
            with pool.Fori(0, DEPTH) as layer:
                pool.wait_ge(*peer_added.after(layer, 0))
                pool.dma_start(vec[:, :], vecs[layer]).then_inc(vec_loaded.sem, 16)
                pool.dma_start(mem, mem_in).then_inc(mem_loaded.sem, 16)
                pool.dma_start(tab, tables).then_inc(tab_loaded.sem, 16)
                for i in range(2):
                    pool.wait_ge(*loaded(layer, "bias", i))
                    w = tile("bias", i)
                    settle(pool)
                    pool.tensor_copy(bias[:, 4 * i:4 * i + 4, :], w.rearrange("p (h s) -> p h s", h=4)) \
                        .then_inc(slot_done[TILES["bias", i] % SLOTS].sem, 1)
                for i in range(2):
                    pool.wait_ge(*slot_done[TILES["bias", i] % SLOTS].after(layer, TILES["bias", i] // SLOTS + 1))
                pool.wait_ge(*tab_loaded.after(layer, 1))
                pool.tensor_tensor(bias, bias, window.unsqueeze(1).broadcast_to([P, 8, SEQ]), ALU.add) \
                    .then_inc(bias_ready.sem, 1)
                pool.wait_ge(*bias_ready.after(layer, 1))
                pool.wait_ge(*roped.after(layer, ROPES.index(("kr", 0)) + 1))
                settle(pool)
                pool.tensor_copy(mk[NOPE:MQK, :, :], krr[NOPE:MQK, :].unsqueeze(1).broadcast_to([ROPE, MH, SEQ])) \
                    .then_inc(kr_spread.sem, 1)
                pool.wait_ge(*kr_spread.after(layer, 1))
                settle(pool)
                with pool.Fori(0, U_ROUNDS) as r:
                    for s in range(SLOTS):
                        pool.wait_ge(*high_ready[s % 2].after(layer, r * 2 + s // 2 + 1))
                        pool.tensor_tensor(lo[:, s % 2, :], ring[:, s, :], hi[:, s % 2, :].bitcast(F32),
                                           ALU.subtract).then_inc(slot_done[s].sem, 1)
                pool.wait_ge(*choiceT_ready.after(layer, 3))
                settle(pool)
                with pool.Fori(0, SEQ // 8) as q:
                    pool.wait_ge(*oh1_ready[3].after(layer, q * 2))
                    settle(pool)
                    pool.tensor_copy(i1col[:, :], chosenT[:, 0, bass.ds(q * 8, 8)]).then_inc(i1_copied.sem, 1)
                    pool.wait_ge(*i1_copied.after(layer, q + 1))
                    for j in range(8):
                        pool.wait_ge(*oh_used[j % 4].after(layer, q * 2 + j // 4))
                        settle(pool)
                        pool.tensor_scalar(oh1[:, j % 4, :], iota, i1col[:, j:j + 1], None, ALU.is_equal) \
                            .then_inc(oh1_ready[j % 4].sem, 1)
                pool.wait_ge(*spread_used[1].after(layer, SEQ // 8))
                settle(pool)
                with pool.Fori(0, NK // 2) as r:
                    for b in range(2):
                        pool.wait_ge(*pair_used[b].after(layer, NK // 2 + r))
                        settle(pool)
                        pool.tensor_copy(w_hi[:, b, :], pre[:, bass.ds(r * 2 + b, 1), :].squeeze(1)).then_inc(w_high[b].sem, 1)
                        pool.wait_ge(*w_high[b].after(layer, r + 1))
                        settle(pool)
                        pool.tensor_tensor(w_lo[:, b, :], pre[:, bass.ds(r * 2 + b, 1), :].squeeze(1), w_hi[:, b, :].bitcast(F32),
                                           ALU.subtract).then_inc(w_low[b].sem, 1)
            pool.wait_ge(*peer_added.after(DEPTH, 0))
            pool.dma_start(gfin, g_final).then_inc(gf_loaded.sem, 16)

        @block.tensor
        def _(pe):
            def project(layer, name, i, src, cols=P):
                pe.wait_ge(*bank_free(layer, name, i))
                ps = bank_of(name, i)
                pe.wait_ge(*loaded(layer, name, i))
                w = tile(name, i)
                for c in range(DC):
                    last = pe.matmul(ps[0:cols, 0:SEQ], w[:, c * P:c * P + cols], src[:, c, :],
                                     start=(c == 0), stop=(c == DC - 1))
                last.then_inc(*ends(name, i))

            def project_tok(layer, name, i, src):
                pe.wait_ge(*bank_free(layer, name, i))
                ps = bank_of(name, i)
                pe.wait_ge(*loaded(layer, name, i))
                w = tile(name, i)
                for t in range(NT):
                    for c in range(DC):
                        last = pe.matmul(ps[:, t * P:t * P + P], src[:, c, t * P:t * P + P], w[:, c * P:c * P + P],
                                         start=(c == 0), stop=(c == DC - 1))
                last.then_inc(*ends(name, i))

            def turn(layer, src, *name):
                pe.wait_ge(*bank_free(layer, *name))
                ps = bank_of(*name)
                for k, s in enumerate(src):
                    last = pe.transpose(ps[:, k * P:k * P + P], s, ident)
                last.then_inc(*ends(*name))

            def turn_norm(layer, name, order):
                src = mem if name == "mem" else xn
                for t in range(NT):
                    pe.wait_ge(*normed.after(layer, 2 * order + t + 1))
                    for half in range(2):
                        turn(layer, [src[:, t, c * P:c * P + P] for c in range(4 * half, 4 * half + 4)], name, t, half)

            def rotate(layer, k):
                name = ROPES[k]
                pe.wait_ge(*bank_free(layer, "rot", *name))
                ps = bank_of("rot", *name)
                pe.wait_ge(*in_sbuf(layer, *name))
                if name[0] in ("rq", "rk"):
                    last = pe.matmul(ps[:, 0:SEQ], perm, raw[:, k % 2, :], start=True, stop=True)
                else:
                    last = pe.matmul(ps[0:MQK, 0:SEQ], perm96, raw[0:MQK, k % 2, :], start=True, stop=True)
                last.then_inc(*ends("rot", *name))

            def open_scores(layer, u):
                if u < 2:
                    pe.wait_ge(*peer_added.after(layer, 0))
                elif u - 2 < RH:
                    pe.wait_ge(*ret_scores.after(layer, u - 1))
                elif u - 2 < RH + MIX_UNITS:
                    pe.wait_ge(*masked.after(layer, u - 2 - RH + 1))
                else:
                    pe.wait_ge(*prob_ready.after(layer, u - 2 - RH + 1))
                return bank[4 + u % 2]

            def ret_score(layer, h):
                ps = open_scores(layer, h)
                pe.wait_ge(*roped.after(layer, 4 + h + 1))
                pe.matmul(ps[:, 0:SEQ], rk[:, h, 0:P], rq[:, h, :], start=True, stop=True)
                pe.matmul(ps[:, SEQ:SEQ + P], rk[:, h, P:SEQ], rq[:, h, P:SEQ], start=True, stop=True) \
                    .then_inc(score_full.sem, 1)

            def ret_out(layer, h):
                ps = bank[6 + h % 2]
                if h >= 2:
                    pe.wait_ge(*ret_stored.after(layer, h - 1))
                else:
                    pe.wait_ge(*in_sbuf(layer, "rv", 3))
                pe.wait_ge(*ret_scores.after(layer, h + 1))
                v = [rv[:, t, h * P:h * P + P] for t in range(NT)]
                s = retT[:, h % 2, :]
                pe.matmul(ps[:, 0:P], s[:, 0:P], v[0], start=True, stop=True)
                pe.matmul(ps[:, P:2 * P], s[:, P:2 * P], v[0], start=True, stop=False)
                pe.matmul(ps[:, P:2 * P], s[:, 2 * P:3 * P], v[1], start=False, stop=True).then_inc(ret_full.sem, 1)

            def turn_y(layer, n):
                pe.wait_ge(*ytok_ready.after(layer, n + 1))
                turn(layer, [ytok[:, n % 2, c * P:c * P + P] for c in range(4)], "ty", n)

            def scores(layer, v):
                kind, t, h = UNITS[v]
                ps = open_scores(layer, RH + v)
                keys = SEQ if kind == "xa" else P * (t + 1)
                q = slice(t * P, t * P + P)
                if kind == "swa":
                    lhs, rhs = swq[64 * (h % 2):64 * (h % 2) + 64, h // 2, q], swk[64 * (h % 2):64 * (h % 2) + 64, h // 4, 0:keys]
                elif kind == "mla":
                    lhs, rhs = mq[:, h, q], mk[0:MQK, h, 0:keys]
                    pe.wait_ge(*roped.after(layer, 9 + h + 1))
                    pe.wait_ge(*kr_spread.after(layer, 1))
                    pe.wait_ge(*in_sbuf(layer, "kn", h))
                else:
                    lhs, rhs = xq[:, h, q], xk[:, h, :]
                    pe.wait_ge(*in_sbuf(layer, "xq", h))
                pe.matmul(ps[:, 0:keys], lhs, rhs, start=True, stop=True).then_inc(score_full.sem, 1)

            def turn_probs(layer, v):
                kind, t, h = UNITS[v]
                blocks = 2 if kind == "xa" else t + 1
                pe.wait_ge(*prob_ready.after(layer, v + 1))
                if v:
                    pe.wait_ge(*probT_ready.after(layer, v))
                else:
                    pe.wait_ge(*ret_stored.after(layer, RH))
                for c in range(blocks):
                    last = pe.transpose(bank[6][:, c * P:c * P + P], prob[:, v % 2, c * P:c * P + P], ident)
                last.then_inc(probT_full.sem, 1)

            def weigh(layer, v):
                kind, t, h = UNITS[v]
                blocks = 2 if kind == "xa" else t + 1
                g = next(n for n, g in enumerate(GROUPS) if g[2] <= v <= g[3])
                if v == GROUPS[g][2]:
                    if g:
                        pe.wait_ge(*ytok_ready.after(layer, NT + g))
                    else:
                        pe.wait_ge(*ret_stored.after(layer, RH))
                pe.wait_ge(*probT_ready.after(layer, v + 1))
                for c in range(blocks):
                    if kind == "swa":
                        o, val = bank[7][:, h * SD:h * SD + SD], sv[:, c, (h // 4) * SD:(h // 4) * SD + SD]
                    elif kind == "mla":
                        o, val = bank[7][:, h * MV:h * MV + MV], mv[:, c, h * MV:h * MV + MV]
                    else:
                        o, val = bank[7][:, h * XD:h * XD + XD], xv[:, c, h * XD:h * XD + XD]
                    last = pe.matmul(o, probT[:, v % 2, c * P:c * P + P], val, start=(c == 0), stop=(c == blocks - 1))
                last.then_inc(pv_done.sem, 1)

            def attend(layer, step, units):
                if step in units:
                    scores(layer, step)
                if step - 1 in units:
                    turn_probs(layer, step - 1)
                if step - 2 in units:
                    weigh(layer, step - 2)

            def product4(layer, name, tiles, src):
                for i in range(4):
                    pe.wait_ge(*bank_free(layer, name, i))
                for n in range(tiles):
                    pe.wait_ge(*loaded(layer, name, n))
                    w = tile(name, n)
                    for i in range(4):
                        t, half = i // 2, i % 2
                        last = pe.matmul(bank_of(name, i)[:, :], src[:, n, t * P:t * P + P], w[:, half * 512:half * 512 + 512],
                                         start=(n == 0), stop=(n == tiles - 1))
                        if n == tiles - 1:
                            last.then_inc(*ends(name, i))
                    if n < tiles - 1:
                        last.then_inc(slot_done[TILES[name, n] % SLOTS].sem, 1)

            pe.wait_ge(cst_loaded.sem, 16)
            with pe.Fori(0, DEPTH) as layer:
                turn_norm(layer, "x0", 0)
                turn_norm(layer, "mem", 1)
                pe.wait_ge(*in_sbuf(layer, "x0", 1, 1))
                for k in range(9):
                    if k < 8:
                        project(layer, *ROPES[k], hT)
                    else:
                        project_tok(layer, "rv", 0, hT)
                    if k:
                        rotate(layer, k - 1)
                for i in range(1, 4):
                    project_tok(layer, "rv", i, hT)
                project_tok(layer, "sv", 0, hT)
                ret_score(layer, 0)
                project_tok(layer, "qa", 0, hT)
                ret_score(layer, 1)
                ret_out(layer, 0)
                project_tok(layer, "qa", 1, hT)
                ret_score(layer, 2)
                ret_out(layer, 1)
                project_tok(layer, "kva", 0, hT)
                ret_score(layer, 3)
                ret_out(layer, 2)
                project(layer, "kr", 0, hT, MQK)
                ret_out(layer, 3)
                project(layer, "sq", 0, hT)
                rotate(layer, 8)
                for i in range(1, 4):
                    project(layer, "sq", i, hT)
                pe.wait_ge(*qk_normed.after(layer, 4))
                turn(layer, [qk[:, t, c * P:c * P + P] for c in range(2) for t in range(NT)], "tqa", 0)
                turn(layer, [qk[:, t, QR:QR + P] for t in range(NT)], "tkv", 0)
                project(layer, "sk", 0, hT)
                for i in range(4):
                    project_tok(layer, "rg", i, hT)
                pe.wait_ge(*in_sbuf(layer, "tqa", 0))
                pe.wait_ge(*in_sbuf(layer, "tkv", 0))
                wkv = None
                for h in range(MH):
                    pe.wait_ge(*bank_free(layer, "qb", h))
                    ps = bank_of("qb", h)
                    pe.wait_ge(*loaded(layer, "qb", h // 4))
                    w = tile("qb", h // 4)
                    for c in range(2):
                        o = (c * 4 + h % 4) * MQK
                        last = pe.matmul(ps[0:MQK, 0:SEQ], w[:, o:o + MQK], qanT[:, c, :], start=(c == 0), stop=(c == 1))
                    last.then_inc(*ends("qb", h))
                    pe.wait_ge(*bank_free(layer, "kn", h))
                    ps = bank_of("kn", h)
                    pe.wait_ge(*loaded(layer, "kvb"))
                    w = tile("kvb")
                    pe.matmul(ps[0:NOPE, 0:SEQ], w[:, h * NOPE:h * NOPE + NOPE], kvanT, start=True, stop=True).then_inc(*ends("kn", h))
                    if h:
                        rotate(layer, 9 + h - 1)
                for t in range(NT):
                    pe.wait_ge(*bank_free(layer, "mv", t))
                    ps = bank_of("mv", t)
                    pe.matmul(ps[:, :], kvanT[:, t * P:t * P + P], w[:, 512:1024], start=True, stop=True).then_inc(*ends("mv", t))
                    if t == 0:
                        rotate(layer, 9 + MH - 1)
                turn_y(layer, 0)
                turn_y(layer, 1)
                pe.wait_ge(*in_sbuf(layer, "sk", 0))
                for step in mix_steps():
                    if step < MIX_UNITS:
                        for g in gates_at(step):
                            project(layer, "gate", g, hT)
                    attend(layer, step, range(MIX_UNITS))
                    if step - 1 in END_AT:
                        turn_y(layer, 2 + END_AT[step - 1])
                turn_y(layer, 5)
                pe.wait_ge(*in_sbuf(layer, "ty", 5))
                for cg in range(4):
                    for br in range(3):
                        pe.wait_ge(*loaded(layer, "branch", cg * 3 + br))
                        w = tile("branch", cg * 3 + br)
                        for m in range(2):
                            pe.wait_ge(*bank_free(layer, "branch", cg, br, m))
                            ps = bank_of("branch", cg, br, m)
                            for c in range(4):
                                last = pe.matmul(ps[:, 0:SEQ], w[:, c * 256 + m * P:c * 256 + m * P + P], yT[:, br * 4 + c, :],
                                                 start=(c == 0), stop=(c == 3))
                            last.then_inc(*ends("branch", cg, br, m))
                pe.wait_ge(*gated.after(layer, 16))
                product4(layer, "wo", 8, merged)
                pe.wait_ge(*in_sbuf(layer, "mem", 1, 1))
                for i in range(4):
                    project(layer, "xk", i, memT)
                for i in range(4):
                    project_tok(layer, "xv", i, memT)
                turn_norm(layer, "x1", 2)
                pe.wait_ge(*in_sbuf(layer, "x1", 1, 1))
                for i in range(4):
                    project(layer, "xq", i, hT)
                for step in xa_steps():
                    attend(layer, step, range(MIX_UNITS, len(UNITS)))
                    if step - 1 in END_AT and END_AT[step - 1] >= 4:
                        turn_y(layer, 2 + END_AT[step - 1])
                turn_y(layer, 7)
                pe.wait_ge(*in_sbuf(layer, "ty", 7))
                product4(layer, "xo", 4, yT)
                turn_norm(layer, "x2", 3)
                pe.wait_ge(*in_sbuf(layer, "x2", 1, 1))
                for i in range(8):
                    project(layer, "pq", i, hT)
                pe.wait_ge(*in_sbuf(layer, "pq", 7))
                pe.wait_ge(*loaded(layer, "keys"))
                w = tile("keys")
                for t in range(NT):
                    for pair in range(PH // 2):
                        for p in range(2):
                            pe.wait_ge(*bank_free(layer, "ps", t, pair, p))
                            ps = bank_of("ps", t, pair, p)
                            for k in range(2):
                                h = 2 * pair + k
                                last = pe.matmul(ps[:, k * NK:k * NK + NK], pq[64 * p:64 * p + 64, h, t * P:t * P + P],
                                                 w[64 * p:64 * p + 64, h * NK:h * NK + NK], start=True, stop=True)
                            last.then_inc(*ends("ps", t, pair, p))
                pe.wait_ge(*h_split.after(layer, 2))
                settle(pe)

                def pre_activations(r):
                    for s in range(SLOTS):
                        b = s % 2
                        pe.wait_ge(*slot_done[s].after(layer, U_ROUND0 + r + 1))
                        pe.wait_ge(*pre_stored[s].after(layer, r))
                        for c in range(DC):
                            cols = slice(c * P, c * P + P)
                            for k, (a, h) in enumerate(((hi, h_hi), (hi, h_lo), (lo, h_hi))):
                                last = pe.matmul(bank[4 + s][:, 0:SEQ], a[:, b, cols], h[:, c, :],
                                                 start=(c == 0 and k == 0), stop=(c == DC - 1 and k == 2))
                        last.then_inc(pair_used[b].sem, 1)

                with pe.Fori(0, TURN_ROUND) as r:
                    pre_activations(r)
                pe.wait_ge(*choice_made.after(layer, 1))
                pe.wait_ge(*in_sbuf(layer, "ps", NT - 1, PH // 2 - 1, 1))
                for a in range(3):
                    for t in range(NT):
                        last = pe.transpose(bank[a][:, t * P:t * P + P], chosen[:, a, t, :], ident)
                    last.then_inc(choice_turned.sem, 1)
                with pe.Fori(TURN_ROUND, U_ROUNDS) as r:
                    pre_activations(r)
                pe.wait_ge(*choiceT_ready.after(layer, 3))
                settle(pe)
                with pe.Fori(0, SEQ // 8) as q:
                    for b in range(2):
                        pe.wait_ge(*spread_used[b].after(layer, q))
                        for s in range(4):
                            pe.wait_ge(*oh1_ready[s].after(layer, q * 2 + b + 1))
                            pe.wait_ge(*oh2_ready[s].after(layer, q * 2 + b + 1))
                            pe.matmul(bank[b][:, s * NK:s * NK + NK], oh1[:, s, :], oh2[:, s, :], start=True, stop=True) \
                                .then_inc(oh_used[s].sem, 1)
                for s in range(4):
                    pe.wait_ge(*pre_stored[s].after(layer, U_ROUNDS))

                def down(r, first, final):
                    for s in range(SLOTS):
                        b = s % 2
                        pe.wait_ge(*slot_done[s].after(layer, V_ROUND0 + r + 1))
                        pe.wait_ge(*w_low[b].after(layer, r * 2 + s // 2 + 1))
                        for i in range(4):
                            t, half = i // 2, i % 2
                            tok, cols = slice(t * P, t * P + P), slice(half * 512, half * 512 + 512)
                            for k, (a, v) in enumerate(((w_hi, hi), (w_hi, lo), (w_lo, hi))):
                                last = pe.matmul(bank[4 + i][:, :], a[:, b, tok], v[:, b, cols],
                                                 start=(first and s == 0 and k == 0),
                                                 stop=(final and s == SLOTS - 1 and k == 2))
                        last.then_inc(pair_used[b].sem, 1)

                down(0, True, False)
                with pe.Fori(1, U_ROUNDS - 1) as r:
                    down(r, False, False)
                down(U_ROUNDS - 1, False, True)

        @block.scalar
        def _(act):
            def copy_job(layer, dst, src, *name, func=ACT.Copy):
                act.wait_ge(*full(layer, *name))
                act.activation(dst, src, func).then_inc(*stores(*name))

            def square_sums(layer, src, junk, order, col):
                for t in range(NT):
                    act.activation(junk[:, t, :], src[:, t, :], ACT.Square, accum_out=stat[:, col + t:col + t + 1]) \
                        .then_inc(squares.sem, 1)
                act.wait_ge(*meansq.after(layer, order + 1))
                act.activation(stat[:, col + 4:col + 6], stat[:, col + 2:col + 4], ACT.Sqrt).then_inc(root.sem, 1)

            def both(name, i, cols=P):
                return bank_of(name, i)[:, 0:NT * P].rearrange("p (t c) -> p t c", t=NT)

            def raw_copy(layer, k):
                name = ROPES[k]
                rows = P if name[0] in ("rq", "rk") else MQK
                if k >= 2:
                    act.wait_ge(*raw_cos.after(layer, k - 1))
                    act.wait_ge(*full(layer, "rot", *ROPES[k - 2]))
                copy_job(layer, raw[0:rows, k % 2, :], bank_of(*name)[0:rows, 0:SEQ], *name)

            def ret_store(layer, h):
                act.wait_ge(*ret_full.after(layer, h + 1))
                act.activation(ytok[:, :, h * P:h * P + P], bank[6 + h % 2][:, 0:2 * P].rearrange("p (t e) -> p t e", t=NT),
                               ACT.Copy).then_inc(ret_stored.sem, 1)

            def yT_store(layer, n):
                copy_job(layer, yT[:, (n // 2 % 3) * 4:(n // 2 % 3) * 4 + 4, (n % 2) * P:(n % 2) * P + P],
                         bank_of("ty", n).rearrange("p (c s) -> p c s", c=4), "ty", n)

            def soft(layer, step, units):
                if step in units:
                    kind, t, h = UNITS[step]
                    keys = SEQ if kind == "xa" else P * (t + 1)
                    act.wait_ge(*negmax_ready.after(layer, step + 1))
                    if step >= 2:
                        act.wait_ge(*probT_full.after(layer, step - 1))
                    src = bank[4 + (RH + step) % 2][:, 0:keys] if kind == "xa" else sm[:, step % 2, 0:keys]
                    act.activation(prob[:, step % 2, 0:keys], src, ACT.Exp, bias=negmax[:, step:step + 1],
                                   scale=XD ** -0.5 if kind == "xa" else 1.0,
                                   accum_out=sums[:, step:step + 1]).then_inc(prob_ready.sem, 1)
                if step - 1 in units:
                    v = step - 1
                    kind, t, h = UNITS[v]
                    keys = SEQ if kind == "xa" else P * (t + 1)
                    act.wait_ge(*probT_full.after(layer, v + 1))
                    if v >= 2:
                        act.wait_ge(*pv_done.after(layer, v - 1))
                    act.activation(probT[:, v % 2, 0:keys], bank[6][:, 0:keys], ACT.Copy).then_inc(probT_ready.sem, 1)
                if step in END_AT and END_AT[step] < NT:
                    g = END_AT[step]
                    act.wait_ge(*sink_shift.after(layer, g + 1))
                    act.activation(sinkexp[:, g, :], sinkexp[:, g, :], ACT.Exp).then_inc(sink_exp.sem, 1)

            with act.Fori(0, DEPTH) as layer:
                act.wait_ge(x_loaded.sem, 16)
                act.wait_ge(*peer_added.after(layer, 0))
                square_sums(layer, x, xn, 0, 0)
                act.wait_ge(*mem_loaded.after(layer, 1))
                square_sums(layer, mem, memT.rearrange("p c s -> p (c s)").rearrange("p (t d) -> p t d", t=NT), 1, 8)
                for k in range(8):
                    raw_copy(layer, k)
                for i in range(4):
                    copy_job(layer, rv[:, :, i * P:i * P + P], both("rv", i), "rv", i)
                copy_job(layer, sv, both("sv", 0), "sv", 0)
                for i in range(2):
                    copy_job(layer, qk[:, :, i * P:i * P + P], both("qa", i), "qa", i)
                ret_store(layer, 0)
                ret_store(layer, 1)
                copy_job(layer, qk[:, :, QR:QR + P], both("kva", 0), "kva", 0)
                act.wait_ge(*in_sbuf(layer, "kva", 0))
                for t in range(NT):
                    for k, cols in enumerate((slice(0, QR), slice(QR, QR + KVR))):
                        act.activation(junk[:, t, cols], qk[:, t, cols], ACT.Square,
                                       accum_out=stat[:, 32 + 2 * k + t:33 + 2 * k + t]).then_inc(qk_sq.sem, 1)
                ret_store(layer, 2)
                raw_copy(layer, 8)
                ret_store(layer, 3)
                copy_job(layer, swq[:, 0, :], bank_of("sq", 0)[:, 0:SEQ], "sq", 0)
                act.wait_ge(*qk_ms.after(layer, 2))
                act.activation(stat[:, 40:44], stat[:, 36:40], ACT.Sqrt).then_inc(qk_root.sem, 1)
                for i in range(1, 4):
                    copy_job(layer, swq[:, i, :], bank_of("sq", i)[:, 0:SEQ], "sq", i)
                act.wait_ge(*ret_ms.after(layer, 1))
                act.activation(stat[:, 56:64], stat[:, 48:56], ACT.Sqrt).then_inc(ret_root.sem, 1)
                for i in range(4):
                    act.wait_ge(*full(layer, "rg", i))
                    if i:
                        act.wait_ge(*in_sbuf(layer, "rg", i - 1))
                    act.activation(sgm, both("rg", i), ACT.Sigmoid).then_inc(gate_sig.sem, 1)
                for h in range(MH):
                    raw_copy(layer, 9 + h)
                    copy_job(layer, mk[0:NOPE, h, :], bank_of("kn", h)[0:NOPE, 0:SEQ], "kn", h)
                for t in range(NT):
                    copy_job(layer, mv[:, t, :], bank_of("mv", t), "mv", t)
                yT_store(layer, 0)
                yT_store(layer, 1)
                for step in mix_steps():
                    if step < MIX_UNITS:
                        for g in gates_at(step):
                            copy_job(layer, gates[:, g, :], bank_of("gate", g)[:, 0:SEQ], "gate", g, func=ACT.Sigmoid)
                    soft(layer, step, range(MIX_UNITS))
                    if step - 1 in END_AT:
                        yT_store(layer, 2 + END_AT[step - 1])
                yT_store(layer, 5)
                for i in range(4):
                    copy_job(layer, xk[:, i, :], bank_of("xk", i)[:, 0:SEQ], "xk", i)
                for i in range(4):
                    copy_job(layer, xv[:, :, i * P:i * P + P], both("xv", i), "xv", i)
                act.wait_ge(*in_sbuf(layer, "wo", 3))
                square_sums(layer, x, xn, 2, 16)
                for i in range(4):
                    copy_job(layer, xq[:, i, :], bank_of("xq", i)[:, 0:SEQ], "xq", i)
                for step in xa_steps():
                    soft(layer, step, range(MIX_UNITS, len(UNITS)))
                    if step - 1 in END_AT and END_AT[step - 1] >= 4:
                        yT_store(layer, 2 + END_AT[step - 1])
                yT_store(layer, 7)
                act.wait_ge(*in_sbuf(layer, "xo", 3))
                square_sums(layer, x, xn, 3, 24)
                act.wait_ge(*in_sbuf(layer, "x2", 1, 1))
                act.activation(h_hi[:, :, :], hT[:, :, :], ACT.Copy).then_inc(h_split.sem, 1)
                for i in range(8):
                    copy_job(layer, pq[:, i, :], bank_of("pq", i)[:, 0:SEQ], "pq", i)
                for t in range(NT):
                    for pair in range(PH // 2):
                        for p in range(2):
                            j = (t * PH + 2 * pair) * 2 + p
                            copy_job(layer, sc[:, j:j + 3:2, :],
                                     bank_of("ps", t, pair, p)[:, 0:2 * NK].rearrange("p (a n) -> p a n", a=2), "ps", t, pair, p)

                def high(first, r, s):
                    b = s % 2
                    act.wait_ge(*slot_full[s].after(layer, first + r + 1))
                    act.wait_ge(*pair_used[b].after(layer, (first - U_ROUND0) * 2 + r * 2 + s // 2))
                    act.activation(hi[:, b, :], ring[:, s, :], ACT.Copy).then_inc(high_ready[b].sem, 1)

                def gelu(r, s):
                    act.wait_ge(*pair_used[s % 2].after(layer, r * 2 + s // 2 + 1))
                    act.activation(pre[:, bass.ds(r * SLOTS + s, 1), :].squeeze(1), bank[4 + s][:, 0:SEQ], ACT.Gelu) \
                        .then_inc(pre_stored[s].sem, 1)

                def u_round(r):
                    for s in range(SLOTS):
                        high(U_ROUND0, r, s)
                        if s:
                            gelu(r, s - 1)
                    gelu(r, SLOTS - 1)

                with act.Fori(0, FREE_ROUNDS) as r:
                    u_round(r)
                act.wait_ge(*best_shift.after(layer, 1))
                act.activation(best, best, ACT.Exp).then_inc(best_exp.sem, 1)
                act.wait_ge(*choice_made.after(layer, 1))
                with act.Fori(FREE_ROUNDS, U_ROUNDS) as r:
                    u_round(r)
                with act.Fori(0, U_ROUNDS) as r:
                    for s in range(SLOTS):
                        high(V_ROUND0, r, s)
            act.wait_ge(*peer_added.after(DEPTH, 0))
            for t in range(NT):
                last = act.activation(xn[:, t, :], x[:, t, :], ACT.Square, accum_out=stat[:, t:t + 1])
            last.then_inc(f_sq.sem, 1)
            act.wait_ge(f_ms.sem, 1)
            act.activation(stat[:, 4:6], stat[:, 2:4], ACT.Sqrt).then_inc(f_root.sem, 1)

        @block.vector
        def _(dve):
            def norm_rows(layer, src, dst, order, col):
                dve.wait_ge(*squares.after(layer, 2 * order + 2))
                dve.tensor_scalar(stat[:, col + 2:col + 4], stat[:, col:col + 2], 1.0 / D, EPS, ALU.mult, ALU.add) \
                    .then_inc(meansq.sem, 1)
                dve.wait_ge(*root.after(layer, order + 1))
                dve.reciprocal(stat[:, col + 6:col + 8], stat[:, col + 4:col + 6]).then_inc(rstd.sem, 1)
                dve.wait_ge(*rstd.after(layer, order + 1))
                for t in range(NT):
                    dve.tensor_scalar(dst[:, t, :], src[:, t, :], stat[:, col + 6 + t:col + 7 + t], None, ALU.mult) \
                        .then_inc(normed.sem, 1)

            def gain_store(layer, name, dst, g):
                for t in range(NT):
                    for half in range(2):
                        dve.wait_ge(*full(layer, name, t, half))
                        ps = bank_of(name, t, half)
                        dve.tensor_tensor(dst[:, 4 * half:4 * half + 4, t * P:t * P + P],
                                                ps.rearrange("p (c s) -> p c s", c=4),
                                                vec[:, g + 4 * half:g + 4 * half + 4].unsqueeze(2).broadcast_to([P, 4, P]),
                                                ALU.mult).then_inc(*stores(name, t, half))

            def rope(layer, k):
                name, b = ROPES[k], k % 2
                wide = name[0] in ("rq", "rk")
                rows = P if wide else MQK
                c, s = (cos, sin) if wide else (cosm, sinm)
                dst = {"rq": lambda i: rq[:, i, :], "rk": lambda i: rk[:, i, :], "kr": lambda i: krr[0:MQK, :],
                       "qb": lambda i: mq[:, i, :]}[name[0]](name[1])
                dve.wait_ge(*in_sbuf(layer, *name))
                dve.tensor_tensor(cosx[0:rows, b, :], raw[0:rows, b, :], c, ALU.mult).then_inc(raw_cos.sem, 1)
                dve.wait_ge(*full(layer, "rot", *name))
                ps = bank_of("rot", *name)
                dve.tensor_tensor(sinx[0:rows, b, :], ps[0:rows, 0:SEQ], s, ALU.mult).then_inc(*stores("rot", *name))
                dve.wait_ge(*raw_cos.after(layer, k + 1))
                dve.wait_ge(*in_sbuf(layer, "rot", *name))
                dve.tensor_tensor(dst, cosx[0:rows, b, :], sinx[0:rows, b, :], ALU.add).then_inc(roped.sem, 1)

            def ret_decay(layer, h):
                dve.wait_ge(*score_full.after(layer, h + 1))
                if h >= 2:
                    dve.wait_ge(*ret_full.after(layer, h - 1))
                ps = bank[4 + h % 2]
                dve.tensor_tensor(retT[:, h % 2, 0:SEQ], ps[:, 0:SEQ], decay[:, h, :], ALU.mult)
                dve.tensor_tensor(retT[:, h % 2, SEQ:SEQ + P], ps[:, SEQ:SEQ + P], decay[:, h, 0:P], ALU.mult) \
                    .then_inc(ret_scores.sem, 1)

            def soft(layer, step, units):
                if step in units:
                    kind, t, h = UNITS[step]
                    keys = SEQ if kind == "xa" else P * (t + 1)
                    ps = bank[4 + (RH + step) % 2]
                    dve.wait_ge(*score_full.after(layer, RH + step + 1))
                    nm = negmax[:, step:step + 1]
                    if kind == "xa":
                        dve.tensor_reduce(rowm[:, step % 2:step % 2 + 1], ps[:, 0:keys], AXX, ALU.max).then_inc(xa_max.sem, 1)
                        dve.wait_ge(*xa_max.after(layer, step - MIX_UNITS + 1))
                        dve.tensor_scalar(nm, rowm[:, step % 2:step % 2 + 1], -(XD ** -0.5), None, ALU.mult) \
                            .then_inc(negmax_ready.sem, 1)
                        return
                    add = bias[:, h, SEQ - keys:SEQ] if kind == "swa" else causal[:, SEQ - keys:SEQ]
                    if step >= 2:
                        dve.wait_ge(*prob_ready.after(layer, step - 1))
                    dve.scalar_tensor_tensor(out=sm[:, step % 2, 0:keys], in0=ps[:, 0:keys],
                                             scalar=(SD if kind == "swa" else MQK) ** -0.5, in1=add,
                                             op0=ALU.mult, op1=ALU.add).then_inc(masked.sem, 1)
                    dve.wait_ge(*masked.after(layer, step + 1))
                    last = dve.tensor_reduce(nm, sm[:, step % 2, 0:keys], AXX, ALU.max, negate=True)
                    if kind == "mla":
                        last.then_inc(negmax_ready.sem, 1)
                        return
                    last.then_inc(rowmax.sem, 1)
                    dve.wait_ge(*rowmax.after(layer, step + 1))
                    dve.tensor_tensor(nm, nm, negsink[:, h:h + 1], ALU.min).then_inc(negmax_ready.sem, 1)

            def end_group(layer, step):
                if step not in END_AT:
                    return
                g = END_AT[step]
                kind, t, v0, v1 = GROUPS[g]
                heads = v1 - v0 + 1
                den = sums[:, v0:v1 + 1]
                if kind == "swa":
                    dve.wait_ge(*negmax_ready.after(layer, v1 + 1))
                    dve.tensor_tensor(sinkexp[:, t, :], negmax[:, v0:v1 + 1], vec[:, SINKS:SINKS + 8], ALU.add) \
                        .then_inc(sink_shift.sem, 1)
                    dve.wait_ge(*prob_ready.after(layer, v1 + 1))
                    dve.wait_ge(*sink_exp.after(layer, t + 1))
                    dve.tensor_tensor(sinkexp[:, t, :], sinkexp[:, t, :], den, ALU.add).then_inc(den_ready.sem, 1)
                    dve.wait_ge(*den_ready.after(layer, t + 1))
                    den = sinkexp[:, t, :]
                dve.wait_ge(*prob_ready.after(layer, v1 + 1))
                dve.reciprocal(rden[:, t, 0:heads], den).then_inc(rden_ready.sem, 1)
                dve.wait_ge(*rden_ready.after(layer, g + 1))
                dve.wait_ge(*pv_done.after(layer, v1 + 1))
                dve.wait_ge(*full(layer, "ty", g))
                dve.tensor_tensor(ytok[:, t, :].rearrange("p (h e) -> p h e", h=heads),
                                  bank[7][:, :].rearrange("p (h e) -> p h e", h=heads),
                                  rden[:, t, 0:heads].unsqueeze(2).broadcast_to([P, heads, 512 // heads]), ALU.mult) \
                    .then_inc(ytok_ready.sem, 1)

            def add_x(layer, name):
                for i in range(4):
                    dve.wait_ge(*full(layer, name, i))
                    ps = bank_of(name, i)
                    xs = x[:, i // 2, (i % 2) * 512:(i % 2) * 512 + 512]
                    dve.tensor_tensor(xs, xs, ps, ALU.add).then_inc(*stores(name, i))

            dve.wait_ge(cst_loaded.sem, 16)
            with dve.Fori(0, DEPTH) as layer:
                norm_rows(layer, x, xn, 0, 0)
                dve.wait_ge(*vec_loaded.after(layer, 1))
                dve.tensor_scalar(negsink, vec[:, SINKS:SINKS + 8], -1.0, None, ALU.mult).then_inc(sink_negated.sem, 1)
                gain_store(layer, "x0", hT, G_MIX)
                norm_rows(layer, mem, mem, 1, 8)
                gain_store(layer, "mem", memT, G_MEM)
                dve.wait_ge(*tab_loaded.after(layer, 1))
                for k in range(8):
                    rope(layer, k)
                for h in range(RH):
                    ret_decay(layer, h)
                rope(layer, 8)
                dve.wait_ge(*qk_sq.after(layer, 4))
                dve.tensor_scalar(stat[:, 36:38], stat[:, 32:34], 1.0 / QR, EPS, ALU.mult, ALU.add).then_inc(qk_ms.sem, 1)
                dve.tensor_scalar(stat[:, 38:40], stat[:, 34:36], 1.0 / KVR, EPS, ALU.mult, ALU.add).then_inc(qk_ms.sem, 1)
                dve.wait_ge(*qk_root.after(layer, 1))
                dve.reciprocal(stat[:, 44:48], stat[:, 40:44]).then_inc(qk_rstd.sem, 1)
                dve.wait_ge(*qk_rstd.after(layer, 1))
                for t in range(NT):
                    for k, cols in enumerate((slice(0, QR), slice(QR, QR + KVR))):
                        dve.tensor_scalar(qk[:, t, cols], qk[:, t, cols], stat[:, 44 + 2 * k + t:45 + 2 * k + t], None,
                                          ALU.mult).then_inc(qk_normed.sem, 1)
                dve.wait_ge(*ret_stored.after(layer, RH))
                ys = ytok.rearrange("p t (h e) -> p t h e", h=RH)
                for t in range(NT):
                    dve.tensor_tensor(rsq[:, t, :], ytok[:, t, :], ytok[:, t, :], ALU.mult).then_inc(ret_sq.sem, 1)
                dve.wait_ge(*ret_sq.after(layer, 2))
                for t in range(NT):
                    dve.tensor_reduce(rsum[:, 4 * t:4 * t + 4], rsq[:, t, :].rearrange("p (h e) -> p h e", h=RH), AXX, ALU.add) \
                        .then_inc(ret_sum.sem, 1)
                dve.wait_ge(*ret_sum.after(layer, 2))
                dve.tensor_scalar(stat[:, 48:56], rsum, 1.0 / P, EPS, ALU.mult, ALU.add).then_inc(ret_ms.sem, 1)
                dve.wait_ge(*ret_root.after(layer, 1))
                dve.reciprocal(rsum, stat[:, 56:64]).then_inc(ret_rstd.sem, 1)
                dve.wait_ge(*ret_rstd.after(layer, 1))
                for t in range(NT):
                    dve.tensor_tensor(ys[:, t], ys[:, t], rsum[:, 4 * t:4 * t + 4].unsqueeze(2).broadcast_to([P, RH, P]),
                                      ALU.mult).then_inc(ret_scaled.sem, 1)
                dve.wait_ge(*full(layer, "tqa", 0))
                ps = bank_of("tqa", 0)
                dve.tensor_tensor(qanT, ps.rearrange("p (c s) -> p c s", c=2),
                                        vec[:, G_Q:G_Q + 2].unsqueeze(2).broadcast_to([P, 2, SEQ]), ALU.mult).then_inc(*stores("tqa", 0))
                dve.wait_ge(*full(layer, "tkv", 0))
                ps = bank_of("tkv", 0)
                dve.tensor_scalar(kvanT, ps[:, 0:SEQ], vec[:, G_KV:G_KV + 1], None, ALU.mult).then_inc(*stores("tkv", 0))
                dve.wait_ge(*full(layer, "sk", 0))
                ps = bank_of("sk", 0)
                for g in range(SKV):
                    for half in range(2):
                        last = dve.tensor_copy(swk[64 * half:64 * half + 64, g, :], ps[64 * g:64 * g + 64, 0:SEQ])
                last.then_inc(*stores("sk", 0))
                for i in range(4):
                    dve.wait_ge(*gate_sig.after(layer, i + 1))
                    ps = bank_of("rg", i)[:, 0:NT * P].rearrange("p (t c) -> p t c", t=NT)
                    dve.tensor_tensor(rgs[:, :, i * P:i * P + P], ps, sgm, ALU.mult).then_inc(*stores("rg", i))
                dve.wait_ge(*in_sbuf(layer, "rg", 3))
                dve.wait_ge(*ret_scaled.after(layer, 2))
                for t in range(NT):
                    dve.tensor_tensor(ytok[:, t, :], ytok[:, t, :], rgs[:, t, :], ALU.mult).then_inc(ytok_ready.sem, 1)
                for h in range(MH):
                    rope(layer, 9 + h)
                dve.wait_ge(*bias_ready.after(layer, 1))
                dve.wait_ge(*sink_negated.after(layer, 1))
                for step in mix_steps():
                    soft(layer, step, range(MIX_UNITS))
                    end_group(layer, step)
                for cg in range(4):
                    for br in range(3):
                        for m in range(2):
                            d = cg * 2 + m
                            dve.wait_ge(*full(layer, "branch", cg, br, m))
                            ps = bank_of("branch", cg, br, m)
                            gate = gates[:, GATE_OF[br] * DC + d, :]
                            if br == 0:
                                dve.tensor_tensor(merged[:, d, :], ps[:, 0:SEQ], gate, ALU.mult).then_inc(*stores("branch", cg, br, m))
                                continue
                            dve.tensor_tensor(gate, ps[:, 0:SEQ], gate, ALU.mult).then_inc(*stores("branch", cg, br, m))
                            dve.wait_ge(*in_sbuf(layer, "branch", cg, br, m))
                            if br == 2:
                                dve.wait_ge(*gated.after(layer, cg * 4 + m + 1))
                            dve.tensor_tensor(merged[:, d, :], merged[:, d, :], gate, ALU.add).then_inc(gated.sem, 1)
                add_x(layer, "wo")
                norm_rows(layer, x, xn, 2, 16)
                gain_store(layer, "x1", hT, G_XA)
                for step in xa_steps():
                    soft(layer, step, range(MIX_UNITS, len(UNITS)))
                    if END_AT.get(step, 0) >= 4:
                        end_group(layer, step)
                add_x(layer, "xo")
                norm_rows(layer, x, xn, 3, 24)
                gain_store(layer, "x2", hT, G_FFN)
                dve.wait_ge(*h_split.after(layer, 1))
                dve.tensor_tensor(h_lo[:, :, :], hT[:, :, :], h_hi[:, :, :].bitcast(F32), ALU.subtract).then_inc(h_split.sem, 1)

                dve.wait_ge(*in_sbuf(layer, "ps", NT - 1, PH // 2 - 1, 1))
                segs = range(NT * PH * 2)
                settle(dve)
                for j in segs:
                    last = dve.max(top[:, j, 0:8], sc[:, j, :])
                last.then_inc(top1.sem, 1)
                dve.wait_ge(*top1.after(layer, 1))
                settle(dve)
                for j in segs:
                    last = dve.max_index(topi[:, j, 0:8], top[:, j, 0:8], sc[:, j, :])
                last.then_inc(top_idx1.sem, 1)
                dve.wait_ge(*top_idx1.after(layer, 1))
                settle(dve)
                for j in segs:
                    last = dve.match_replace(sc[:, j, :], top[:, j, 0:8], sc[:, j, :], LEAST)
                last.then_inc(top_cut.sem, 1)
                dve.wait_ge(*top_cut.after(layer, 1))
                settle(dve)
                for j in segs:
                    last = dve.max(top[:, j, 8:16], sc[:, j, :])
                last.then_inc(top2.sem, 1)
                dve.wait_ge(*top2.after(layer, 1))
                settle(dve)
                for j in segs:
                    last = dve.max_index(topi[:, j, 8:16], top[:, j, 8:16], sc[:, j, :])
                last.then_inc(top_idx2.sem, 1)
                dve.wait_ge(*top_idx2.after(layer, 1))
                dve.tensor_copy(topf, topi).then_inc(top_float.sem, 1)
                top_v = top.rearrange("p (t h a) k -> p t h a k", t=NT, h=PH)
                for t in range(NT):
                    if t:
                        dve.wait_ge(*best_idx2.after(layer, t))
                    dve.tensor_tensor(cand.rearrange("p h (i j) -> p h i j", i=TOPK),
                                      top_v[:, t, :, 0, :].unsqueeze(3).broadcast_to([P, PH, TOPK, TOPK]),
                                      top_v[:, t, :, 1, :].unsqueeze(2).broadcast_to([P, PH, TOPK, TOPK]), ALU.add) \
                        .then_inc(cand_ready.sem, 1)
                    dve.wait_ge(*cand_ready.after(layer, t + 1))
                    settle(dve)
                    for h in range(PH):
                        last = dve.max(best[:, t * PH + h, 0:8], cand[:, h, :])
                    last.then_inc(best1.sem, 1)
                    dve.wait_ge(*best1.after(layer, t + 1))
                    settle(dve)
                    for h in range(PH):
                        last = dve.max_index(besti[:, t * PH + h, 0:8], best[:, t * PH + h, 0:8], cand[:, h, :])
                    last.then_inc(best_idx1.sem, 1)
                    dve.wait_ge(*best_idx1.after(layer, t + 1))
                    settle(dve)
                    for h in range(PH):
                        last = dve.match_replace(cand[:, h, :], best[:, t * PH + h, 0:8], cand[:, h, :], LEAST)
                    last.then_inc(best_cut.sem, 1)
                    dve.wait_ge(*best_cut.after(layer, t + 1))
                    settle(dve)
                    for h in range(PH):
                        last = dve.max(best[:, t * PH + h, 8:16], cand[:, h, :])
                    last.then_inc(best2.sem, 1)
                    dve.wait_ge(*best2.after(layer, t + 1))
                    settle(dve)
                    for h in range(PH):
                        last = dve.max_index(besti[:, t * PH + h, 8:16], best[:, t * PH + h, 8:16], cand[:, h, :])
                    last.then_inc(best_idx2.sem, 1)
                dve.wait_ge(*best_idx2.after(layer, NT))
                chosen_v = chosen[:, :, :, :].rearrange("p a t (h k) -> p a t h k", h=PH)
                best_v = best.rearrange("p g k -> p (g k)")
                besti_v = besti.rearrange("p g k -> p (g k)")
                dve.tensor_copy(bestmax, best[:, :, 0:1]).then_inc(best_top.sem, 1)
                dve.tensor_scalar(posi[:, 0, :], besti_v, 4, None, ALU.logical_shift_right)
                dve.tensor_scalar(posi[:, 1, :], besti_v, TOPK - 1, None, ALU.bitwise_and).then_inc(pos_split.sem, 1)
                dve.wait_ge(*best_top.after(layer, 1))
                dve.tensor_tensor(best, best, bestmax.broadcast_to([P, NT * PH, TOPK]), ALU.subtract) \
                    .then_inc(best_shift.sem, 1)
                dve.wait_ge(*pos_split.after(layer, 1))
                dve.tensor_copy(posf.rearrange("p a b -> p (a b)"), posi.rearrange("p a b -> p (a b)")).then_inc(pos_float.sem, 1)
                dve.wait_ge(*pos_float.after(layer, 1))
                dve.wait_ge(*top_float.after(layer, 1))
                topf_v = topf.rearrange("p (t h a) k -> p t h a k", t=NT, h=PH)
                oh4 = onehot.rearrange("p (h k) i -> p h k i", h=PH)
                n = 0
                for a in range(2):
                    for t in range(NT):
                        if n:
                            dve.wait_ge(*index_ready.after(layer, n))
                        dve.tensor_tensor(onehot, posf[:, a * NT + t, :].unsqueeze(2).broadcast_to([P, PH * TOPK, TOPK]),
                                          iota[:, 0:TOPK].unsqueeze(1).broadcast_to([P, PH * TOPK, TOPK]), ALU.is_equal) \
                            .then_inc(onehot_ready.sem, 1)
                        dve.wait_ge(*onehot_ready.after(layer, n + 1))
                        dve.tensor_tensor(oh4, oh4, topf_v[:, t, :, a, :].unsqueeze(2).broadcast_to([P, PH, TOPK, TOPK]),
                                          ALU.mult).then_inc(picked.sem, 1)
                        dve.wait_ge(*picked.after(layer, n + 1))
                        dve.tensor_reduce(chosen[:, a, t, :], onehot, AXX, ALU.add).then_inc(index_ready.sem, 1)
                        n += 1
                dve.wait_ge(*best_exp.after(layer, 1))
                dve.tensor_reduce(bestsum, best, AXX, ALU.add).then_inc(best_sum.sem, 1)
                dve.wait_ge(*best_sum.after(layer, 1))
                dve.reciprocal(bestsum, bestsum).then_inc(best_rsum.sem, 1)
                dve.wait_ge(*best_rsum.after(layer, 1))
                dve.wait_ge(*index_ready.after(layer, 2 * NT))
                dve.tensor_tensor(chosen[:, 2, :, :].rearrange("p t (h k) -> p (t h) k", h=PH), best,
                                  bestsum.unsqueeze(2).broadcast_to([P, NT * PH, TOPK]), ALU.mult).then_inc(choice_made.sem, 1)
                for a in range(3):
                    dve.wait_ge(*choice_turned.after(layer, a + 1))
                    dve.tensor_copy(chosenT[:, a, :], bank[a][:, 0:SEQ]).then_inc(choiceT_ready.sem, 1)
                dve.wait_ge(*choiceT_ready.after(layer, 3))
                for b in range(4):
                    dve.wait_ge(*pre_stored[b].after(layer, U_ROUNDS))
                settle(dve)
                with dve.Fori(0, SEQ // 8) as q:
                    for b in range(2):
                        for s in range(4):
                            dve.wait_ge(*oh_used[s].after(layer, q * 2 + b))
                            tok = q * 8 + b * 4 + s
                            dve.tensor_scalar(oh2[:, s, :], iota, chosenT[:, 1, bass.ds(tok, 1)], chosenT[:, 2, bass.ds(tok, 1)],
                                              ALU.is_equal, ALU.mult).then_inc(oh2_ready[s].sem, 1)
                        dve.wait_ge(*oh_used[3].after(layer, q * 2 + b + 1))
                        cell = pre[:, :, bass.ds(q * 8 + b * 4, 4)]
                        dve.tensor_tensor(cell, bank[b][:, :].rearrange("p (s n) -> p n s", s=4), cell, ALU.mult) \
                            .then_inc(spread_used[b].sem, 1)
                with dve.Fori(0, U_ROUNDS) as r:
                    for s in range(SLOTS):
                        dve.wait_ge(*high_ready[s % 2].after(layer, NK // 2 + r * 2 + s // 2 + 1))
                        dve.tensor_tensor(lo[:, s % 2, :], ring[:, s, :], hi[:, s % 2, :].bitcast(F32), ALU.subtract) \
                            .then_inc(slot_done[s].sem, 1)
                dve.wait_ge(*pair_used[1].after(layer, NK))
                for i in range(4):
                    xs = x[:, i // 2, (i % 2) * 512:(i % 2) * 512 + 512]
                    dve.tensor_tensor(xs, xs, bank[4 + i][:, :], ALU.add).then_inc(peer_added.sem, 1)
            dve.wait_ge(f_sq.sem, 1)
            dve.tensor_scalar(stat[:, 2:4], stat[:, 0:2], 1.0 / D, EPS, ALU.mult, ALU.add).then_inc(f_ms.sem, 1)
            dve.wait_ge(f_root.sem, 1)
            dve.reciprocal(stat[:, 6:8], stat[:, 4:6]).then_inc(f_rstd.sem, 1)
            dve.wait_ge(f_rstd.sem, 1)
            for t in range(NT):
                last = dve.tensor_scalar(xn[:, t, :], x[:, t, :], stat[:, 6 + t:7 + t], None, ALU.mult)
            last.then_inc(f_scaled.sem, 1)
            dve.wait_ge(f_scaled.sem, 1)
            dve.wait_ge(gf_loaded.sem, 16)
            dve.tensor_tensor(xn, xn, gfin.unsqueeze(1).broadcast_to([P, NT, D]), ALU.mult).then_inc(f_ready.sem, 1)


def constants():
    cst = np.zeros((P, NCONST), np.float32)
    cst[:, C_ID:C_ID + P] = np.eye(P)
    cst[np.arange(P), C_PERM + (np.arange(P) + P // 2) % P] = 1
    half = ROPE // 2
    swap = np.arange(MQK)
    swap[NOPE:] = NOPE + (np.arange(ROPE) + half) % ROPE
    cst[np.arange(MQK), C_PERM96 + swap] = 1
    cst[:, C_IOTA:C_IOTA + P] = np.arange(P)
    tab = np.zeros((P, NTAB), np.float32)

    def angles(n):
        inv = np.power(np.float32(10000.0), -np.arange(n, dtype=np.float32) / np.float32(n)).astype(np.float32)
        a = inv[:, None] * np.arange(SEQ, dtype=np.float32)[None, :]
        return np.cos(a.astype(np.float32)), np.sin(a.astype(np.float32))

    c, s = angles(P // 2)
    tab[:, T_COS:T_COS + SEQ] = np.concatenate([c, c])
    tab[:, T_SIN:T_SIN + SEQ] = np.concatenate([-s, s])
    c, s = angles(half)
    tab[0:NOPE, T_COSM:T_COSM + SEQ] = 1
    tab[NOPE:MQK, T_COSM:T_COSM + SEQ] = np.concatenate([c, c])
    tab[NOPE:MQK, T_SINM:T_SINM + SEQ] = np.concatenate([-s, s])
    j, i = np.arange(P)[:, None], np.arange(SEQ)[None, :]
    for h in range(RH):
        log_gamma = np.log(1.0 - 2.0 ** (-5.0 - h))
        tab[:, T_DECAY + h * SEQ:T_DECAY + (h + 1) * SEQ] = \
            np.where(i >= j, np.exp(log_gamma * np.maximum(i - j, 0)) * P ** -0.5, 0)
    q, k = np.arange(P)[:, None], np.arange(SEQ)[None, :]
    tab[:, T_CAUSAL:T_CAUSAL + SEQ] = np.where(k <= q + P, 0, NEG)
    rel = q + P - k
    tab[:, T_WINDOW:T_WINDOW + SEQ] = np.where((rel >= 0) & (rel < P), 0, NEG)
    return cst, tab


def buckets():
    rel = np.arange(P)[:, None] + P - np.arange(SEQ)[None, :]
    n = np.maximum(rel, 0)
    exact = 16
    large = exact + (np.log(np.maximum(n, 1) / exact) / np.log(128 / exact) * (32 - exact)).astype(np.int32)
    return np.where(n < exact, n, np.minimum(large, 31)).astype(np.int32)


def lay_out(a):
    L = DEPTH
    mix = np.zeros((L, MIX_TILES, P, D), np.float32)

    def by_columns(w, name, cols=P):
        rows = w.shape[1] // P
        for i in range(w.shape[2] // cols):
            t = w[:, :, i * cols:(i + 1) * cols].reshape(L, rows, P, cols).transpose(0, 2, 1, 3)
            mix[:, TILES[name, i]] = t.reshape(L, P, rows * cols)

    w_in = a["w_in"]
    at = 0
    for name, n in (("rq", 512), ("rk", 512), ("rv", 512), ("rg", 512), ("qa", 256), ("kva", 128), ("kr", 32),
                    ("sq", 512), ("sk", 128), ("sv", 128), ("gate", 3072)):
        w = w_in[:, :, at:at + n]
        at += n
        if name == "kr":
            w = np.concatenate([np.zeros((L, D, NOPE), np.float32), w, np.zeros((L, D, 32), np.float32)], axis=2)
        by_columns(w, name)
    table = a["rel_bias"][buckets()].transpose(2, 0, 1)
    for i in range(2):
        mix[:, TILES["bias", i]] = table[4 * i:4 * i + 4].transpose(1, 0, 2).reshape(P, D)
    qb = a["w_mla_qb"].reshape(L, 2, P, 2, 4 * MQK)
    for i in range(2):
        mix[:, TILES["qb", i], :, 0:8 * MQK] = qb[:, :, :, i].transpose(0, 2, 1, 3).reshape(L, P, 8 * MQK)
    mix[:, TILES["kvb", 0]] = a["w_mla_kvb"].reshape(L, P, MH, 2, 64).transpose(0, 1, 3, 2, 4).reshape(L, P, D)
    for br, name in enumerate(("w_branch_ret", "w_branch_swa", "w_branch_mla")):
        for cg in range(4):
            t = a[name][:, :, cg * 256:(cg + 1) * 256].reshape(L, 4, P, 256).transpose(0, 2, 1, 3)
            mix[:, TILES["branch", cg * 3 + br]] = t.reshape(L, P, D)
    mix[:, TILES["wo", 0]:TILES["wo", 0] + 8] = a["w_out"].reshape(L, 8, P, D)
    by_columns(a["w_xkv"][:, :, 0:512], "xk")
    by_columns(a["w_xkv"][:, :, 512:1024], "xv")
    by_columns(a["w_xq"], "xq")
    mix[:, TILES["xo", 0]:TILES["xo", 0] + 4] = a["w_xo"].reshape(L, 4, P, D)
    by_columns(a["w_peer_query"], "pq")
    mix[:, TILES["keys", 0]] = a["peer_sub_keys"].transpose(0, 2, 4, 1, 3).reshape(L, P, D)
    vecs = np.zeros((L, P, NVEC), np.float32)
    for at, name, n in ((G_MIX, "g_mix", 8), (G_XA, "g_xattn", 8), (G_MEM, "g_mem", 8), (G_FFN, "g_ffn", 8),
                        (G_Q, "mla_q_norm", 2), (G_KV, "mla_kv_norm", 1)):
        vecs[:, :, at:at + n] = a[name].reshape(L, n, P).transpose(0, 2, 1)
    vecs[:, :, SINKS:SINKS + 8] = a["swa_sinks"][:, None, :]
    u = a["peer_u"].reshape(L, NK, NK, DC, P).transpose(0, 2, 4, 3, 1)
    v = a["peer_v"].reshape(L, NK, NK, D).transpose(0, 2, 1, 3)
    return {
        "mix_w": mix, "u_t": np.ascontiguousarray(u).reshape(L, NK, P, D), "v_t": np.ascontiguousarray(v), "vecs": vecs,
        "g_final": np.ascontiguousarray(np.broadcast_to(a["g_final"], (P, D))),
        "x_in": np.ascontiguousarray(a["x"].reshape(NT, P, D).transpose(1, 0, 2)),
        "mem_in": np.ascontiguousarray(a["mem"].reshape(NT, P, D).transpose(1, 0, 2)),
    }


def kernel(**inputs):
    import concourse.bacc as bacc
    from concourse.bass_utils import run_bass_kernel_spmd

    arrays = lay_out({k: np.asarray(v) for k, v in inputs.items()})
    arrays["consts"], arrays["tables"] = constants()
    nc = bacc.Bacc("TRN2", target_bir_lowering=False, num_devices=1)
    aps = {n: nc.dram_tensor(n, a.shape, mybir.dt.from_np(a.dtype), kind="ExternalInput").ap() for n, a in arrays.items()}
    out = nc.dram_tensor("out", (P, NT, D), F32, kind="ExternalOutput").ap()
    trunk(nc, **aps, out=out)
    r = run_bass_kernel_spmd(nc, [arrays], core_ids=[0])
    got = r.results[0]["out"]
    return np.ascontiguousarray(got.transpose(1, 0, 2)).reshape(1, SEQ, D)
```

```python
from contextlib import ExitStack

import numpy as np
import concourse.bass as bass
from concourse import mybir

F32 = mybir.dt.float32
F32R = mybir.dt.float32r
BF16 = mybir.dt.bfloat16
U32 = mybir.dt.uint32
ALU = mybir.AluOpType
ACT = mybir.ActivationFunctionType
AXX = mybir.AxisListType.X

P = 128
D = 1024
DC = D // P
SEQ = 256
NT = SEQ // P
DEPTH = 2
EPS = 1e-6
NEG = -1e30
RH = 4
MH, NOPE, ROPE, MV = 8, 64, 32, 64
MQK = NOPE + ROPE
QR, KVR = 256, 128
SH, SKV, SD = 8, 2, 64
XH, XD = 4, 128
PH, TOPK, NK = 8, 16, 128
SLOTS = 4

TILES = {}


def _tiles():
    n = 0
    for name, count in (("rq", 4), ("rk", 4), ("rv", 4), ("sv", 1), ("qa", 2), ("kva", 1), ("kr", 1),
                        ("sq", 4), ("sk", 1), ("rg", 4), ("bias", 2), ("qb", 2), ("kvb", 1),
                        ("gate", 24), ("branch", 12), ("wo", 8), ("xk", 4), ("xv", 4), ("xq", 4),
                        ("xo", 4), ("pq", 8), ("keys", 1)):
        for i in range(count):
            TILES[name, i] = n
            n += 1
    return n


MIX_TILES = _tiles()
assert MIX_TILES % SLOTS == 0 and NK % SLOTS == 0
ROUNDS = (MIX_TILES + 2 * NK) // SLOTS
U_ROUND0 = MIX_TILES // SLOTS
V_ROUND0 = U_ROUND0 + NK // SLOTS
U_ROUNDS = NK // SLOTS

JOBS, JOB_ORDER = {}, []


def _jobs():
    def job(*name):
        JOBS[name] = len(JOB_ORDER)
        JOB_ORDER.append(name)

    for n in ("x0", "mem"):
        for t in range(NT):
            for half in range(2):
                job(n, t, half)
    ropes = [("rq", i) for i in range(4)] + [("rk", i) for i in range(4)]
    for i, r in enumerate(ropes):
        job(*r)
        if i:
            job("rot", *ropes[i - 1])
    job("rv", 0)
    job("rot", *ropes[-1])
    for i in range(1, 4):
        job("rv", i)
    for n in (("sv", 0), ("qa", 0), ("qa", 1), ("kva", 0), ("kr", 0), ("sq", 0), ("rot", "kr", 0), ("sq", 1),
              ("sq", 2), ("sq", 3), ("tqa", 0), ("tkv", 0), ("sk", 0), ("rg", 0), ("rg", 1), ("rg", 2), ("rg", 3)):
        job(*n)
    for h in range(MH):
        job("qb", h)
        job("kn", h)
        if h:
            job("rot", "qb", h - 1)
    job("mv", 0)
    job("rot", "qb", MH - 1)
    job("mv", 1)
    job("ty", 0)
    job("ty", 1)


def _late_jobs():
    def job(*name):
        JOBS[name] = len(JOB_ORDER)
        JOB_ORDER.append(name)

    for cg in range(4):
        for br in range(3):
            for m in range(2):
                job("branch", cg, br, m)
    for n in ("wo", "xk", "xv"):
        for i in range(4):
            job(n, i)
    for t in range(NT):
        for half in range(2):
            job("x1", t, half)
    for i in range(4):
        job("xq", i)


UNITS = [("swa", t, h) for t in range(NT) for h in range(SH)] + [("mla", t, h) for t in range(NT) for h in range(MH)]
MIX_UNITS = len(UNITS)
UNITS += [("xa", t, h) for t in range(NT) for h in range(XH)]
GROUPS = []
for _v, (_k, _t, _h) in enumerate(UNITS):
    if not GROUPS or GROUPS[-1][:2] != [_k, _t]:
        GROUPS.append([_k, _t, _v, _v])
    GROUPS[-1][3] = _v
LAG = 2
END_AT = {g[3] + LAG: n for n, g in enumerate(GROUPS)}
GATES = 3 * DC


def gates_at(step):
    return range(step * GATES // MIX_UNITS, (step + 1) * GATES // MIX_UNITS)


def mix_steps():
    return range(MIX_UNITS + LAG)


def xa_steps():
    return range(MIX_UNITS, len(UNITS) + LAG)


def _unit_jobs():
    def job(*name):
        JOBS[name] = len(JOB_ORDER)
        JOB_ORDER.append(name)

    for step in mix_steps():
        for g in gates_at(step) if step < MIX_UNITS else ():
            job("gate", g)
        if step - 1 in END_AT:
            job("ty", 2 + END_AT[step - 1])
    job("ty", 2 + 3)


def _xa_jobs():
    def job(*name):
        JOBS[name] = len(JOB_ORDER)
        JOB_ORDER.append(name)

    for step in xa_steps():
        if step - 1 in END_AT and END_AT[step - 1] >= 4:
            job("ty", 2 + END_AT[step - 1])
    job("ty", 2 + 5)
    for i in range(4):
        job("xo", i)
    for t in range(NT):
        for half in range(2):
            job("x2", t, half)
    for i in range(8):
        job("pq", i)
    for t in range(NT):
        for pair in range(PH // 2):
            for half in range(2):
                job("ps", t, pair, half)


_jobs()
_unit_jobs()
_late_jobs()
_xa_jobs()
ROPES = [("rq", i) for i in range(4)] + [("rk", i) for i in range(4)] + [("kr", 0)] + [("qb", h) for h in range(MH)]
NROPE = len(ROPES)
TILE_ENDS = {n: TILES[n] for n in JOB_ORDER if n in TILES and n[0] in
             ("rq", "rk", "rv", "sv", "qa", "kva", "kr", "sq", "sk", "rg", "gate", "xk", "xv", "xq", "pq")}
TILE_ENDS |= {("qb", 3): TILES["qb", 0], ("qb", 7): TILES["qb", 1], ("mv", 1): TILES["kvb", 0],
              ("wo", 3): TILES["wo", 7], ("xo", 3): TILES["xo", 3], ("ps", NT - 1, PH // 2 - 1, 1): TILES["keys", 0]}
TILE_ENDS |= {("branch", cg, br, 1): TILES["branch", cg * 3 + br] for cg in range(4) for br in range(3)}
PLAIN_JOBS = {n: k for k, n in enumerate(n for n in JOB_ORDER if n not in TILE_ENDS)}
GATE_OF = (0, 2, 1)
HALF = D // 2
CHUNK = NK // 2
CHUNK_ROUNDS = CHUNK // SLOTS
BATCH = 512 // CHUNK
TURN_ROUND = CHUNK_ROUNDS - 1
EXP_ROUND = 12
ROUNDS_BELOW = 18
assert EXP_ROUND < TURN_ROUND <= ROUNDS_BELOW
assert CHUNK_ROUNDS * 2 * BATCH == SEQ
LEAST = -3.0e38
NJOBS = len(JOB_ORDER)
JOB_BANKS = 4
BANK_JOBS = [len(range(b, NJOBS, JOB_BANKS)) for b in range(JOB_BANKS)]

G_MIX, G_XA, G_MEM, G_FFN, G_Q, G_KV, SINKS = 0, 8, 16, 24, 32, 34, 35
NVEC = 43
C_ID, C_PERM, C_PERM96, C_IOTA = 0, 128, 256, 352
NCONST = 480
T_COS, T_SIN, T_COSM, T_SINM, T_DECAY, T_CAUSAL, T_WINDOW = 0, 256, 512, 768, 1024, 2048, 2304
NTAB = 2560


class Signal:

    def __init__(self, sem, per_layer, by=1, base=0):
        self.sem, self.per_layer, self.by, self.base = sem, per_layer, by, base

    def after(self, layer, events):
        return self.sem, (layer * self.per_layer + events) * self.by + self.base


def trunk(nc, mix_w, u_t, v_t, vecs, consts, tables, g_final, x_in, mem_in, out):
    ctx = ExitStack()
    with ctx:
        def sb(name, shape, dt=F32):
            return ctx.enter_context(nc.sbuf_tensor(name, shape, dt))

        def sig(name, per_layer=1, by=1, base=0):
            return Signal(ctx.enter_context(nc.semaphore(name)), per_layer, by, base)

        arena = sb("arena", [P, NK * SEQ])
        ring = sb("ring", [P, SLOTS, D])
        hi = sb("table_hi", [P, 2, D], F32R)
        lo = sb("table_lo", [P, 2, D], F32R)
        h_hi = sb("h_hi", [P, DC, SEQ], F32R)
        h_lo = sb("h_lo", [P, DC, SEQ], F32R)
        w_hi = sb("w_hi", [P, 2, SEQ], F32R)
        w_lo = sb("w_lo", [P, 2, SEQ], F32R)
        x = sb("x", [P, NT, D])
        hT = sb("hT", [P, DC, SEQ])
        chosen = sb("chosen", [P, 3, NT, P])
        cst = sb("cst", [P, NCONST])
        vec = sb("vec", [P, NVEC])
        stat = sb("stat", [P, 64])
        negmax = sb("negmax", [P, len(UNITS)])
        sums = sb("sums", [P, len(UNITS)])
        sinkexp = sb("sinkexp", [P, 2, 8])
        rden = sb("rden", [P, 2, 8])
        negsink = sb("negsink", [P, 8])[:, :]
        rowm = sb("rowm", [P, 2])
        rsum = sb("rsum", [P, 8])[:, :]
        hot_gate = sb("hot_gate", [P, 2, 3, BATCH, CHUNK], BF16)

        flat = arena[:, :]
        where = [0]

        def part(n, *dims):
            a = flat[:, where[0]:where[0] + n]
            where[0] += n
            if len(dims) == 2:
                return a.rearrange("p (a b) -> p a b", a=dims[0])
            if len(dims) == 3:
                return a.rearrange("p (a b c) -> p a b c", a=dims[0], b=dims[1])
            return a

        gates = part(3 * DC * SEQ, 3 * DC, SEQ)
        xn = flat[:, 0:2 * D].rearrange("p (t d) -> p t d", t=NT)
        junk = flat[:, 2 * D:3 * D].rearrange("p (t d) -> p t d", t=NT)
        rsq = flat[:, 0:D].rearrange("p (t d) -> p t d", t=NT)
        gfin = flat[:, 3 * D:4 * D]
        mem = part(2 * D, NT, D)
        merged = mem.rearrange("p t d -> p (t d)").rearrange("p (c s) -> p c s", c=DC)
        memT = part(2 * D, DC, SEQ)
        raw = part(2 * SEQ, 2, SEQ)
        cosx = part(2 * SEQ, 2, SEQ)
        sinx = part(2 * SEQ, 2, SEQ)
        at_q = where[0]
        rq = part(4 * SEQ, 4, SEQ)
        rk = part(4 * SEQ, 4, SEQ)
        mq = flat[0:MQK, at_q:at_q + MH * SEQ].rearrange("p (h s) -> p h s", h=MH)
        at_v = where[0]
        rv = part(NT * 512, NT, 512)
        mv = flat[:, at_v:at_v + NT * 512].rearrange("p (t s) -> p t s", t=NT)
        rgs = part(NT * 512, NT, 512)
        sgm = part(SEQ, NT, P)
        qk = part(NT * 384, NT, 384)
        qanT = part(2 * SEQ, 2, SEQ)
        kvanT = part(SEQ)
        krr = part(SEQ)
        mk = part(MH * SEQ, MH, SEQ)
        at_sw = where[0]
        swq = part(4 * SEQ, 4, SEQ)
        swk = part(2 * SEQ, 2, SEQ)
        sv = part(NT * P, NT, P)
        yT = part(3 * 4 * SEQ, 12, SEQ)
        ytok = part(NT * 512, NT, 512)
        tab = part(NTAB)
        bias = part(8 * SEQ, 8, SEQ)
        sm = part(2 * SEQ, 2, SEQ)
        prob = part(2 * SEQ, 2, SEQ)
        probT = part(2 * SEQ, 2, SEQ)
        retT = part(2 * 384, 2, 384)
        assert where[0] <= NK * SEQ, where[0]
        xk = flat[:, at_q:at_q + 4 * SEQ].rearrange("p (h s) -> p h s", h=4)
        xq = flat[:, at_q + 4 * SEQ:at_q + 8 * SEQ].rearrange("p (h s) -> p h s", h=4)
        xv = flat[:, at_v:at_v + NT * 512].rearrange("p (t s) -> p t s", t=NT)
        where[0] = ROUNDS_BELOW * SLOTS * SEQ
        pq = part(8 * SEQ, 8, SEQ)
        sc = part(NT * PH * 2 * NK, NT * PH * 2, NK)
        cand = part(PH * 256, PH, 256)
        onehot = part(PH * 256, PH * TOPK, TOPK)
        top = part(NT * PH * 2 * TOPK, NT * PH * 2, TOPK)
        topf = part(NT * PH * 2 * TOPK, NT * PH * 2, TOPK)
        topi = part(NT * PH * 2 * TOPK, NT * PH * 2, TOPK).bitcast(U32)
        best = part(NT * PH * TOPK, NT * PH, TOPK)
        besti = part(NT * PH * TOPK, NT * PH, TOPK).bitcast(U32)
        posi = part(2 * NT * PH * TOPK, 2, NT * PH * TOPK).bitcast(U32)
        posf = part(2 * NT * PH * TOPK, 2 * NT, PH * TOPK)
        bestmax = part(NT * PH).unsqueeze(2)
        bestsum = part(NT * PH)
        assert where[0] <= NK * SEQ, where[0]
        hflat = hT[:, :, :].rearrange("p c s -> p (c s)")
        chosenT = hflat[:, 0:3 * SEQ].rearrange("p (a s) -> p a s", a=3)
        spare = hflat[:, 3 * SEQ:].bitcast(BF16)
        hot1 = spare[:, 0:2 * BATCH * P].rearrange("p (b k n) -> p b k n", b=2, k=BATCH)
        turned = chosen[:, :, :, :].rearrange("p a t n -> p (a t n)").bitcast(BF16)
        hot2 = turned[:, 0:2 * BATCH * CHUNK].rearrange("p (b k n) -> p b k n", b=2, k=BATCH)
        gate_part = spare[:, 2 * BATCH * P:2 * BATCH * P + 2 * SEQ].rearrange("p (a s) -> p a s", a=2)
        gate_parts = [gate_part[:, 0], gate_part[:, 1], turned[:, 2 * BATCH * CHUNK:2 * BATCH * CHUNK + SEQ]]
        pre = arena[:, :].rearrange("p (g s) -> p g s", g=NK)

        ident = cst[:, C_ID:C_ID + P]
        perm = cst[:, C_PERM:C_PERM + P]
        perm96 = cst[0:MQK, C_PERM96:C_PERM96 + MQK]
        iota = cst[:, C_IOTA:C_IOTA + P]
        cos, sin = tab[:, T_COS:T_COS + SEQ], tab[:, T_SIN:T_SIN + SEQ]
        cosm, sinm = tab[0:MQK, T_COSM:T_COSM + SEQ], tab[0:MQK, T_SINM:T_SINM + SEQ]
        decay = tab[:, T_DECAY:T_DECAY + 4 * SEQ].rearrange("p (h s) -> p h s", h=4)
        causal = tab[:, T_CAUSAL:T_CAUSAL + SEQ]
        window = tab[:, T_WINDOW:T_WINDOW + SEQ]

        bank = [ctx.enter_context(nc.psum_tensor(f"bank{b}", [P, 512], F32))[:, :] for b in range(8)]


        slot_full = [sig(f"slot_full{s}", ROUNDS, 16) for s in range(SLOTS)]
        slot_done = [sig(f"slot_done{s}", ROUNDS, base=1) for s in range(SLOTS)]
        job_full = sig("job_full", len(PLAIN_JOBS))
        job_stored = [sig(f"job_stored{b}", BANK_JOBS[b], base=1) for b in range(JOB_BANKS)]
        x_loaded = sig("x_loaded")
        cst_loaded = sig("cst_loaded")
        vec_loaded = sig("vec_loaded", 1, 16)
        tab_loaded = sig("tab_loaded", 1, 16)
        mem_loaded = sig("mem_loaded", 1, 16)
        squares = sig("squares", 8)
        meansq = sig("meansq", 4)
        root = sig("root", 4)
        rstd = sig("rstd", 4)
        normed = sig("normed", 8)
        raw_cos = sig("raw_cos", NROPE)
        roped = sig("roped", NROPE)
        kr_spread = sig("kr_spread")
        qk_sq = sig("qk_sq", 4)
        qk_ms = sig("qk_ms", 2)
        qk_root = sig("qk_root")
        qk_rstd = sig("qk_rstd")
        qk_normed = sig("qk_normed", 4)
        gate_sig = sig("gate_sig", 4)
        bias_ready = sig("bias_ready")
        score_full = sig("score_full", RH + len(UNITS))
        ret_scores = sig("ret_scores", RH)
        ret_full = sig("ret_full", RH)
        ret_stored = sig("ret_stored", RH)
        ret_sq = sig("ret_sq", NT)
        ret_sum = sig("ret_sum", NT)
        ret_ms = sig("ret_ms")
        ret_root = sig("ret_root")
        ret_rstd = sig("ret_rstd")
        ret_scaled = sig("ret_scaled", NT)
        ytok_ready = sig("ytok_ready", NT + len(GROUPS))
        masked = sig("masked", MIX_UNITS)
        rowmax = sig("rowmax", SH * NT)
        negmax_ready = sig("negmax_ready", len(UNITS))
        prob_ready = sig("prob_ready", len(UNITS))
        probT_full = sig("probT_full", len(UNITS))
        probT_ready = sig("probT_ready", len(UNITS))
        pv_done = sig("pv_done", len(UNITS))
        sink_shift = sig("sink_shift", NT)
        sink_exp = sig("sink_exp", NT)
        den_ready = sig("den_ready", NT)
        rden_ready = sig("rden_ready", len(GROUPS))
        gates_open = sig("gates_open", 12)
        gated = sig("gated", 16)
        peer_added = sig("peer_added", 4, base=1)
        sink_negated, best_top = sig("sink_negated"), sig("best_top")
        xa_max = sig("xa_max", XH * NT)
        settled = sig("settled")
        h_split = sig("h_split", 2)
        top1, top_idx1, top_cut, top2, top_idx2, top_float = (
            sig(n) for n in ("top1", "top_idx1", "top_cut", "top2", "top_idx2", "top_float"))
        cand_ready, best1, best_idx1, best_cut, best2, best_idx2 = (
            sig(n, NT) for n in ("cand_ready", "best1", "best_idx1", "best_cut", "best2", "best_idx2"))
        pos_split, pos_float = sig("pos_split"), sig("pos_float")
        onehot_ready, picked, index_ready = (sig(n, 2 * NT) for n in ("onehot_ready", "picked", "index_ready"))
        best_shift, best_exp, best_sum, best_rsum, choice_made = (
            sig(n) for n in ("best_shift", "best_exp", "best_sum", "best_rsum", "choice_made"))
        choice_turned = sig("choice_turned", 3)
        choiceT_ready = sig("choiceT_ready", 3)
        high_ready = [sig(f"high_ready{h}", NK) for h in range(4)]
        part_used = [sig(f"part_used{h}", NK, base=1) for h in range(4)]
        low_first = [sig(f"low_first{b}", NK) for b in range(2)]
        pre_stored = [sig(f"pre_stored{b}", U_ROUNDS, base=1) for b in range(SLOTS)]
        hot2_open = [sig(f"hot2_open{b}", U_ROUNDS) for b in range(2)]
        hot_ready = [sig(f"hot_ready{b}", U_ROUNDS) for b in range(2)]
        pool_hot_ready = [sig(f"pool_hot_ready{b}", CHUNK_ROUNDS) for b in range(2)]
        gate_rest = sig("gate_rest", 5)
        spread = [sig(f"spread{b}", U_ROUNDS, base=1) for b in range(2)]
        cells_gated = [sig(f"cells_gated{b}", U_ROUNDS, base=1) for b in range(2)]
        w_high = [sig(f"w_high{b}", NK // 2) for b in range(2)]
        w_low = [sig(f"w_low{b}", NK // 2) for b in range(2)]
        f_sq, f_ms, f_root, f_rstd, f_scaled, f_ready, gf_loaded, stored = (
            sig(n) for n in ("f_sq", "f_ms", "f_root", "f_rstd", "f_scaled", "f_ready", "gf_loaded", "stored"))

        def settle(eng):
            eng.sem_inc(settled.sem, 1)

        def start(eng, *signals):
            for signal in signals:
                eng.sem_inc(signal.sem, 1)

        def tile(name, i=0):
            return ring[:, TILES[name, i] % SLOTS, :]

        def loaded(layer, name, i=0):
            n = TILES[name, i]
            return slot_full[n % SLOTS].after(layer, n // SLOTS + 1)

        def bank_of(*name):
            return bank[JOBS[name] % JOB_BANKS]

        def bank_free(layer, *name):
            k = JOBS[name]
            return job_stored[k % JOB_BANKS].after(layer, k // JOB_BANKS)

        def ends(*name):
            if name in TILE_ENDS:
                return slot_done[TILE_ENDS[name] % SLOTS].sem, 1
            return job_full.sem, 1

        def full(layer, *name):
            if name in TILE_ENDS:
                n = TILE_ENDS[name]
                return slot_done[n % SLOTS].after(layer, n // SLOTS + 1)
            return job_full.after(layer, PLAIN_JOBS[name] + 1)

        def stores(*name):
            return job_stored[JOBS[name] % JOB_BANKS].sem, 1

        def in_sbuf(layer, *name):
            k = JOBS[name]
            return job_stored[k % JOB_BANKS].after(layer, k // JOB_BANKS + 1)

        block = ctx.enter_context(nc.Block())

        @block.sync
        def _(sp):
            start(sp, *slot_done, *job_stored, peer_added, *part_used, *pre_stored, *spread, *cells_gated)
            sp.dma_start(cst[:, :], consts).then_inc(cst_loaded.sem, 16)
            sp.dma_start(x[:, :, :], x_in).then_inc(x_loaded.sem, 16)
            with sp.Fori(0, DEPTH) as layer:
                with sp.Fori(0, U_ROUND0) as r:
                    for s in range(SLOTS):
                        sp.wait_ge(*slot_done[s].after(layer, r))
                        sp.dma_start(ring[:, s, :], mix_w[layer, r * SLOTS + s]).then_inc(slot_full[s].sem, 16)
                for table, first in ((u_t, U_ROUND0), (v_t, V_ROUND0)):
                    with sp.Fori(0, U_ROUNDS) as r:
                        for s in range(SLOTS):
                            sp.wait_ge(*slot_done[s].after(layer, r + first))
                            sp.dma_start(ring[:, s, :], table[layer, r * SLOTS + s]).then_inc(slot_full[s].sem, 16)
            sp.wait_ge(f_ready.sem, 1)
            sp.dma_start(out, xn).then_inc(stored.sem, 16)
            sp.wait_ge(stored.sem, 16)

        @block.gpsimd
        def _(pool):
            pool.wait_ge(cst_loaded.sem, 16)
            with pool.Fori(0, DEPTH) as layer:
                pool.wait_ge(*peer_added.after(layer, 0))
                pool.dma_start(vec[:, :], vecs[layer]).then_inc(vec_loaded.sem, 16)
                pool.dma_start(mem, mem_in).then_inc(mem_loaded.sem, 16)
                pool.dma_start(tab, tables).then_inc(tab_loaded.sem, 16)
                for i in range(2):
                    pool.wait_ge(*loaded(layer, "bias", i))
                    w = tile("bias", i)
                    settle(pool)
                    pool.tensor_copy(bias[:, 4 * i:4 * i + 4, :], w.rearrange("p (h s) -> p h s", h=4)) \
                        .then_inc(slot_done[TILES["bias", i] % SLOTS].sem, 1)
                for i in range(2):
                    pool.wait_ge(*slot_done[TILES["bias", i] % SLOTS].after(layer, TILES["bias", i] // SLOTS + 1))
                pool.wait_ge(*tab_loaded.after(layer, 1))
                pool.tensor_tensor(bias, bias, window.unsqueeze(1).broadcast_to([P, 8, SEQ]), ALU.add) \
                    .then_inc(bias_ready.sem, 1)
                pool.wait_ge(*bias_ready.after(layer, 1))
                pool.wait_ge(*roped.after(layer, ROPES.index(("kr", 0)) + 1))
                settle(pool)
                pool.tensor_copy(mk[NOPE:MQK, :, :], krr[NOPE:MQK, :].unsqueeze(1).broadcast_to([ROPE, MH, SEQ])) \
                    .then_inc(kr_spread.sem, 1)
                pool.wait_ge(*kr_spread.after(layer, 1))
                settle(pool)
                with pool.Fori(0, U_ROUNDS) as r:
                    for s in range(SLOTS):
                        b = s % 2
                        pool.wait_ge(*high_ready[2 * b].after(layer, r * 2 + s // 2 + 1))
                        pool.tensor_tensor(lo[:, b, 0:HALF], ring[:, s, 0:HALF], hi[:, b, 0:HALF].bitcast(F32),
                                           ALU.subtract).then_inc(low_first[b].sem, 1)
                        pool.wait_ge(*high_ready[2 * b + 1].after(layer, r * 2 + s // 2 + 1))
                        pool.tensor_tensor(lo[:, b, HALF:D], ring[:, s, HALF:D], hi[:, b, HALF:D].bitcast(F32),
                                           ALU.subtract).then_inc(slot_done[s].sem, 1)
                def pool_hots(q, b):
                    toks = bass.ds(q * (2 * BATCH) + b * BATCH, BATCH)
                    pool.wait_ge(*hot2_open[b].after(layer, CHUNK_ROUNDS + q + 1))
                    settle(pool)
                    for n in (1, 2):
                        last = pool.tensor_tensor(hot_gate[:, b, n], hot2[:, b],
                                                  gate_parts[n][:, toks].unsqueeze(2).broadcast_to([P, BATCH, CHUNK]), ALU.mult)
                    last.then_inc(pool_hot_ready[b].sem, 1)

                def pool_lows(r):
                    for b in range(2):
                        pool.wait_ge(*w_high[b].after(layer, r + 1))
                        settle(pool)
                        pool.tensor_tensor(w_lo[:, b, :], pre[:, bass.ds(r * 2 + b, 1), :].squeeze(1), w_hi[:, b, :].bitcast(F32),
                                           ALU.subtract).then_inc(w_low[b].sem, 1)

                pool_hots(0, 0)
                pool_hots(0, 1)
                with pool.Fori(0, CHUNK_ROUNDS - 1) as q:
                    for b in range(2):
                        pool_lows(q * 2 + b)
                        pool_hots(q + 1, b)
                with pool.Fori((CHUNK_ROUNDS - 1) * 2, NK // 2) as r:
                    pool_lows(r)
            pool.wait_ge(*peer_added.after(DEPTH, 0))
            pool.dma_start(gfin, g_final).then_inc(gf_loaded.sem, 16)

        @block.tensor
        def _(pe):
            def project(layer, name, i, src, cols=P):
                pe.wait_ge(*bank_free(layer, name, i))
                ps = bank_of(name, i)
                pe.wait_ge(*loaded(layer, name, i))
                w = tile(name, i)
                for c in range(DC):
                    last = pe.matmul(ps[0:cols, 0:SEQ], w[:, c * P:c * P + cols], src[:, c, :],
                                     start=(c == 0), stop=(c == DC - 1))
                last.then_inc(*ends(name, i))

            def project_tok(layer, name, i, src):
                pe.wait_ge(*bank_free(layer, name, i))
                ps = bank_of(name, i)
                pe.wait_ge(*loaded(layer, name, i))
                w = tile(name, i)
                for t in range(NT):
                    for c in range(DC):
                        last = pe.matmul(ps[:, t * P:t * P + P], src[:, c, t * P:t * P + P], w[:, c * P:c * P + P],
                                         start=(c == 0), stop=(c == DC - 1))
                last.then_inc(*ends(name, i))

            def turn(layer, src, *name):
                pe.wait_ge(*bank_free(layer, *name))
                ps = bank_of(*name)
                for k, s in enumerate(src):
                    last = pe.transpose(ps[:, k * P:k * P + P], s, ident)
                last.then_inc(*ends(*name))

            def turn_norm(layer, name, order):
                src = mem if name == "mem" else xn
                for t in range(NT):
                    pe.wait_ge(*normed.after(layer, 2 * order + t + 1))
                    for half in range(2):
                        turn(layer, [src[:, t, c * P:c * P + P] for c in range(4 * half, 4 * half + 4)], name, t, half)

            def rotate(layer, k):
                name = ROPES[k]
                pe.wait_ge(*bank_free(layer, "rot", *name))
                ps = bank_of("rot", *name)
                pe.wait_ge(*in_sbuf(layer, *name))
                if name[0] in ("rq", "rk"):
                    last = pe.matmul(ps[:, 0:SEQ], perm, raw[:, k % 2, :], start=True, stop=True)
                else:
                    last = pe.matmul(ps[0:MQK, 0:SEQ], perm96, raw[0:MQK, k % 2, :], start=True, stop=True)
                last.then_inc(*ends("rot", *name))

            def open_scores(layer, u):
                if u < 2:
                    pe.wait_ge(*peer_added.after(layer, 0))
                elif u - 2 < RH:
                    pe.wait_ge(*ret_scores.after(layer, u - 1))
                elif u - 2 < RH + MIX_UNITS:
                    pe.wait_ge(*masked.after(layer, u - 2 - RH + 1))
                else:
                    pe.wait_ge(*prob_ready.after(layer, u - 2 - RH + 1))
                return bank[4 + u % 2]

            def ret_score(layer, h):
                ps = open_scores(layer, h)
                pe.wait_ge(*roped.after(layer, 4 + h + 1))
                pe.matmul(ps[:, 0:SEQ], rk[:, h, 0:P], rq[:, h, :], start=True, stop=True)
                pe.matmul(ps[:, SEQ:SEQ + P], rk[:, h, P:SEQ], rq[:, h, P:SEQ], start=True, stop=True) \
                    .then_inc(score_full.sem, 1)

            def ret_out(layer, h):
                ps = bank[6 + h % 2]
                if h >= 2:
                    pe.wait_ge(*ret_stored.after(layer, h - 1))
                else:
                    pe.wait_ge(*in_sbuf(layer, "rv", 3))
                pe.wait_ge(*ret_scores.after(layer, h + 1))
                v = [rv[:, t, h * P:h * P + P] for t in range(NT)]
                s = retT[:, h % 2, :]
                pe.matmul(ps[:, 0:P], s[:, 0:P], v[0], start=True, stop=True)
                pe.matmul(ps[:, P:2 * P], s[:, P:2 * P], v[0], start=True, stop=False)
                pe.matmul(ps[:, P:2 * P], s[:, 2 * P:3 * P], v[1], start=False, stop=True).then_inc(ret_full.sem, 1)

            def turn_y(layer, n):
                pe.wait_ge(*ytok_ready.after(layer, n + 1))
                turn(layer, [ytok[:, n % 2, c * P:c * P + P] for c in range(4)], "ty", n)

            def scores(layer, v):
                kind, t, h = UNITS[v]
                ps = open_scores(layer, RH + v)
                keys = SEQ if kind == "xa" else P * (t + 1)
                q = slice(t * P, t * P + P)
                if kind == "swa":
                    lhs, rhs = swq[64 * (h % 2):64 * (h % 2) + 64, h // 2, q], swk[64 * (h % 2):64 * (h % 2) + 64, h // 4, 0:keys]
                elif kind == "mla":
                    lhs, rhs = mq[:, h, q], mk[0:MQK, h, 0:keys]
                    pe.wait_ge(*roped.after(layer, 9 + h + 1))
                    pe.wait_ge(*kr_spread.after(layer, 1))
                    pe.wait_ge(*in_sbuf(layer, "kn", h))
                else:
                    lhs, rhs = xq[:, h, q], xk[:, h, :]
                    pe.wait_ge(*in_sbuf(layer, "xq", h))
                pe.matmul(ps[:, 0:keys], lhs, rhs, start=True, stop=True).then_inc(score_full.sem, 1)

            def turn_probs(layer, v):
                kind, t, h = UNITS[v]
                blocks = 2 if kind == "xa" else t + 1
                pe.wait_ge(*prob_ready.after(layer, v + 1))
                if v:
                    pe.wait_ge(*probT_ready.after(layer, v))
                else:
                    pe.wait_ge(*ret_stored.after(layer, RH))
                for c in range(blocks):
                    last = pe.transpose(bank[6][:, c * P:c * P + P], prob[:, v % 2, c * P:c * P + P], ident)
                last.then_inc(probT_full.sem, 1)

            def weigh(layer, v):
                kind, t, h = UNITS[v]
                blocks = 2 if kind == "xa" else t + 1
                g = next(n for n, g in enumerate(GROUPS) if g[2] <= v <= g[3])
                if v == GROUPS[g][2]:
                    if g:
                        pe.wait_ge(*ytok_ready.after(layer, NT + g))
                    else:
                        pe.wait_ge(*ret_stored.after(layer, RH))
                pe.wait_ge(*probT_ready.after(layer, v + 1))
                for c in range(blocks):
                    if kind == "swa":
                        o, val = bank[7][:, h * SD:h * SD + SD], sv[:, c, (h // 4) * SD:(h // 4) * SD + SD]
                    elif kind == "mla":
                        o, val = bank[7][:, h * MV:h * MV + MV], mv[:, c, h * MV:h * MV + MV]
                    else:
                        o, val = bank[7][:, h * XD:h * XD + XD], xv[:, c, h * XD:h * XD + XD]
                    last = pe.matmul(o, probT[:, v % 2, c * P:c * P + P], val, start=(c == 0), stop=(c == blocks - 1))
                last.then_inc(pv_done.sem, 1)

            def attend(layer, step, units):
                if step in units:
                    scores(layer, step)
                if step - 1 in units:
                    turn_probs(layer, step - 1)
                if step - 2 in units:
                    weigh(layer, step - 2)

            def product4(layer, name, tiles, src):
                for i in range(4):
                    pe.wait_ge(*bank_free(layer, name, i))
                for n in range(tiles):
                    pe.wait_ge(*loaded(layer, name, n))
                    w = tile(name, n)
                    for i in range(4):
                        t, half = i // 2, i % 2
                        last = pe.matmul(bank_of(name, i)[:, :], src[:, n, t * P:t * P + P], w[:, half * 512:half * 512 + 512],
                                         start=(n == 0), stop=(n == tiles - 1))
                        if n == tiles - 1:
                            last.then_inc(*ends(name, i))
                    if n < tiles - 1:
                        last.then_inc(slot_done[TILES[name, n] % SLOTS].sem, 1)

            pe.wait_ge(cst_loaded.sem, 16)
            with pe.Fori(0, DEPTH) as layer:
                turn_norm(layer, "x0", 0)
                turn_norm(layer, "mem", 1)
                pe.wait_ge(*in_sbuf(layer, "x0", 1, 1))
                for k in range(9):
                    if k < 8:
                        project(layer, *ROPES[k], hT)
                    else:
                        project_tok(layer, "rv", 0, hT)
                    if k:
                        rotate(layer, k - 1)
                for i in range(1, 4):
                    project_tok(layer, "rv", i, hT)
                project_tok(layer, "sv", 0, hT)
                ret_score(layer, 0)
                project_tok(layer, "qa", 0, hT)
                ret_score(layer, 1)
                ret_out(layer, 0)
                project_tok(layer, "qa", 1, hT)
                ret_score(layer, 2)
                ret_out(layer, 1)
                project_tok(layer, "kva", 0, hT)
                ret_score(layer, 3)
                ret_out(layer, 2)
                project(layer, "kr", 0, hT, MQK)
                ret_out(layer, 3)
                project(layer, "sq", 0, hT)
                rotate(layer, 8)
                for i in range(1, 4):
                    project(layer, "sq", i, hT)
                pe.wait_ge(*qk_normed.after(layer, 4))
                turn(layer, [qk[:, t, c * P:c * P + P] for c in range(2) for t in range(NT)], "tqa", 0)
                turn(layer, [qk[:, t, QR:QR + P] for t in range(NT)], "tkv", 0)
                project(layer, "sk", 0, hT)
                for i in range(4):
                    project_tok(layer, "rg", i, hT)
                pe.wait_ge(*in_sbuf(layer, "tqa", 0))
                pe.wait_ge(*in_sbuf(layer, "tkv", 0))
                wkv = None
                for h in range(MH):
                    pe.wait_ge(*bank_free(layer, "qb", h))
                    ps = bank_of("qb", h)
                    pe.wait_ge(*loaded(layer, "qb", h // 4))
                    w = tile("qb", h // 4)
                    for c in range(2):
                        o = (c * 4 + h % 4) * MQK
                        last = pe.matmul(ps[0:MQK, 0:SEQ], w[:, o:o + MQK], qanT[:, c, :], start=(c == 0), stop=(c == 1))
                    last.then_inc(*ends("qb", h))
                    pe.wait_ge(*bank_free(layer, "kn", h))
                    ps = bank_of("kn", h)
                    pe.wait_ge(*loaded(layer, "kvb"))
                    w = tile("kvb")
                    pe.matmul(ps[0:NOPE, 0:SEQ], w[:, h * NOPE:h * NOPE + NOPE], kvanT, start=True, stop=True).then_inc(*ends("kn", h))
                    if h:
                        rotate(layer, 9 + h - 1)
                for t in range(NT):
                    pe.wait_ge(*bank_free(layer, "mv", t))
                    ps = bank_of("mv", t)
                    pe.matmul(ps[:, :], kvanT[:, t * P:t * P + P], w[:, 512:1024], start=True, stop=True).then_inc(*ends("mv", t))
                    if t == 0:
                        rotate(layer, 9 + MH - 1)
                turn_y(layer, 0)
                turn_y(layer, 1)
                pe.wait_ge(*in_sbuf(layer, "sk", 0))
                for step in mix_steps():
                    if step < MIX_UNITS:
                        for g in gates_at(step):
                            project(layer, "gate", g, hT)
                    attend(layer, step, range(MIX_UNITS))
                    if step - 1 in END_AT:
                        turn_y(layer, 2 + END_AT[step - 1])
                turn_y(layer, 5)
                pe.wait_ge(*in_sbuf(layer, "ty", 5))
                for cg in range(4):
                    for br in range(3):
                        pe.wait_ge(*loaded(layer, "branch", cg * 3 + br))
                        w = tile("branch", cg * 3 + br)
                        for m in range(2):
                            pe.wait_ge(*bank_free(layer, "branch", cg, br, m))
                            ps = bank_of("branch", cg, br, m)
                            for c in range(4):
                                last = pe.matmul(ps[:, 0:SEQ], w[:, c * 256 + m * P:c * 256 + m * P + P], yT[:, br * 4 + c, :],
                                                 start=(c == 0), stop=(c == 3))
                            last.then_inc(*ends("branch", cg, br, m))
                pe.wait_ge(*gated.after(layer, 16))
                product4(layer, "wo", 8, merged)
                pe.wait_ge(*in_sbuf(layer, "mem", 1, 1))
                for i in range(4):
                    project(layer, "xk", i, memT)
                for i in range(4):
                    project_tok(layer, "xv", i, memT)
                turn_norm(layer, "x1", 2)
                pe.wait_ge(*in_sbuf(layer, "x1", 1, 1))
                for i in range(4):
                    project(layer, "xq", i, hT)
                for step in xa_steps():
                    attend(layer, step, range(MIX_UNITS, len(UNITS)))
                    if step - 1 in END_AT and END_AT[step - 1] >= 4:
                        turn_y(layer, 2 + END_AT[step - 1])
                turn_y(layer, 7)
                pe.wait_ge(*in_sbuf(layer, "ty", 7))
                product4(layer, "xo", 4, yT)
                turn_norm(layer, "x2", 3)
                pe.wait_ge(*in_sbuf(layer, "x2", 1, 1))
                for i in range(8):
                    project(layer, "pq", i, hT)
                pe.wait_ge(*in_sbuf(layer, "pq", 7))
                pe.wait_ge(*loaded(layer, "keys"))
                w = tile("keys")
                for t in range(NT):
                    for pair in range(PH // 2):
                        for p in range(2):
                            pe.wait_ge(*bank_free(layer, "ps", t, pair, p))
                            ps = bank_of("ps", t, pair, p)
                            for k in range(2):
                                h = 2 * pair + k
                                last = pe.matmul(ps[:, k * NK:k * NK + NK], pq[64 * p:64 * p + 64, h, t * P:t * P + P],
                                                 w[64 * p:64 * p + 64, h * NK:h * NK + NK], start=True, stop=True)
                            last.then_inc(*ends("ps", t, pair, p))
                pe.wait_ge(*h_split.after(layer, 2))
                settle(pe)

                def spread_gates(chunk, q, b):
                    step = q + chunk * CHUNK_ROUNDS
                    pe.wait_ge(*cells_gated[b].after(layer, step))
                    pe.wait_ge(*hot_ready[b].after(layer, step + 1))
                    if chunk:
                        pe.wait_ge(*pool_hot_ready[b].after(layer, q + 1))
                    for k in range(BATCH):
                        for n in range(3):
                            last = pe.matmul(bank[b][:, k * CHUNK:k * CHUNK + CHUNK], hot1[:, b, k, :], hot_gate[:, b, n, k, :],
                                             start=(n == 0), stop=(n == 2))
                    last.then_inc(spread[b].sem, 1)

                def pre_activations(r, q=None):
                    for s in range(SLOTS):
                        b = s % 2
                        if q is not None and b == 0:
                            spread_gates(0, q, s // 2)
                        pe.wait_ge(*pre_stored[s].after(layer, r))
                        for half in range(2):
                            if half == 0:
                                pe.wait_ge(*low_first[b].after(layer, r * 2 + s // 2 + 1))
                            else:
                                pe.wait_ge(*slot_done[s].after(layer, U_ROUND0 + r + 1))
                            for c in range(4 * half, 4 * half + 4):
                                cols = slice(c * P, c * P + P)
                                for k, (a, h) in enumerate(((hi, h_hi), (hi, h_lo), (lo, h_hi))):
                                    last = pe.matmul(bank[4 + s][:, 0:SEQ], a[:, b, cols], h[:, c, :],
                                                     start=(c == 0 and k == 0), stop=(c == DC - 1 and k == 2))
                            last.then_inc(part_used[2 * b + half].sem, 1)

                with pe.Fori(0, TURN_ROUND) as r:
                    pre_activations(r)
                pe.wait_ge(*choice_made.after(layer, 1))
                pe.wait_ge(*in_sbuf(layer, "ps", NT - 1, PH // 2 - 1, 1))
                for a in range(3):
                    for t in range(NT):
                        last = pe.transpose(bank[a][:, t * P:t * P + P], chosen[:, a, t, :], ident)
                    last.then_inc(choice_turned.sem, 1)
                pre_activations(TURN_ROUND)
                with pe.Fori(0, CHUNK_ROUNDS) as q:
                    pre_activations(q + CHUNK_ROUNDS, q)
                for s in range(4):
                    pe.wait_ge(*pre_stored[s].after(layer, U_ROUNDS))

                def down(r, q=None, first=False, final=False):
                    for s in range(SLOTS):
                        b = s % 2
                        if q is not None and b == 0:
                            spread_gates(1, q, s // 2)
                        pe.wait_ge(*w_low[b].after(layer, r * 2 + s // 2 + 1))
                        for half in range(2):
                            if half == 0:
                                pe.wait_ge(*low_first[b].after(layer, NK // 2 + r * 2 + s // 2 + 1))
                            else:
                                pe.wait_ge(*slot_done[s].after(layer, V_ROUND0 + r + 1))
                            for t in range(NT):
                                tok, cols = slice(t * P, t * P + P), slice(half * HALF, half * HALF + HALF)
                                for k, (a, v) in enumerate(((w_hi, hi), (w_hi, lo), (w_lo, hi))):
                                    last = pe.matmul(bank[4 + 2 * t + half][:, :], a[:, b, tok], v[:, b, cols],
                                                     start=(first and s == 0 and k == 0),
                                                     stop=(final and s == SLOTS - 1 and k == 2))
                            last.then_inc(part_used[2 * b + half].sem, 1)

                down(0, 0, first=True)
                with pe.Fori(1, CHUNK_ROUNDS) as r:
                    down(r, r)
                with pe.Fori(CHUNK_ROUNDS, U_ROUNDS - 1) as r:
                    down(r)
                down(U_ROUNDS - 1, final=True)

        @block.scalar
        def _(act):
            def copy_job(layer, dst, src, *name):
                act.wait_ge(*full(layer, *name))
                act.activation(dst, src, ACT.Copy).then_inc(*stores(*name))

            def square_sums(layer, src, junk, order, col):
                for t in range(NT):
                    act.activation(junk[:, t, :], src[:, t, :], ACT.Square, accum_out=stat[:, col + t:col + t + 1]) \
                        .then_inc(squares.sem, 1)
                act.wait_ge(*meansq.after(layer, order + 1))
                act.activation(stat[:, col + 4:col + 6], stat[:, col + 2:col + 4], ACT.Sqrt).then_inc(root.sem, 1)

            def both(name, i, cols=P):
                return bank_of(name, i)[:, 0:NT * P].rearrange("p (t c) -> p t c", t=NT)

            def raw_copy(layer, k):
                name = ROPES[k]
                rows = P if name[0] in ("rq", "rk") else MQK
                if k >= 2:
                    act.wait_ge(*raw_cos.after(layer, k - 1))
                    act.wait_ge(*full(layer, "rot", *ROPES[k - 2]))
                copy_job(layer, raw[0:rows, k % 2, :], bank_of(*name)[0:rows, 0:SEQ], *name)

            def ret_store(layer, h):
                act.wait_ge(*ret_full.after(layer, h + 1))
                act.activation(ytok[:, :, h * P:h * P + P], bank[6 + h % 2][:, 0:2 * P].rearrange("p (t e) -> p t e", t=NT),
                               ACT.Copy).then_inc(ret_stored.sem, 1)

            def yT_store(layer, n):
                copy_job(layer, yT[:, (n // 2 % 3) * 4:(n // 2 % 3) * 4 + 4, (n % 2) * P:(n % 2) * P + P],
                         bank_of("ty", n).rearrange("p (c s) -> p c s", c=4), "ty", n)

            def soft(layer, step, units):
                if step in units:
                    kind, t, h = UNITS[step]
                    keys = SEQ if kind == "xa" else P * (t + 1)
                    act.wait_ge(*negmax_ready.after(layer, step + 1))
                    if step >= 2:
                        act.wait_ge(*probT_full.after(layer, step - 1))
                    src = bank[4 + (RH + step) % 2][:, 0:keys] if kind == "xa" else sm[:, step % 2, 0:keys]
                    act.activation(prob[:, step % 2, 0:keys], src, ACT.Exp, bias=negmax[:, step:step + 1],
                                   scale=XD ** -0.5 if kind == "xa" else 1.0,
                                   accum_out=sums[:, step:step + 1]).then_inc(prob_ready.sem, 1)
                if step - 1 in units:
                    v = step - 1
                    kind, t, h = UNITS[v]
                    keys = SEQ if kind == "xa" else P * (t + 1)
                    act.wait_ge(*probT_full.after(layer, v + 1))
                    if v >= 2:
                        act.wait_ge(*pv_done.after(layer, v - 1))
                    act.activation(probT[:, v % 2, 0:keys], bank[6][:, 0:keys], ACT.Copy).then_inc(probT_ready.sem, 1)
                if step in END_AT and END_AT[step] < NT:
                    g = END_AT[step]
                    act.wait_ge(*sink_shift.after(layer, g + 1))
                    act.activation(sinkexp[:, g, :], sinkexp[:, g, :], ACT.Exp).then_inc(sink_exp.sem, 1)

            with act.Fori(0, DEPTH) as layer:
                act.wait_ge(x_loaded.sem, 16)
                act.wait_ge(*peer_added.after(layer, 0))
                square_sums(layer, x, xn, 0, 0)
                act.wait_ge(*mem_loaded.after(layer, 1))
                square_sums(layer, mem, memT.rearrange("p c s -> p (c s)").rearrange("p (t d) -> p t d", t=NT), 1, 8)
                for k in range(8):
                    raw_copy(layer, k)
                for i in range(4):
                    copy_job(layer, rv[:, :, i * P:i * P + P], both("rv", i), "rv", i)
                copy_job(layer, sv, both("sv", 0), "sv", 0)
                for i in range(2):
                    copy_job(layer, qk[:, :, i * P:i * P + P], both("qa", i), "qa", i)
                ret_store(layer, 0)
                ret_store(layer, 1)
                copy_job(layer, qk[:, :, QR:QR + P], both("kva", 0), "kva", 0)
                act.wait_ge(*in_sbuf(layer, "kva", 0))
                for t in range(NT):
                    for k, cols in enumerate((slice(0, QR), slice(QR, QR + KVR))):
                        act.activation(junk[:, t, cols], qk[:, t, cols], ACT.Square,
                                       accum_out=stat[:, 32 + 2 * k + t:33 + 2 * k + t]).then_inc(qk_sq.sem, 1)
                ret_store(layer, 2)
                raw_copy(layer, 8)
                ret_store(layer, 3)
                copy_job(layer, swq[:, 0, :], bank_of("sq", 0)[:, 0:SEQ], "sq", 0)
                act.wait_ge(*qk_ms.after(layer, 2))
                act.activation(stat[:, 40:44], stat[:, 36:40], ACT.Sqrt).then_inc(qk_root.sem, 1)
                for i in range(1, 4):
                    copy_job(layer, swq[:, i, :], bank_of("sq", i)[:, 0:SEQ], "sq", i)
                act.wait_ge(*ret_ms.after(layer, 1))
                act.activation(stat[:, 56:64], stat[:, 48:56], ACT.Sqrt).then_inc(ret_root.sem, 1)
                for i in range(4):
                    act.wait_ge(*full(layer, "rg", i))
                    if i:
                        act.wait_ge(*in_sbuf(layer, "rg", i - 1))
                    act.activation(sgm, both("rg", i), ACT.Sigmoid).then_inc(gate_sig.sem, 1)
                for h in range(MH):
                    raw_copy(layer, 9 + h)
                    copy_job(layer, mk[0:NOPE, h, :], bank_of("kn", h)[0:NOPE, 0:SEQ], "kn", h)
                for t in range(NT):
                    copy_job(layer, mv[:, t, :], bank_of("mv", t), "mv", t)
                yT_store(layer, 0)
                yT_store(layer, 1)
                for step in mix_steps():
                    if step < MIX_UNITS:
                        for g in gates_at(step):
                            copy_job(layer, gates[:, g, :], bank_of("gate", g)[:, 0:SEQ], "gate", g)
                    soft(layer, step, range(MIX_UNITS))
                    if step - 1 in END_AT:
                        yT_store(layer, 2 + END_AT[step - 1])
                yT_store(layer, 5)
                for g in range(GATES - JOB_BANKS, GATES):
                    act.wait_ge(*in_sbuf(layer, "gate", g))
                for cg in range(4):
                    for br in range(3):
                        g = GATE_OF[br] * DC + cg * 2
                        act.activation(gates[:, g:g + 2, :], gates[:, g:g + 2, :], ACT.Sigmoid).then_inc(gates_open.sem, 1)
                for i in range(4):
                    copy_job(layer, xk[:, i, :], bank_of("xk", i)[:, 0:SEQ], "xk", i)
                for i in range(4):
                    copy_job(layer, xv[:, :, i * P:i * P + P], both("xv", i), "xv", i)
                act.wait_ge(*in_sbuf(layer, "wo", 3))
                square_sums(layer, x, xn, 2, 16)
                for i in range(4):
                    copy_job(layer, xq[:, i, :], bank_of("xq", i)[:, 0:SEQ], "xq", i)
                for step in xa_steps():
                    soft(layer, step, range(MIX_UNITS, len(UNITS)))
                    if step - 1 in END_AT and END_AT[step - 1] >= 4:
                        yT_store(layer, 2 + END_AT[step - 1])
                yT_store(layer, 7)
                act.wait_ge(*in_sbuf(layer, "xo", 3))
                square_sums(layer, x, xn, 3, 24)
                act.wait_ge(*in_sbuf(layer, "x2", 1, 1))
                act.activation(h_hi[:, :, :], hT[:, :, :], ACT.Copy).then_inc(h_split.sem, 1)
                for i in range(8):
                    copy_job(layer, pq[:, i, :], bank_of("pq", i)[:, 0:SEQ], "pq", i)
                for t in range(NT):
                    for pair in range(PH // 2):
                        for p in range(2):
                            j = (t * PH + 2 * pair) * 2 + p
                            copy_job(layer, sc[:, j:j + 3:2, :],
                                     bank_of("ps", t, pair, p)[:, 0:2 * NK].rearrange("p (a n) -> p a n", a=2), "ps", t, pair, p)

                def high(r, s):
                    for half in range(2):
                        part, cols = 2 * (s % 2) + half, slice(half * HALF, half * HALF + HALF)
                        if half == 0:
                            act.wait_ge(*slot_full[s].after(layer, U_ROUND0 + r + 1))
                        act.wait_ge(*part_used[part].after(layer, r * 2 + s // 2))
                        act.activation(hi[:, s % 2, cols], ring[:, s, cols], ACT.Copy).then_inc(high_ready[part].sem, 1)

                def high_ahead(r, s):
                    high(r + (s + 2) // SLOTS, (s + 2) % SLOTS)

                def u_round(r):
                    for s in range(SLOTS):
                        high_ahead(r, s)
                        act.wait_ge(*part_used[2 * (s % 2) + 1].after(layer, r * 2 + s // 2 + 1))
                        act.activation(pre[:, bass.ds(r * SLOTS + s, 1), :].squeeze(1), bank[4 + s][:, 0:SEQ], ACT.Gelu) \
                            .then_inc(pre_stored[s].sem, 1)

                def w_part(r, s):
                    b = s % 2
                    act.wait_ge(*part_used[2 * b + 1].after(layer, NK // 2 + r * 2 + s // 2))
                    act.activation(w_hi[:, b, :], pre[:, bass.ds(r * SLOTS + s, 1), :].squeeze(1), ACT.Copy).then_inc(w_high[b].sem, 1)

                def v_round(r, opens_chunk=False, final=False):
                    for s in range(SLOTS):
                        if final and s >= 2:
                            break
                        high_ahead(r + U_ROUNDS, s)
                        if opens_chunk and s == 2:
                            for b in range(2):
                                act.wait_ge(*cells_gated[b].after(layer, 2 * CHUNK_ROUNDS))
                        w_part(r + (s + 2) // SLOTS, (s + 2) % SLOTS)

                high(0, 0)
                high(0, 1)
                act.preload_act_table(ACT.Gelu)
                with act.Fori(0, EXP_ROUND) as r:
                    u_round(r)
                act.wait_ge(*best_shift.after(layer, 1))
                act.activation(best, best, ACT.Exp).then_inc(best_exp.sem, 1)
                act.preload_act_table(ACT.Gelu)
                with act.Fori(EXP_ROUND, TURN_ROUND) as r:
                    u_round(r)
                act.wait_ge(*choice_made.after(layer, 1))
                with act.Fori(TURN_ROUND, U_ROUNDS) as r:
                    u_round(r)
                for b in range(2):
                    act.wait_ge(*cells_gated[b].after(layer, CHUNK_ROUNDS))
                w_part(0, 0)
                w_part(0, 1)
                with act.Fori(0, CHUNK_ROUNDS - 1) as r:
                    v_round(r)
                v_round(CHUNK_ROUNDS - 1, opens_chunk=True)
                with act.Fori(CHUNK_ROUNDS, U_ROUNDS - 1) as r:
                    v_round(r)
                v_round(U_ROUNDS - 1, final=True)
            act.wait_ge(*peer_added.after(DEPTH, 0))
            for t in range(NT):
                last = act.activation(xn[:, t, :], x[:, t, :], ACT.Square, accum_out=stat[:, t:t + 1])
            last.then_inc(f_sq.sem, 1)
            act.wait_ge(f_ms.sem, 1)
            act.activation(stat[:, 4:6], stat[:, 2:4], ACT.Sqrt).then_inc(f_root.sem, 1)

        @block.vector
        def _(dve):
            def norm_rows(layer, src, dst, order, col):
                dve.wait_ge(*squares.after(layer, 2 * order + 2))
                dve.tensor_scalar(stat[:, col + 2:col + 4], stat[:, col:col + 2], 1.0 / D, EPS, ALU.mult, ALU.add) \
                    .then_inc(meansq.sem, 1)
                dve.wait_ge(*root.after(layer, order + 1))
                dve.reciprocal(stat[:, col + 6:col + 8], stat[:, col + 4:col + 6]).then_inc(rstd.sem, 1)
                dve.wait_ge(*rstd.after(layer, order + 1))
                for t in range(NT):
                    dve.tensor_scalar(dst[:, t, :], src[:, t, :], stat[:, col + 6 + t:col + 7 + t], None, ALU.mult) \
                        .then_inc(normed.sem, 1)

            def gain_store(layer, name, dst, g):
                for t in range(NT):
                    for half in range(2):
                        dve.wait_ge(*full(layer, name, t, half))
                        ps = bank_of(name, t, half)
                        dve.tensor_tensor(dst[:, 4 * half:4 * half + 4, t * P:t * P + P],
                                                ps.rearrange("p (c s) -> p c s", c=4),
                                                vec[:, g + 4 * half:g + 4 * half + 4].unsqueeze(2).broadcast_to([P, 4, P]),
                                                ALU.mult).then_inc(*stores(name, t, half))

            def rope(layer, k):
                name, b = ROPES[k], k % 2
                wide = name[0] in ("rq", "rk")
                rows = P if wide else MQK
                c, s = (cos, sin) if wide else (cosm, sinm)
                dst = {"rq": lambda i: rq[:, i, :], "rk": lambda i: rk[:, i, :], "kr": lambda i: krr[0:MQK, :],
                       "qb": lambda i: mq[:, i, :]}[name[0]](name[1])
                dve.wait_ge(*in_sbuf(layer, *name))
                dve.tensor_tensor(cosx[0:rows, b, :], raw[0:rows, b, :], c, ALU.mult).then_inc(raw_cos.sem, 1)
                dve.wait_ge(*full(layer, "rot", *name))
                ps = bank_of("rot", *name)
                dve.tensor_tensor(sinx[0:rows, b, :], ps[0:rows, 0:SEQ], s, ALU.mult).then_inc(*stores("rot", *name))
                dve.wait_ge(*raw_cos.after(layer, k + 1))
                dve.wait_ge(*in_sbuf(layer, "rot", *name))
                dve.tensor_tensor(dst, cosx[0:rows, b, :], sinx[0:rows, b, :], ALU.add).then_inc(roped.sem, 1)

            def ret_decay(layer, h):
                dve.wait_ge(*score_full.after(layer, h + 1))
                if h >= 2:
                    dve.wait_ge(*ret_full.after(layer, h - 1))
                ps = bank[4 + h % 2]
                dve.tensor_tensor(retT[:, h % 2, 0:SEQ], ps[:, 0:SEQ], decay[:, h, :], ALU.mult)
                dve.tensor_tensor(retT[:, h % 2, SEQ:SEQ + P], ps[:, SEQ:SEQ + P], decay[:, h, 0:P], ALU.mult) \
                    .then_inc(ret_scores.sem, 1)

            def soft(layer, step, units):
                if step in units:
                    kind, t, h = UNITS[step]
                    keys = SEQ if kind == "xa" else P * (t + 1)
                    ps = bank[4 + (RH + step) % 2]
                    dve.wait_ge(*score_full.after(layer, RH + step + 1))
                    nm = negmax[:, step:step + 1]
                    if kind == "xa":
                        dve.tensor_reduce(rowm[:, step % 2:step % 2 + 1], ps[:, 0:keys], AXX, ALU.max).then_inc(xa_max.sem, 1)
                        dve.wait_ge(*xa_max.after(layer, step - MIX_UNITS + 1))
                        dve.tensor_scalar(nm, rowm[:, step % 2:step % 2 + 1], -(XD ** -0.5), None, ALU.mult) \
                            .then_inc(negmax_ready.sem, 1)
                        return
                    add = bias[:, h, SEQ - keys:SEQ] if kind == "swa" else causal[:, SEQ - keys:SEQ]
                    if step >= 2:
                        dve.wait_ge(*prob_ready.after(layer, step - 1))
                    dve.scalar_tensor_tensor(out=sm[:, step % 2, 0:keys], in0=ps[:, 0:keys],
                                             scalar=(SD if kind == "swa" else MQK) ** -0.5, in1=add,
                                             op0=ALU.mult, op1=ALU.add).then_inc(masked.sem, 1)
                    dve.wait_ge(*masked.after(layer, step + 1))
                    last = dve.tensor_reduce(nm, sm[:, step % 2, 0:keys], AXX, ALU.max, negate=True)
                    if kind == "mla":
                        last.then_inc(negmax_ready.sem, 1)
                        return
                    last.then_inc(rowmax.sem, 1)
                    dve.wait_ge(*rowmax.after(layer, step + 1))
                    dve.tensor_tensor(nm, nm, negsink[:, h:h + 1], ALU.min).then_inc(negmax_ready.sem, 1)

            def end_group(layer, step):
                if step not in END_AT:
                    return
                g = END_AT[step]
                kind, t, v0, v1 = GROUPS[g]
                heads = v1 - v0 + 1
                den = sums[:, v0:v1 + 1]
                if kind == "swa":
                    dve.wait_ge(*negmax_ready.after(layer, v1 + 1))
                    dve.tensor_tensor(sinkexp[:, t, :], negmax[:, v0:v1 + 1], vec[:, SINKS:SINKS + 8], ALU.add) \
                        .then_inc(sink_shift.sem, 1)
                    dve.wait_ge(*prob_ready.after(layer, v1 + 1))
                    dve.wait_ge(*sink_exp.after(layer, t + 1))
                    dve.tensor_tensor(sinkexp[:, t, :], sinkexp[:, t, :], den, ALU.add).then_inc(den_ready.sem, 1)
                    dve.wait_ge(*den_ready.after(layer, t + 1))
                    den = sinkexp[:, t, :]
                dve.wait_ge(*prob_ready.after(layer, v1 + 1))
                dve.reciprocal(rden[:, t, 0:heads], den).then_inc(rden_ready.sem, 1)
                dve.wait_ge(*rden_ready.after(layer, g + 1))
                dve.wait_ge(*pv_done.after(layer, v1 + 1))
                dve.wait_ge(*full(layer, "ty", g))
                dve.tensor_tensor(ytok[:, t, :].rearrange("p (h e) -> p h e", h=heads),
                                  bank[7][:, :].rearrange("p (h e) -> p h e", h=heads),
                                  rden[:, t, 0:heads].unsqueeze(2).broadcast_to([P, heads, 512 // heads]), ALU.mult) \
                    .then_inc(ytok_ready.sem, 1)

            def add_x(layer, name):
                for i in range(4):
                    dve.wait_ge(*full(layer, name, i))
                    ps = bank_of(name, i)
                    xs = x[:, i // 2, (i % 2) * 512:(i % 2) * 512 + 512]
                    dve.tensor_tensor(xs, xs, ps, ALU.add).then_inc(*stores(name, i))

            dve.wait_ge(cst_loaded.sem, 16)
            with dve.Fori(0, DEPTH) as layer:
                norm_rows(layer, x, xn, 0, 0)
                dve.wait_ge(*vec_loaded.after(layer, 1))
                dve.tensor_scalar(negsink, vec[:, SINKS:SINKS + 8], -1.0, None, ALU.mult).then_inc(sink_negated.sem, 1)
                gain_store(layer, "x0", hT, G_MIX)
                norm_rows(layer, mem, mem, 1, 8)
                gain_store(layer, "mem", memT, G_MEM)
                dve.wait_ge(*tab_loaded.after(layer, 1))
                for k in range(8):
                    rope(layer, k)
                for h in range(RH):
                    ret_decay(layer, h)
                rope(layer, 8)
                dve.wait_ge(*qk_sq.after(layer, 4))
                dve.tensor_scalar(stat[:, 36:38], stat[:, 32:34], 1.0 / QR, EPS, ALU.mult, ALU.add).then_inc(qk_ms.sem, 1)
                dve.tensor_scalar(stat[:, 38:40], stat[:, 34:36], 1.0 / KVR, EPS, ALU.mult, ALU.add).then_inc(qk_ms.sem, 1)
                dve.wait_ge(*qk_root.after(layer, 1))
                dve.reciprocal(stat[:, 44:48], stat[:, 40:44]).then_inc(qk_rstd.sem, 1)
                dve.wait_ge(*qk_rstd.after(layer, 1))
                for t in range(NT):
                    for k, cols in enumerate((slice(0, QR), slice(QR, QR + KVR))):
                        dve.tensor_scalar(qk[:, t, cols], qk[:, t, cols], stat[:, 44 + 2 * k + t:45 + 2 * k + t], None,
                                          ALU.mult).then_inc(qk_normed.sem, 1)
                dve.wait_ge(*ret_stored.after(layer, RH))
                ys = ytok.rearrange("p t (h e) -> p t h e", h=RH)
                for t in range(NT):
                    dve.tensor_tensor(rsq[:, t, :], ytok[:, t, :], ytok[:, t, :], ALU.mult).then_inc(ret_sq.sem, 1)
                dve.wait_ge(*ret_sq.after(layer, 2))
                for t in range(NT):
                    dve.tensor_reduce(rsum[:, 4 * t:4 * t + 4], rsq[:, t, :].rearrange("p (h e) -> p h e", h=RH), AXX, ALU.add) \
                        .then_inc(ret_sum.sem, 1)
                dve.wait_ge(*ret_sum.after(layer, 2))
                dve.tensor_scalar(stat[:, 48:56], rsum, 1.0 / P, EPS, ALU.mult, ALU.add).then_inc(ret_ms.sem, 1)
                dve.wait_ge(*ret_root.after(layer, 1))
                dve.reciprocal(rsum, stat[:, 56:64]).then_inc(ret_rstd.sem, 1)
                dve.wait_ge(*ret_rstd.after(layer, 1))
                for t in range(NT):
                    dve.tensor_tensor(ys[:, t], ys[:, t], rsum[:, 4 * t:4 * t + 4].unsqueeze(2).broadcast_to([P, RH, P]),
                                      ALU.mult).then_inc(ret_scaled.sem, 1)
                dve.wait_ge(*full(layer, "tqa", 0))
                ps = bank_of("tqa", 0)
                dve.tensor_tensor(qanT, ps.rearrange("p (c s) -> p c s", c=2),
                                        vec[:, G_Q:G_Q + 2].unsqueeze(2).broadcast_to([P, 2, SEQ]), ALU.mult).then_inc(*stores("tqa", 0))
                dve.wait_ge(*full(layer, "tkv", 0))
                ps = bank_of("tkv", 0)
                dve.tensor_scalar(kvanT, ps[:, 0:SEQ], vec[:, G_KV:G_KV + 1], None, ALU.mult).then_inc(*stores("tkv", 0))
                dve.wait_ge(*full(layer, "sk", 0))
                ps = bank_of("sk", 0)
                for g in range(SKV):
                    for half in range(2):
                        last = dve.tensor_copy(swk[64 * half:64 * half + 64, g, :], ps[64 * g:64 * g + 64, 0:SEQ])
                last.then_inc(*stores("sk", 0))
                for i in range(4):
                    dve.wait_ge(*gate_sig.after(layer, i + 1))
                    ps = bank_of("rg", i)[:, 0:NT * P].rearrange("p (t c) -> p t c", t=NT)
                    dve.tensor_tensor(rgs[:, :, i * P:i * P + P], ps, sgm, ALU.mult).then_inc(*stores("rg", i))
                dve.wait_ge(*in_sbuf(layer, "rg", 3))
                dve.wait_ge(*ret_scaled.after(layer, 2))
                for t in range(NT):
                    dve.tensor_tensor(ytok[:, t, :], ytok[:, t, :], rgs[:, t, :], ALU.mult).then_inc(ytok_ready.sem, 1)
                for h in range(MH):
                    rope(layer, 9 + h)
                dve.wait_ge(*bias_ready.after(layer, 1))
                dve.wait_ge(*sink_negated.after(layer, 1))
                for step in mix_steps():
                    soft(layer, step, range(MIX_UNITS))
                    end_group(layer, step)
                for cg in range(4):
                    for br in range(3):
                        for m in range(2):
                            d = cg * 2 + m
                            dve.wait_ge(*full(layer, "branch", cg, br, m))
                            ps = bank_of("branch", cg, br, m)
                            gate = gates[:, GATE_OF[br] * DC + d, :]
                            if m == 0:
                                dve.wait_ge(*gates_open.after(layer, cg * 3 + br + 1))
                            if br == 0:
                                dve.tensor_tensor(merged[:, d, :], ps[:, 0:SEQ], gate, ALU.mult).then_inc(*stores("branch", cg, br, m))
                                continue
                            dve.tensor_tensor(gate, ps[:, 0:SEQ], gate, ALU.mult).then_inc(*stores("branch", cg, br, m))
                            dve.wait_ge(*in_sbuf(layer, "branch", cg, br, m))
                            if br == 2:
                                dve.wait_ge(*gated.after(layer, cg * 4 + m + 1))
                            dve.tensor_tensor(merged[:, d, :], merged[:, d, :], gate, ALU.add).then_inc(gated.sem, 1)
                add_x(layer, "wo")
                norm_rows(layer, x, xn, 2, 16)
                gain_store(layer, "x1", hT, G_XA)
                for step in xa_steps():
                    soft(layer, step, range(MIX_UNITS, len(UNITS)))
                    if END_AT.get(step, 0) >= 4:
                        end_group(layer, step)
                add_x(layer, "xo")
                norm_rows(layer, x, xn, 3, 24)
                gain_store(layer, "x2", hT, G_FFN)
                dve.wait_ge(*h_split.after(layer, 1))
                dve.tensor_tensor(h_lo[:, :, :], hT[:, :, :], h_hi[:, :, :].bitcast(F32), ALU.subtract).then_inc(h_split.sem, 1)

                dve.wait_ge(*in_sbuf(layer, "ps", NT - 1, PH // 2 - 1, 1))
                segs = range(NT * PH * 2)
                settle(dve)
                for j in segs:
                    last = dve.max(top[:, j, 0:8], sc[:, j, :])
                last.then_inc(top1.sem, 1)
                dve.wait_ge(*top1.after(layer, 1))
                settle(dve)
                for j in segs:
                    last = dve.max_index(topi[:, j, 0:8], top[:, j, 0:8], sc[:, j, :])
                last.then_inc(top_idx1.sem, 1)
                dve.wait_ge(*top_idx1.after(layer, 1))
                settle(dve)
                for j in segs:
                    last = dve.match_replace(sc[:, j, :], top[:, j, 0:8], sc[:, j, :], LEAST)
                last.then_inc(top_cut.sem, 1)
                dve.wait_ge(*top_cut.after(layer, 1))
                settle(dve)
                for j in segs:
                    last = dve.max(top[:, j, 8:16], sc[:, j, :])
                last.then_inc(top2.sem, 1)
                dve.wait_ge(*top2.after(layer, 1))
                settle(dve)
                for j in segs:
                    last = dve.max_index(topi[:, j, 8:16], top[:, j, 8:16], sc[:, j, :])
                last.then_inc(top_idx2.sem, 1)
                dve.wait_ge(*top_idx2.after(layer, 1))
                dve.tensor_copy(topf, topi).then_inc(top_float.sem, 1)
                top_v = top.rearrange("p (t h a) k -> p t h a k", t=NT, h=PH)
                for t in range(NT):
                    if t:
                        dve.wait_ge(*best_idx2.after(layer, t))
                    dve.tensor_tensor(cand.rearrange("p h (i j) -> p h i j", i=TOPK),
                                      top_v[:, t, :, 0, :].unsqueeze(3).broadcast_to([P, PH, TOPK, TOPK]),
                                      top_v[:, t, :, 1, :].unsqueeze(2).broadcast_to([P, PH, TOPK, TOPK]), ALU.add) \
                        .then_inc(cand_ready.sem, 1)
                    dve.wait_ge(*cand_ready.after(layer, t + 1))
                    settle(dve)
                    for h in range(PH):
                        last = dve.max(best[:, t * PH + h, 0:8], cand[:, h, :])
                    last.then_inc(best1.sem, 1)
                    dve.wait_ge(*best1.after(layer, t + 1))
                    settle(dve)
                    for h in range(PH):
                        last = dve.max_index(besti[:, t * PH + h, 0:8], best[:, t * PH + h, 0:8], cand[:, h, :])
                    last.then_inc(best_idx1.sem, 1)
                    dve.wait_ge(*best_idx1.after(layer, t + 1))
                    settle(dve)
                    for h in range(PH):
                        last = dve.match_replace(cand[:, h, :], best[:, t * PH + h, 0:8], cand[:, h, :], LEAST)
                    last.then_inc(best_cut.sem, 1)
                    dve.wait_ge(*best_cut.after(layer, t + 1))
                    settle(dve)
                    for h in range(PH):
                        last = dve.max(best[:, t * PH + h, 8:16], cand[:, h, :])
                    last.then_inc(best2.sem, 1)
                    dve.wait_ge(*best2.after(layer, t + 1))
                    settle(dve)
                    for h in range(PH):
                        last = dve.max_index(besti[:, t * PH + h, 8:16], best[:, t * PH + h, 8:16], cand[:, h, :])
                    last.then_inc(best_idx2.sem, 1)
                dve.wait_ge(*best_idx2.after(layer, NT))
                chosen_v = chosen[:, :, :, :].rearrange("p a t (h k) -> p a t h k", h=PH)
                best_v = best.rearrange("p g k -> p (g k)")
                besti_v = besti.rearrange("p g k -> p (g k)")
                dve.tensor_copy(bestmax, best[:, :, 0:1]).then_inc(best_top.sem, 1)
                dve.tensor_scalar(posi[:, 0, :], besti_v, 4, None, ALU.logical_shift_right)
                dve.tensor_scalar(posi[:, 1, :], besti_v, TOPK - 1, None, ALU.bitwise_and).then_inc(pos_split.sem, 1)
                dve.wait_ge(*best_top.after(layer, 1))
                dve.tensor_tensor(best, best, bestmax.broadcast_to([P, NT * PH, TOPK]), ALU.subtract) \
                    .then_inc(best_shift.sem, 1)
                dve.wait_ge(*pos_split.after(layer, 1))
                dve.tensor_copy(posf.rearrange("p a b -> p (a b)"), posi.rearrange("p a b -> p (a b)")).then_inc(pos_float.sem, 1)
                dve.wait_ge(*pos_float.after(layer, 1))
                dve.wait_ge(*top_float.after(layer, 1))
                topf_v = topf.rearrange("p (t h a) k -> p t h a k", t=NT, h=PH)
                oh4 = onehot.rearrange("p (h k) i -> p h k i", h=PH)
                n = 0
                for a in range(2):
                    for t in range(NT):
                        if n:
                            dve.wait_ge(*index_ready.after(layer, n))
                        dve.tensor_tensor(onehot, posf[:, a * NT + t, :].unsqueeze(2).broadcast_to([P, PH * TOPK, TOPK]),
                                          iota[:, 0:TOPK].unsqueeze(1).broadcast_to([P, PH * TOPK, TOPK]), ALU.is_equal) \
                            .then_inc(onehot_ready.sem, 1)
                        dve.wait_ge(*onehot_ready.after(layer, n + 1))
                        dve.tensor_tensor(oh4, oh4, topf_v[:, t, :, a, :].unsqueeze(2).broadcast_to([P, PH, TOPK, TOPK]),
                                          ALU.mult).then_inc(picked.sem, 1)
                        dve.wait_ge(*picked.after(layer, n + 1))
                        dve.tensor_reduce(chosen[:, a, t, :], onehot, AXX, ALU.add).then_inc(index_ready.sem, 1)
                        n += 1
                dve.wait_ge(*best_exp.after(layer, 1))
                dve.tensor_reduce(bestsum, best, AXX, ALU.add).then_inc(best_sum.sem, 1)
                dve.wait_ge(*best_sum.after(layer, 1))
                dve.reciprocal(bestsum, bestsum).then_inc(best_rsum.sem, 1)
                dve.wait_ge(*best_rsum.after(layer, 1))
                dve.wait_ge(*index_ready.after(layer, 2 * NT))
                dve.tensor_tensor(chosen[:, 2, :, :].rearrange("p t (h k) -> p (t h) k", h=PH), best,
                                  bestsum.unsqueeze(2).broadcast_to([P, NT * PH, TOPK]), ALU.mult).then_inc(choice_made.sem, 1)
                for a in range(3):
                    dve.wait_ge(*choice_turned.after(layer, a + 1))
                    dve.tensor_copy(chosenT[:, a, :], bank[a][:, 0:SEQ]).then_inc(choiceT_ready.sem, 1)
                dve.wait_ge(*choiceT_ready.after(layer, 3))

                rest = chosenT[:, 2, :]
                for n in range(3):
                    if n:
                        dve.wait_ge(*gate_rest.after(layer, 2 * n))
                    dve.tensor_copy(gate_parts[n], rest).then_inc(gate_rest.sem, 1)
                    if n < 2:
                        dve.wait_ge(*gate_rest.after(layer, 2 * n + 1))
                        dve.tensor_tensor(rest, rest, gate_parts[n], ALU.subtract).then_inc(gate_rest.sem, 1)
                dve.wait_ge(*gate_rest.after(layer, 5))

                def hots(chunk, q, b):
                    step = q + chunk * CHUNK_ROUNDS
                    toks = bass.ds(q * (2 * BATCH) + b * BATCH, BATCH)

                    def over(src, n):
                        return src[:, toks].unsqueeze(2).broadcast_to([P, BATCH, n])

                    dve.wait_ge(*spread[b].after(layer, step))
                    dve.tensor_tensor(hot2[:, b], iota[:, chunk * CHUNK:chunk * CHUNK + CHUNK].unsqueeze(1)
                                      .broadcast_to([P, BATCH, CHUNK]), over(chosenT[:, 1], CHUNK), ALU.is_equal) \
                        .then_inc(hot2_open[b].sem, 1)
                    dve.tensor_tensor(hot1[:, b], iota.unsqueeze(1).broadcast_to([P, BATCH, P]), over(chosenT[:, 0], P), ALU.is_equal)
                    dve.wait_ge(*hot2_open[b].after(layer, step + 1))
                    for n in range(1 if chunk else 3):
                        last = dve.tensor_tensor(hot_gate[:, b, n], hot2[:, b], over(gate_parts[n], CHUNK), ALU.mult)
                    last.then_inc(hot_ready[b].sem, 1)

                def gate_cells(chunk, q, b):
                    dve.wait_ge(*spread[b].after(layer, q + chunk * CHUNK_ROUNDS + 1))
                    cell = pre[:, chunk * CHUNK:chunk * CHUNK + CHUNK, bass.ds(q * (2 * BATCH) + b * BATCH, BATCH)]
                    dve.tensor_tensor(cell, bank[b][:, :].rearrange("p (k n) -> p n k", k=BATCH), cell, ALU.mult) \
                        .then_inc(cells_gated[b].sem, 1)

                def v_low(r, s):
                    b = s % 2
                    for half in range(2):
                        cols = slice(half * HALF, half * HALF + HALF)
                        dve.wait_ge(*high_ready[2 * b + half].after(layer, NK // 2 + r * 2 + s // 2 + 1))
                        last = dve.tensor_tensor(lo[:, b, cols], ring[:, s, cols], hi[:, b, cols].bitcast(F32), ALU.subtract)
                        if half == 0:
                            last.then_inc(low_first[b].sem, 1)
                        else:
                            last.then_inc(slot_done[s].sem, 1)

                def v_lows_ahead(r, b):
                    for s in (2 * b, 2 * b + 1):
                        v_low(r + (s + 2) // SLOTS, (s + 2) % SLOTS)

                hots(0, 0, 0)
                hots(0, 0, 1)
                for b in range(SLOTS):
                    dve.wait_ge(*pre_stored[b].after(layer, CHUNK_ROUNDS))
                settle(dve)
                with dve.Fori(0, CHUNK_ROUNDS - 1) as q:
                    for b in range(2):
                        gate_cells(0, q, b)
                        hots(0, q + 1, b)
                for b in range(2):
                    gate_cells(0, CHUNK_ROUNDS - 1, b)
                    hots(1, 0, b)
                for b in range(SLOTS):
                    dve.wait_ge(*pre_stored[b].after(layer, U_ROUNDS))
                v_low(0, 0)
                v_low(0, 1)
                with dve.Fori(0, CHUNK_ROUNDS - 1) as q:
                    for b in range(2):
                        gate_cells(1, q, b)
                        hots(1, q + 1, b)
                        v_lows_ahead(q, b)
                for b in range(2):
                    gate_cells(1, CHUNK_ROUNDS - 1, b)
                    v_lows_ahead(CHUNK_ROUNDS - 1, b)
                with dve.Fori(CHUNK_ROUNDS, U_ROUNDS - 1) as r:
                    for b in range(2):
                        v_lows_ahead(r, b)
                v_lows_ahead(U_ROUNDS - 1, 0)
                for b in range(2):
                    dve.wait_ge(*part_used[2 * b + 1].after(layer, NK))
                for i in range(4):
                    xs = x[:, i // 2, (i % 2) * 512:(i % 2) * 512 + 512]
                    dve.tensor_tensor(xs, xs, bank[4 + i][:, :], ALU.add).then_inc(peer_added.sem, 1)
            dve.wait_ge(f_sq.sem, 1)
            dve.tensor_scalar(stat[:, 2:4], stat[:, 0:2], 1.0 / D, EPS, ALU.mult, ALU.add).then_inc(f_ms.sem, 1)
            dve.wait_ge(f_root.sem, 1)
            dve.reciprocal(stat[:, 6:8], stat[:, 4:6]).then_inc(f_rstd.sem, 1)
            dve.wait_ge(f_rstd.sem, 1)
            for t in range(NT):
                last = dve.tensor_scalar(xn[:, t, :], x[:, t, :], stat[:, 6 + t:7 + t], None, ALU.mult)
            last.then_inc(f_scaled.sem, 1)
            dve.wait_ge(f_scaled.sem, 1)
            dve.wait_ge(gf_loaded.sem, 16)
            dve.tensor_tensor(xn, xn, gfin.unsqueeze(1).broadcast_to([P, NT, D]), ALU.mult).then_inc(f_ready.sem, 1)


def constants():
    cst = np.zeros((P, NCONST), np.float32)
    cst[:, C_ID:C_ID + P] = np.eye(P)
    cst[np.arange(P), C_PERM + (np.arange(P) + P // 2) % P] = 1
    half = ROPE // 2
    swap = np.arange(MQK)
    swap[NOPE:] = NOPE + (np.arange(ROPE) + half) % ROPE
    cst[np.arange(MQK), C_PERM96 + swap] = 1
    cst[:, C_IOTA:C_IOTA + P] = np.arange(P)
    tab = np.zeros((P, NTAB), np.float32)

    def angles(n):
        inv = np.power(np.float32(10000.0), -np.arange(n, dtype=np.float32) / np.float32(n)).astype(np.float32)
        a = inv[:, None] * np.arange(SEQ, dtype=np.float32)[None, :]
        return np.cos(a.astype(np.float32)), np.sin(a.astype(np.float32))

    c, s = angles(P // 2)
    tab[:, T_COS:T_COS + SEQ] = np.concatenate([c, c])
    tab[:, T_SIN:T_SIN + SEQ] = np.concatenate([-s, s])
    c, s = angles(half)
    tab[0:NOPE, T_COSM:T_COSM + SEQ] = 1
    tab[NOPE:MQK, T_COSM:T_COSM + SEQ] = np.concatenate([c, c])
    tab[NOPE:MQK, T_SINM:T_SINM + SEQ] = np.concatenate([-s, s])
    j, i = np.arange(P)[:, None], np.arange(SEQ)[None, :]
    for h in range(RH):
        log_gamma = np.log(1.0 - 2.0 ** (-5.0 - h))
        tab[:, T_DECAY + h * SEQ:T_DECAY + (h + 1) * SEQ] = \
            np.where(i >= j, np.exp(log_gamma * np.maximum(i - j, 0)) * P ** -0.5, 0)
    q, k = np.arange(P)[:, None], np.arange(SEQ)[None, :]
    tab[:, T_CAUSAL:T_CAUSAL + SEQ] = np.where(k <= q + P, 0, NEG)
    rel = q + P - k
    tab[:, T_WINDOW:T_WINDOW + SEQ] = np.where((rel >= 0) & (rel < P), 0, NEG)
    return cst, tab


def buckets():
    rel = np.arange(P)[:, None] + P - np.arange(SEQ)[None, :]
    n = np.maximum(rel, 0)
    exact = 16
    large = exact + (np.log(np.maximum(n, 1) / exact) / np.log(128 / exact) * (32 - exact)).astype(np.int32)
    return np.where(n < exact, n, np.minimum(large, 31)).astype(np.int32)


def lay_out(a):
    L = DEPTH
    mix = np.zeros((L, MIX_TILES, P, D), np.float32)

    def by_columns(w, name, cols=P):
        rows = w.shape[1] // P
        for i in range(w.shape[2] // cols):
            t = w[:, :, i * cols:(i + 1) * cols].reshape(L, rows, P, cols).transpose(0, 2, 1, 3)
            mix[:, TILES[name, i]] = t.reshape(L, P, rows * cols)

    w_in = a["w_in"]
    at = 0
    for name, n in (("rq", 512), ("rk", 512), ("rv", 512), ("rg", 512), ("qa", 256), ("kva", 128), ("kr", 32),
                    ("sq", 512), ("sk", 128), ("sv", 128), ("gate", 3072)):
        w = w_in[:, :, at:at + n]
        at += n
        if name == "kr":
            w = np.concatenate([np.zeros((L, D, NOPE), np.float32), w, np.zeros((L, D, 32), np.float32)], axis=2)
        by_columns(w, name)
    table = a["rel_bias"][buckets()].transpose(2, 0, 1)
    for i in range(2):
        mix[:, TILES["bias", i]] = table[4 * i:4 * i + 4].transpose(1, 0, 2).reshape(P, D)
    qb = a["w_mla_qb"].reshape(L, 2, P, 2, 4 * MQK)
    for i in range(2):
        mix[:, TILES["qb", i], :, 0:8 * MQK] = qb[:, :, :, i].transpose(0, 2, 1, 3).reshape(L, P, 8 * MQK)
    mix[:, TILES["kvb", 0]] = a["w_mla_kvb"].reshape(L, P, MH, 2, 64).transpose(0, 1, 3, 2, 4).reshape(L, P, D)
    for br, name in enumerate(("w_branch_ret", "w_branch_swa", "w_branch_mla")):
        for cg in range(4):
            t = a[name][:, :, cg * 256:(cg + 1) * 256].reshape(L, 4, P, 256).transpose(0, 2, 1, 3)
            mix[:, TILES["branch", cg * 3 + br]] = t.reshape(L, P, D)
    mix[:, TILES["wo", 0]:TILES["wo", 0] + 8] = a["w_out"].reshape(L, 8, P, D)
    by_columns(a["w_xkv"][:, :, 0:512], "xk")
    by_columns(a["w_xkv"][:, :, 512:1024], "xv")
    by_columns(a["w_xq"], "xq")
    mix[:, TILES["xo", 0]:TILES["xo", 0] + 4] = a["w_xo"].reshape(L, 4, P, D)
    by_columns(a["w_peer_query"], "pq")
    mix[:, TILES["keys", 0]] = a["peer_sub_keys"].transpose(0, 2, 4, 1, 3).reshape(L, P, D)
    vecs = np.zeros((L, P, NVEC), np.float32)
    for at, name, n in ((G_MIX, "g_mix", 8), (G_XA, "g_xattn", 8), (G_MEM, "g_mem", 8), (G_FFN, "g_ffn", 8),
                        (G_Q, "mla_q_norm", 2), (G_KV, "mla_kv_norm", 1)):
        vecs[:, :, at:at + n] = a[name].reshape(L, n, P).transpose(0, 2, 1)
    vecs[:, :, SINKS:SINKS + 8] = a["swa_sinks"][:, None, :]
    u = a["peer_u"].reshape(L, NK, NK, DC, P).transpose(0, 2, 4, 3, 1)
    v = a["peer_v"].reshape(L, NK, NK, D).transpose(0, 2, 1, 3)
    return {
        "mix_w": mix, "u_t": np.ascontiguousarray(u).reshape(L, NK, P, D), "v_t": np.ascontiguousarray(v), "vecs": vecs,
        "g_final": np.ascontiguousarray(np.broadcast_to(a["g_final"], (P, D))),
        "x_in": np.ascontiguousarray(a["x"].reshape(NT, P, D).transpose(1, 0, 2)),
        "mem_in": np.ascontiguousarray(a["mem"].reshape(NT, P, D).transpose(1, 0, 2)),
    }


def kernel(**inputs):
    import concourse.bacc as bacc
    from concourse.bass_utils import run_bass_kernel_spmd

    arrays = lay_out({k: np.asarray(v) for k, v in inputs.items()})
    arrays["consts"], arrays["tables"] = constants()
    nc = bacc.Bacc("TRN2", target_bir_lowering=False, num_devices=1)
    aps = {n: nc.dram_tensor(n, a.shape, mybir.dt.from_np(a.dtype), kind="ExternalInput").ap() for n, a in arrays.items()}
    out = nc.dram_tensor("out", (P, NT, D), F32, kind="ExternalOutput").ap()
    trunk(nc, **aps, out=out)
    r = run_bass_kernel_spmd(nc, [arrays], core_ids=[0])
    got = r.results[0]["out"]
    return np.ascontiguousarray(got.transpose(1, 0, 2)).reshape(1, SEQ, D)
```

```python
from contextlib import ExitStack

import numpy as np
import concourse.bass as bass
from concourse import mybir

F32 = mybir.dt.float32
F32R = mybir.dt.float32r
BF16 = mybir.dt.bfloat16
U32 = mybir.dt.uint32
ALU = mybir.AluOpType
ACT = mybir.ActivationFunctionType
AXX = mybir.AxisListType.X

P = 128
D = 1024
DC = D // P
SEQ = 256
NT = SEQ // P
DEPTH = 2
EPS = 1e-6
NEG = -1e30
RH = 4
MH, NOPE, ROPE, MV = 8, 64, 32, 64
MQK = NOPE + ROPE
QR, KVR = 256, 128
SH, SKV, SD = 8, 2, 64
XH, XD = 4, 128
PH, TOPK, NK = 8, 16, 128
SLOTS = 4

TILES = {}


def _tiles():
    n = 0
    for name, count in (("rv", 4), ("rq", 4), ("rk", 4), ("sv", 1), ("qa", 2), ("kva", 1), ("kr", 1),
                        ("sq", 4), ("bias", 2), ("sk", 1), ("rg", 4), ("qb", 2), ("kvb", 1),
                        ("gate", 24), ("branch", 12), ("wo", 8), ("xk", 4), ("xq", 4), ("xv", 4),
                        ("xo", 4), ("pq", 8), ("keys", 1)):
        for i in range(count):
            TILES[name, i] = n
            n += 1
    return n


MIX_TILES = _tiles()
assert MIX_TILES % SLOTS == 0 and NK % SLOTS == 0
ROUNDS = (MIX_TILES + 2 * NK) // SLOTS
U_ROUND0 = MIX_TILES // SLOTS
V_ROUND0 = U_ROUND0 + NK // SLOTS
U_ROUNDS = NK // SLOTS

JOBS, JOB_ORDER = {}, []


def _jobs():
    def job(*name):
        JOBS[name] = len(JOB_ORDER)
        JOB_ORDER.append(name)

    for n, first in (("x0", 0), ("mem", 2)):
        for t in range(NT):
            for half in range(2):
                job(n, t, half)
        for i in range(first, first + 2):
            job("rv", i)
    ropes = [("rq", i) for i in range(4)] + [("rk", i) for i in range(4)]
    for i, r in enumerate(ropes):
        job(*r)
        if i:
            job("rot", *ropes[i - 1])
    for n in (("sv", 0), ("rot", *ropes[-1]), ("qa", 0), ("qa", 1), ("kva", 0), ("kr", 0), ("sq", 0), ("rot", "kr", 0), ("sq", 1),
              ("sq", 2), ("sq", 3), ("tqa", 0), ("tkv", 0), ("sk", 0), ("rg", 0), ("rg", 1), ("rg", 2), ("rg", 3)):
        job(*n)
    for h in range(MH):
        job("qb", h)
        job("kn", h)
        if h:
            job("rot", "qb", h - 1)
    job("mv", 0)
    job("rot", "qb", MH - 1)
    job("mv", 1)
    job("ty", 0)
    job("ty", 1)


def _late_jobs():
    def job(*name):
        JOBS[name] = len(JOB_ORDER)
        JOB_ORDER.append(name)

    for br in range(3):
        for cg in range(4):
            for m in range(2):
                job("branch", br, cg, m)
        if br == 0:
            job("ty", 2 + 3)
    for i in range(4):
        job("wo", i)
    for i in range(3):
        job("xk", i)
    for t in range(NT):
        for half in range(2):
            job("x1", t, half)
    job("xk", 3)
    for i in range(4):
        job("xq", i)


UNITS = [("swa", t, h) for t in range(NT) for h in range(SH)] + [("mla", t, h) for t in range(NT) for h in range(MH)]
MIX_UNITS = len(UNITS)
UNITS += [("xa", t, h) for t in range(NT) for h in range(XH)]
GROUPS = []
for _v, (_k, _t, _h) in enumerate(UNITS):
    if not GROUPS or GROUPS[-1][:2] != [_k, _t]:
        GROUPS.append([_k, _t, _v, _v])
    GROUPS[-1][3] = _v
LAG = 2
END_AT = {g[3] + LAG: n for n, g in enumerate(GROUPS)}
GATES = 3 * DC


def gate_halves_at(step):
    return [divmod(n, 2) for n in range(step * 2 * GATES // MIX_UNITS, min((step + 1) * 2 * GATES // MIX_UNITS, 2 * GATES))]


def mix_steps():
    return range(MIX_UNITS + LAG)


def xa_steps():
    return range(MIX_UNITS, len(UNITS) + LAG)


def _unit_jobs():
    def job(*name):
        JOBS[name] = len(JOB_ORDER)
        JOB_ORDER.append(name)

    for step in mix_steps():
        for g, half in gate_halves_at(step):
            if half == 0:
                job("gate", g)
        if step - 1 in END_AT:
            job("ty", 2 + END_AT[step - 1])


def _xa_jobs():
    def job(*name):
        JOBS[name] = len(JOB_ORDER)
        JOB_ORDER.append(name)

    for step in xa_steps():
        if step - MIX_UNITS < XH:
            job("xv", step - MIX_UNITS)
        if step - 1 in END_AT and END_AT[step - 1] >= 4:
            job("ty", 2 + END_AT[step - 1])
    job("ty", 2 + 5)
    for i in range(4):
        job("xo", i)
    for t in range(NT):
        for half in range(2):
            job("x2", t, half)
    for i in range(8):
        job("pq", i)
    for t in range(NT):
        for pair in range(PH // 2):
            for half in range(2):
                job("ps", t, pair, half)


_jobs()
_unit_jobs()
_late_jobs()
_xa_jobs()
ROPES = [("rq", i) for i in range(4)] + [("rk", i) for i in range(4)] + [("kr", 0)] + [("qb", h) for h in range(MH)]
NROPE = len(ROPES)
TILE_ENDS = {n: TILES[n] for n in JOB_ORDER if n in TILES and n[0] in
             ("rq", "rk", "rv", "sv", "qa", "kva", "kr", "sq", "sk", "rg", "gate", "xk", "xv", "xq", "pq")}
TILE_ENDS |= {("qb", 3): TILES["qb", 0], ("qb", 7): TILES["qb", 1], ("mv", 1): TILES["kvb", 0],
              ("ps", NT - 1, PH // 2 - 1, 1): TILES["keys", 0]}
SPLITS = {n: m for m, n in enumerate([("rq", i) for i in range(4)] + [("rk", i) for i in range(4)] + [("kr", 0)] +
                                     [("sq", i) for i in range(4)] + [("sk", 0)] + [("gate", g) for g in range(GATES)] +
                                     [("branch", i) for i in range(12)] + [("wo", i) for i in range(8)] +
                                     [("xo", i) for i in range(4)] + [("pq", i) for i in range(2, 8)])}
LONG_RUN = GATES + 12 + 8
assert len(SPLITS) % 2 == 0 and LONG_RUN % SLOTS == 0
assert TILES["wo", 7] - TILES["gate", 0] == SPLITS["wo", 7] - SPLITS["gate", 0] == LONG_RUN - 1
U_PAIRS = len(SPLITS) // 2
V_PAIRS = U_PAIRS + NK // 2
ALL_PAIRS = V_PAIRS + NK // 2
PLAIN_JOBS = {n: k for k, n in enumerate(n for n in JOB_ORDER
                                            if n not in TILE_ENDS and n[0] not in ("branch", "wo", "xo"))}
GATE_OF = (0, 2, 1)
HALF = D // 2
CHUNK = NK // 2
CHUNK_ROUNDS = CHUNK // SLOTS
BATCH = 512 // CHUNK
TURN_ROUND = CHUNK_ROUNDS - 1
EXP_ROUND = 12
ROUNDS_BELOW = 18
assert EXP_ROUND < TURN_ROUND <= ROUNDS_BELOW
assert CHUNK_ROUNDS * 2 * BATCH == SEQ
LEAST = -3.0e38
NJOBS = len(JOB_ORDER)
JOB_BANKS = 4
BANK_JOBS = [len(range(b, NJOBS, JOB_BANKS)) for b in range(JOB_BANKS)]

G_MIX, G_XA, G_MEM, G_FFN, G_Q, G_KV, SINKS = 0, 8, 16, 24, 32, 34, 35
NVEC = 43
C_ID, C_PERM, C_PERM96, C_IOTA = 0, 128, 256, 352
NCONST = 480
T_COS, T_SIN, T_COSM, T_SINM, T_DECAY, T_CAUSAL, T_WINDOW = 0, 256, 512, 768, 1024, 2048, 2304
NTAB = 2560


class Signal:

    def __init__(self, sem, per_layer, by=1, base=0):
        self.sem, self.per_layer, self.by, self.base = sem, per_layer, by, base

    def after(self, layer, events):
        return self.sem, (layer * self.per_layer + events) * self.by + self.base


def trunk(nc, mix_w, u_t, v_t, vecs, consts, tables, g_final, x_in, mem_in, out):
    ctx = ExitStack()
    with ctx:
        def sb(name, shape, dt=F32):
            return ctx.enter_context(nc.sbuf_tensor(name, shape, dt))

        def sig(name, per_layer=1, by=1, base=0):
            return Signal(ctx.enter_context(nc.semaphore(name)), per_layer, by, base)

        arena = sb("arena", [P, NK * SEQ])
        ring = sb("ring", [P, SLOTS, D])
        hi = sb("table_hi", [P, 2, D], F32R)
        lo = sb("table_lo", [P, 2, D], F32R)
        h_hi = sb("h_hi", [P, DC, SEQ], F32R)
        h_lo = sb("h_lo", [P, DC, SEQ], F32R)
        w_hi = sb("w_hi", [P, 2, SEQ], F32R)
        w_lo = sb("w_lo", [P, 2, SEQ], F32R)
        x = sb("x", [P, NT, D])
        hT = sb("hT", [P, DC, SEQ])
        chosen = sb("chosen", [P, 3, NT, P])
        cst = sb("cst", [P, NCONST])
        vec = sb("vec", [P, NVEC])
        stat = sb("stat", [P, 64])
        negmax = sb("negmax", [P, len(UNITS)])
        sums = sb("sums", [P, len(UNITS)])
        sinkexp = sb("sinkexp", [P, 2, 8])
        rden = sb("rden", [P, 2, 8])
        negsink = sb("negsink", [P, 8])[:, :]
        rowm = sb("rowm", [P, 2])
        rsum = sb("rsum", [P, 8])[:, :]
        hot_gate = sb("hot_gate", [P, 2, 3, BATCH, CHUNK], BF16)

        flat = arena[:, :]
        where = [0]

        def part(n, *dims):
            a = flat[:, where[0]:where[0] + n]
            where[0] += n
            if len(dims) == 2:
                return a.rearrange("p (a b) -> p a b", a=dims[0])
            if len(dims) == 3:
                return a.rearrange("p (a b c) -> p a b c", a=dims[0], b=dims[1])
            return a

        gates = part(3 * DC * SEQ, 3 * DC, SEQ)
        xn = flat[:, 0:2 * D].rearrange("p (t d) -> p t d", t=NT)
        junk = flat[:, 2 * D:3 * D].rearrange("p (t d) -> p t d", t=NT)
        rsq = flat[:, 0:D].rearrange("p (t d) -> p t d", t=NT)
        gfin = flat[:, 3 * D:4 * D]
        mem = part(2 * D, NT, D)
        merged = mem.rearrange("p t d -> p (t d)").rearrange("p (c s) -> p c s", c=DC)
        memT = part(2 * D, DC, SEQ)
        raw = part(2 * SEQ, 2, SEQ)
        cosx = part(2 * SEQ, 2, SEQ)
        sinx = part(2 * SEQ, 2, SEQ)
        at_q = where[0]
        rq = part(4 * SEQ, 4, SEQ)
        rk = part(4 * SEQ, 4, SEQ)
        mq = flat[0:MQK, at_q:at_q + MH * SEQ].rearrange("p (h s) -> p h s", h=MH)
        at_v = where[0]
        rv = part(NT * 512, NT, 512)
        mv = flat[:, at_v:at_v + NT * 512].rearrange("p (t s) -> p t s", t=NT)
        rgs = part(NT * 512, NT, 512)
        sgm = part(SEQ, NT, P)
        qk = part(NT * 384, NT, 384)
        qanT = part(2 * SEQ, 2, SEQ)
        kvanT = part(SEQ)
        krr = part(SEQ)
        mk = part(MH * SEQ, MH, SEQ)
        at_sw = where[0]
        swq = part(4 * SEQ, 4, SEQ)
        swk = part(2 * SEQ, 2, SEQ)
        sv = part(NT * P, NT, P)
        yT = part(3 * 4 * SEQ, 12, SEQ)
        ytok = part(NT * 512, NT, 512)
        tab = part(NTAB)
        bias = part(8 * SEQ, 8, SEQ)
        sm = part(2 * SEQ, 2, SEQ)
        prob = part(2 * SEQ, 2, SEQ)
        probT = part(2 * SEQ, 2, SEQ)
        retT = part(2 * 384, 2, 384)
        assert where[0] <= NK * SEQ, where[0]
        xk = flat[:, at_q:at_q + 4 * SEQ].rearrange("p (h s) -> p h s", h=4)
        xq = flat[:, at_q + 4 * SEQ:at_q + 8 * SEQ].rearrange("p (h s) -> p h s", h=4)
        xv = flat[:, at_v:at_v + NT * 512].rearrange("p (t s) -> p t s", t=NT)
        where[0] = ROUNDS_BELOW * SLOTS * SEQ
        pq = part(8 * SEQ, 8, SEQ)
        sc = part(NT * PH * 2 * NK, NT * PH * 2, NK)
        cand = part(PH * 256, PH, 256)
        onehot = part(PH * 256, PH * TOPK, TOPK)
        top = part(NT * PH * 2 * TOPK, NT * PH * 2, TOPK)
        topf = part(NT * PH * 2 * TOPK, NT * PH * 2, TOPK)
        topi = part(NT * PH * 2 * TOPK, NT * PH * 2, TOPK).bitcast(U32)
        best = part(NT * PH * TOPK, NT * PH, TOPK)
        besti = part(NT * PH * TOPK, NT * PH, TOPK).bitcast(U32)
        posi = part(2 * NT * PH * TOPK, 2, NT * PH * TOPK).bitcast(U32)
        posf = part(2 * NT * PH * TOPK, 2 * NT, PH * TOPK)
        bestmax = part(NT * PH).unsqueeze(2)
        bestsum = part(NT * PH)
        assert where[0] <= NK * SEQ, where[0]
        hflat = hT[:, :, :].rearrange("p c s -> p (c s)")
        chosenT = hflat[:, 0:3 * SEQ].rearrange("p (a s) -> p a s", a=3)
        spare = hflat[:, 3 * SEQ:].bitcast(BF16)
        hot1 = spare[:, 0:2 * BATCH * P].rearrange("p (b k n) -> p b k n", b=2, k=BATCH)
        turned = chosen[:, :, :, :].rearrange("p a t n -> p (a t n)").bitcast(BF16)
        hot2 = turned[:, 0:2 * BATCH * CHUNK].rearrange("p (b k n) -> p b k n", b=2, k=BATCH)
        gate_part = spare[:, 2 * BATCH * P:2 * BATCH * P + 2 * SEQ].rearrange("p (a s) -> p a s", a=2)
        gate_parts = [gate_part[:, 0], gate_part[:, 1], turned[:, 2 * BATCH * CHUNK:2 * BATCH * CHUNK + SEQ]]
        pre = arena[:, :].rearrange("p (g s) -> p g s", g=NK)

        ident = cst[:, C_ID:C_ID + P]
        perm = cst[:, C_PERM:C_PERM + P]
        perm96 = cst[0:MQK, C_PERM96:C_PERM96 + MQK]
        iota = cst[:, C_IOTA:C_IOTA + P]
        cos, sin = tab[:, T_COS:T_COS + SEQ], tab[:, T_SIN:T_SIN + SEQ]
        cosm, sinm = tab[0:MQK, T_COSM:T_COSM + SEQ], tab[0:MQK, T_SINM:T_SINM + SEQ]
        decay = tab[:, T_DECAY:T_DECAY + 4 * SEQ].rearrange("p (h s) -> p h s", h=4)
        causal = tab[:, T_CAUSAL:T_CAUSAL + SEQ]
        window = tab[:, T_WINDOW:T_WINDOW + SEQ]

        bank = [ctx.enter_context(nc.psum_tensor(f"bank{b}", [P, 512], F32))[:, :] for b in range(8)]


        slot_full = [sig(f"slot_full{s}", ROUNDS, 16) for s in range(SLOTS)]
        slot_done = [sig(f"slot_done{s}", ROUNDS, base=1) for s in range(SLOTS)]
        job_full = sig("job_full", len(PLAIN_JOBS))
        job_stored = [sig(f"job_stored{b}", BANK_JOBS[b], base=1) for b in range(JOB_BANKS)]
        x_loaded = sig("x_loaded")
        cst_loaded = sig("cst_loaded")
        vec_loaded = sig("vec_loaded", 1, 16)
        tab_loaded = sig("tab_loaded", 1, 16)
        mem_loaded = sig("mem_loaded", 1, 16)
        squares = sig("squares", 8)
        meansq = sig("meansq", 4)
        root = sig("root", 4)
        rstd = sig("rstd", 4)
        normed = sig("normed", 8)
        raw_cos = sig("raw_cos", NROPE)
        roped = sig("roped", NROPE)
        kr_spread = sig("kr_spread")
        qk_sq = sig("qk_sq", 4)
        qk_ms = sig("qk_ms", 2)
        qk_root = sig("qk_root")
        qk_rstd = sig("qk_rstd")
        qk_normed = sig("qk_normed", 4)
        gate_sig = sig("gate_sig", 4)
        score_full = sig("score_full", RH + len(UNITS))
        ret_scores = sig("ret_scores", RH)
        ret_full = sig("ret_full", RH)
        ret_stored = sig("ret_stored", RH)
        ret_sq = sig("ret_sq", NT)
        ret_sum = sig("ret_sum", NT)
        ret_ms = sig("ret_ms")
        ret_root = sig("ret_root")
        ret_rstd = sig("ret_rstd")
        ret_scaled = sig("ret_scaled", NT)
        ytok_ready = sig("ytok_ready", NT + len(GROUPS))
        masked = sig("masked", MIX_UNITS)
        rowmax = sig("rowmax", SH * NT)
        negmax_ready = sig("negmax_ready", len(UNITS))
        prob_ready = sig("prob_ready", len(UNITS))
        probT_full = sig("probT_full", len(UNITS))
        probT_ready = sig("probT_ready", len(UNITS))
        pv_done = sig("pv_done", len(UNITS))
        sink_shift = sig("sink_shift", NT)
        sink_exp = sig("sink_exp", NT)
        den_ready = sig("den_ready", NT)
        rden_ready = sig("rden_ready", len(GROUPS))
        gates_open = sig("gates_open", 12)
        gated = sig("gated", 16)
        in_high, in_low = sig("in_high", 7), sig("in_low", 5)
        peer_added = sig("peer_added", 4, base=1)
        sink_negated, best_top = sig("sink_negated"), sig("best_top")
        xa_max = sig("xa_max", XH * NT)
        settled = sig("settled")
        h_split = sig("h_split", 4)
        top1, top_idx1, top_cut, top2, top_idx2, top_float = (
            sig(n) for n in ("top1", "top_idx1", "top_cut", "top2", "top_idx2", "top_float"))
        cand_ready, best1, best_idx1, best_cut, best2, best_idx2 = (
            sig(n, NT) for n in ("cand_ready", "best1", "best_idx1", "best_cut", "best2", "best_idx2"))
        pos_split, pos_float = sig("pos_split"), sig("pos_float")
        onehot_ready, picked, index_ready = (sig(n, 2 * NT) for n in ("onehot_ready", "picked", "index_ready"))
        best_shift, best_exp, best_sum, best_rsum, choice_made = (
            sig(n) for n in ("best_shift", "best_exp", "best_sum", "best_rsum", "choice_made"))
        choice_turned = sig("choice_turned", 3)
        choiceT_ready = sig("choiceT_ready", 3)
        high_ready = [sig(f"high_ready{h}", ALL_PAIRS) for h in range(4)]
        part_used = [sig(f"part_used{h}", ALL_PAIRS, base=1) for h in range(4)]
        low_first = [sig(f"low_first{b}", ALL_PAIRS) for b in range(2)]
        pre_stored = [sig(f"pre_stored{b}", U_ROUNDS, base=1) for b in range(SLOTS)]
        hot2_open = [sig(f"hot2_open{b}", U_ROUNDS) for b in range(2)]
        hot_ready = [sig(f"hot_ready{b}", U_ROUNDS) for b in range(2)]
        pool_hot_ready = [sig(f"pool_hot_ready{b}", CHUNK_ROUNDS) for b in range(2)]
        gate_rest = sig("gate_rest", 5)
        spread = [sig(f"spread{b}", U_ROUNDS, base=1) for b in range(2)]
        cells_gated = [sig(f"cells_gated{b}", U_ROUNDS, base=1) for b in range(2)]
        w_high = [sig(f"w_high{b}", NK // 2) for b in range(2)]
        w_low = [sig(f"w_low{b}", NK // 2) for b in range(2)]
        f_sq, f_ms, f_root, f_rstd, f_scaled, f_ready, gf_loaded, stored = (
            sig(n) for n in ("f_sq", "f_ms", "f_root", "f_rstd", "f_scaled", "f_ready", "gf_loaded", "stored"))

        def settle(eng):
            eng.sem_inc(settled.sem, 1)

        def start(eng, *signals):
            for signal in signals:
                eng.sem_inc(signal.sem, 1)

        def tile(name, i=0):
            return ring[:, TILES[name, i] % SLOTS, :]

        def loaded(layer, name, i=0):
            n = TILES[name, i]
            return slot_full[n % SLOTS].after(layer, n // SLOTS + 1)

        def bank_of(*name):
            return bank[JOBS[name] % JOB_BANKS]

        def bank_free(layer, *name):
            k = JOBS[name]
            return job_stored[k % JOB_BANKS].after(layer, k // JOB_BANKS)

        def ends(*name):
            assert name not in SPLITS and name[0] not in ("branch", "wo", "xo")
            if name in TILE_ENDS:
                return slot_done[TILE_ENDS[name] % SLOTS].sem, 1
            return job_full.sem, 1

        def full(layer, *name):
            if name[0] == "branch":
                m, half = SPLITS["branch", name[1] * 4 + name[2]], name[3]
            elif name[0] in ("wo", "xo"):
                m, half = SPLITS[name[0], 7 if name[0] == "wo" else 3], name[1] % 2
            elif name in SPLITS:
                m, half = SPLITS[name], 1
            else:
                m = None
            if m is not None:
                return part_used[2 * (m % 2) + half].after(layer, m // 2 + 1)
            if name in TILE_ENDS:
                n = TILE_ENDS[name]
                return slot_done[n % SLOTS].after(layer, n // SLOTS + 1)
            return job_full.after(layer, PLAIN_JOBS[name] + 1)

        def stores(*name):
            return job_stored[JOBS[name] % JOB_BANKS].sem, 1

        def in_sbuf(layer, *name):
            k = JOBS[name]
            return job_stored[k % JOB_BANKS].after(layer, k // JOB_BANKS + 1)

        block = ctx.enter_context(nc.Block())

        @block.sync
        def _(sp):
            start(sp, *slot_done, *job_stored, peer_added, *part_used, *pre_stored, *spread, *cells_gated)
            sp.dma_start(cst[:, :], consts).then_inc(cst_loaded.sem, 16)
            sp.dma_start(x[:, :, :], x_in).then_inc(x_loaded.sem, 16)
            with sp.Fori(0, DEPTH) as layer:
                with sp.Fori(0, U_ROUND0) as r:
                    for s in range(SLOTS):
                        sp.wait_ge(*slot_done[s].after(layer, r))
                        sp.dma_start(ring[:, s, :], mix_w[layer, r * SLOTS + s]).then_inc(slot_full[s].sem, 16)
                for table, first in ((u_t, U_ROUND0), (v_t, V_ROUND0)):
                    with sp.Fori(0, U_ROUNDS) as r:
                        for s in range(SLOTS):
                            sp.wait_ge(*slot_done[s].after(layer, r + first))
                            sp.dma_start(ring[:, s, :], table[layer, r * SLOTS + s]).then_inc(slot_full[s].sem, 16)
            sp.wait_ge(f_ready.sem, 1)
            sp.dma_start(out, xn).then_inc(stored.sem, 16)
            sp.wait_ge(stored.sem, 16)

        @block.gpsimd
        def _(pool):
            pool.wait_ge(cst_loaded.sem, 16)
            with pool.Fori(0, DEPTH) as layer:
                pool.wait_ge(*peer_added.after(layer, 0))
                pool.dma_start(vec[:, :], vecs[layer]).then_inc(vec_loaded.sem, 16)
                pool.dma_start(mem, mem_in).then_inc(mem_loaded.sem, 16)
                pool.dma_start(tab, tables).then_inc(tab_loaded.sem, 16)

                def table_low(s, b, pairs):
                    pool.wait_ge(*high_ready[2 * b].after(layer, pairs))
                    pool.tensor_tensor(lo[:, b, 0:HALF], ring[:, s, 0:HALF], hi[:, b, 0:HALF].bitcast(F32),
                                       ALU.subtract).then_inc(low_first[b].sem, 1)
                    pool.wait_ge(*high_ready[2 * b + 1].after(layer, pairs))
                    pool.tensor_tensor(lo[:, b, HALF:D], ring[:, s, HALF:D], hi[:, b, HALF:D].bitcast(F32),
                                       ALU.subtract).then_inc(slot_done[s].sem, 1)

                for name, m in SPLITS.items():
                    if m < SPLITS["gate", 0]:
                        table_low(TILES[name] % SLOTS, m % 2, m // 2 + 1)
                with pool.Fori(0, LONG_RUN // SLOTS) as r:
                    for i in range(SLOTS):
                        m = SPLITS["gate", i]
                        table_low(TILES["gate", i] % SLOTS, m % 2, r * (SLOTS // 2) + (m // 2 + 1))
                for name, m in SPLITS.items():
                    if m > SPLITS["wo", 7]:
                        table_low(TILES[name] % SLOTS, m % 2, m // 2 + 1)
                with pool.Fori(0, U_ROUNDS) as r:
                    for s in range(SLOTS):
                        table_low(s, s % 2, r * 2 + s // 2 + (U_PAIRS + 1))

                def pool_hots(q, b):
                    toks = bass.ds(q * (2 * BATCH) + b * BATCH, BATCH)
                    pool.wait_ge(*hot2_open[b].after(layer, CHUNK_ROUNDS + q + 1))
                    settle(pool)
                    for n in (1, 2):
                        last = pool.tensor_tensor(hot_gate[:, b, n], hot2[:, b],
                                                  gate_parts[n][:, toks].unsqueeze(2).broadcast_to([P, BATCH, CHUNK]), ALU.mult)
                    last.then_inc(pool_hot_ready[b].sem, 1)

                def pool_lows(r):
                    for b in range(2):
                        pool.wait_ge(*w_high[b].after(layer, r + 1))
                        settle(pool)
                        pool.tensor_tensor(w_lo[:, b, :], pre[:, bass.ds(r * 2 + b, 1), :].squeeze(1), w_hi[:, b, :].bitcast(F32),
                                           ALU.subtract).then_inc(w_low[b].sem, 1)

                pool_hots(0, 0)
                pool_hots(0, 1)
                with pool.Fori(0, CHUNK_ROUNDS - 1) as q:
                    for b in range(2):
                        pool_lows(q * 2 + b)
                        pool_hots(q + 1, b)
                with pool.Fori((CHUNK_ROUNDS - 1) * 2, NK // 2) as r:
                    pool_lows(r)
            pool.wait_ge(*peer_added.after(DEPTH, 0))
            pool.dma_start(gfin, g_final).then_inc(gf_loaded.sem, 16)

        @block.tensor
        def _(pe):
            def project(layer, name, i, src):
                pe.wait_ge(*bank_free(layer, name, i))
                ps = bank_of(name, i)
                pe.wait_ge(*loaded(layer, name, i))
                w = tile(name, i)
                for c in range(DC):
                    last = pe.matmul(ps[:, 0:SEQ], w[:, c * P:c * P + P], src[:, c, :],
                                     start=(c == 0), stop=(c == DC - 1))
                last.then_inc(*ends(name, i))

            def project_split(layer, name, i, cols=P):
                for half in range(2):
                    project_half(layer, name, i, half, cols)

            def project_half(layer, name, i, half, cols=P):
                n, m = TILES[name, i], SPLITS[name, i]
                b = m % 2
                if half == 0:
                    pe.wait_ge(*bank_free(layer, name, i))
                    pe.wait_ge(*low_first[b].after(layer, m // 2 + 1))
                else:
                    pe.wait_ge(*slot_done[n % SLOTS].after(layer, n // SLOTS + 1))
                for c in range(4 * half, 4 * half + 4):
                    for k, (a, h) in enumerate(((hi, h_hi), (hi, h_lo), (lo, h_hi))):
                        last = pe.matmul(bank_of(name, i)[0:cols, 0:SEQ], a[:, b, c * P:c * P + cols], h[:, c, :],
                                         start=(c == 0 and k == 0), stop=(c == DC - 1 and k == 2))
                last.then_inc(part_used[2 * b + half].sem, 1)

            def project_tok(layer, name, i, src):
                pe.wait_ge(*bank_free(layer, name, i))
                ps = bank_of(name, i)
                pe.wait_ge(*loaded(layer, name, i))
                w = tile(name, i)
                for t in range(NT):
                    for c in range(DC):
                        last = pe.matmul(ps[:, t * P:t * P + P], src[:, c, t * P:t * P + P], w[:, c * P:c * P + P],
                                         start=(c == 0), stop=(c == DC - 1))
                last.then_inc(*ends(name, i))

            def turn(layer, src, *name):
                pe.wait_ge(*bank_free(layer, *name))
                ps = bank_of(*name)
                for k, s in enumerate(src):
                    last = pe.transpose(ps[:, k * P:k * P + P], s, ident)
                last.then_inc(*ends(*name))

            def turn_norm(layer, name, order):
                src = mem if name == "mem" else xn
                for t in range(NT):
                    pe.wait_ge(*normed.after(layer, 2 * order + t + 1))
                    for half in range(2):
                        turn(layer, [src[:, t, c * P:c * P + P] for c in range(4 * half, 4 * half + 4)], name, t, half)

            def rotate(layer, k):
                name = ROPES[k]
                pe.wait_ge(*bank_free(layer, "rot", *name))
                ps = bank_of("rot", *name)
                pe.wait_ge(*in_sbuf(layer, *name))
                if name[0] in ("rq", "rk"):
                    last = pe.matmul(ps[:, 0:SEQ], perm, raw[:, k % 2, :], start=True, stop=True)
                else:
                    last = pe.matmul(ps[0:MQK, 0:SEQ], perm96, raw[0:MQK, k % 2, :], start=True, stop=True)
                last.then_inc(*ends("rot", *name))

            def open_scores(layer, u):
                if u < 2:
                    pe.wait_ge(*peer_added.after(layer, 0))
                elif u - 2 < RH:
                    pe.wait_ge(*ret_scores.after(layer, u - 1))
                elif u - 2 < RH + MIX_UNITS:
                    pe.wait_ge(*masked.after(layer, u - 2 - RH + 1))
                else:
                    pe.wait_ge(*prob_ready.after(layer, u - 2 - RH + 1))
                return bank[4 + u % 2]

            def ret_score(layer, h):
                ps = open_scores(layer, h)
                pe.wait_ge(*roped.after(layer, 4 + h + 1))
                pe.matmul(ps[:, 0:SEQ], rk[:, h, 0:P], rq[:, h, :], start=True, stop=True)
                pe.matmul(ps[:, SEQ:SEQ + P], rk[:, h, P:SEQ], rq[:, h, P:SEQ], start=True, stop=True) \
                    .then_inc(score_full.sem, 1)

            def ret_out(layer, h):
                ps = bank[6 + h % 2]
                if h >= 2:
                    pe.wait_ge(*ret_stored.after(layer, h - 1))
                else:
                    pe.wait_ge(*in_sbuf(layer, "rv", 3))
                pe.wait_ge(*ret_scores.after(layer, h + 1))
                v = [rv[:, t, h * P:h * P + P] for t in range(NT)]
                s = retT[:, h % 2, :]
                pe.matmul(ps[:, 0:P], s[:, 0:P], v[0], start=True, stop=True)
                pe.matmul(ps[:, P:2 * P], s[:, P:2 * P], v[0], start=True, stop=False)
                pe.matmul(ps[:, P:2 * P], s[:, 2 * P:3 * P], v[1], start=False, stop=True).then_inc(ret_full.sem, 1)

            def turn_y(layer, n):
                pe.wait_ge(*ytok_ready.after(layer, n + 1))
                turn(layer, [ytok[:, n % 2, c * P:c * P + P] for c in range(4)], "ty", n)

            def scores(layer, v):
                kind, t, h = UNITS[v]
                ps = open_scores(layer, RH + v)
                keys = SEQ if kind == "xa" else P * (t + 1)
                q = slice(t * P, t * P + P)
                if kind == "swa":
                    lhs, rhs = swq[64 * (h % 2):64 * (h % 2) + 64, h // 2, q], swk[64 * (h % 2):64 * (h % 2) + 64, h // 4, 0:keys]
                elif kind == "mla":
                    lhs, rhs = mq[:, h, q], mk[0:MQK, h, 0:keys]
                    pe.wait_ge(*roped.after(layer, 9 + h + 1))
                    pe.wait_ge(*kr_spread.after(layer, 1))
                    pe.wait_ge(*in_sbuf(layer, "kn", h))
                else:
                    lhs, rhs = xq[:, h, q], xk[:, h, :]
                    pe.wait_ge(*in_sbuf(layer, "xq", h))
                pe.matmul(ps[:, 0:keys], lhs, rhs, start=True, stop=True).then_inc(score_full.sem, 1)

            def turn_probs(layer, v):
                kind, t, h = UNITS[v]
                blocks = 2 if kind == "xa" else t + 1
                pe.wait_ge(*prob_ready.after(layer, v + 1))
                if v:
                    pe.wait_ge(*probT_ready.after(layer, v))
                else:
                    pe.wait_ge(*ret_stored.after(layer, RH))
                for c in range(blocks):
                    last = pe.transpose(bank[6][:, c * P:c * P + P], prob[:, v % 2, c * P:c * P + P], ident)
                last.then_inc(probT_full.sem, 1)

            def weigh(layer, v):
                kind, t, h = UNITS[v]
                blocks = 2 if kind == "xa" else t + 1
                g = next(n for n, g in enumerate(GROUPS) if g[2] <= v <= g[3])
                if v == GROUPS[g][2]:
                    if g:
                        pe.wait_ge(*ytok_ready.after(layer, NT + g))
                    else:
                        pe.wait_ge(*ret_stored.after(layer, RH))
                pe.wait_ge(*probT_ready.after(layer, v + 1))
                for c in range(blocks):
                    if kind == "swa":
                        o, val = bank[7][:, h * SD:h * SD + SD], sv[:, c, (h // 4) * SD:(h // 4) * SD + SD]
                    elif kind == "mla":
                        o, val = bank[7][:, h * MV:h * MV + MV], mv[:, c, h * MV:h * MV + MV]
                    else:
                        o, val = bank[7][:, h * XD:h * XD + XD], xv[:, c, h * XD:h * XD + XD]
                    last = pe.matmul(o, probT[:, v % 2, c * P:c * P + P], val, start=(c == 0), stop=(c == blocks - 1))
                last.then_inc(pv_done.sem, 1)

            def attend(layer, step, units):
                if step in units:
                    scores(layer, step)
                if step - 1 in units:
                    turn_probs(layer, step - 1)
                if step - 2 in units:
                    weigh(layer, step - 2)

            def product4(layer, name, tiles, shift=0):
                for i in range(4):
                    pe.wait_ge(*bank_free(layer, name, i))
                for n in range(tiles):
                    slot, m = TILES[name, n], SPLITS[name, n]
                    b, chunk = m % 2, (n + shift) % DC
                    if name == "wo":
                        pe.wait_ge(*in_low.after(layer, 4 + n // 4))
                    for half in range(2):
                        if half == 0:
                            pe.wait_ge(*low_first[b].after(layer, m // 2 + 1))
                        else:
                            pe.wait_ge(*slot_done[slot % SLOTS].after(layer, slot // SLOTS + 1))
                        cols = slice(half * HALF, half * HALF + HALF)
                        for t in range(NT):
                            tok = slice(t * P, t * P + P)
                            for k, (h, v) in enumerate(((h_hi, hi), (h_hi, lo), (h_lo, hi))):
                                last = pe.matmul(bank_of(name, 2 * t + half)[:, :], h[:, chunk, tok], v[:, b, cols],
                                                 start=(n == 0 and k == 0), stop=(n == tiles - 1 and k == 2))
                        last.then_inc(part_used[2 * b + half].sem, 1)

            pe.wait_ge(cst_loaded.sem, 16)
            with pe.Fori(0, DEPTH) as layer:
                turn_norm(layer, "x0", 0)
                pe.wait_ge(*in_sbuf(layer, "x0", 1, 1))
                for i in range(2):
                    project_tok(layer, "rv", i, hT)
                turn_norm(layer, "mem", 1)
                for i in range(2, 4):
                    project_tok(layer, "rv", i, hT)
                pe.wait_ge(*h_split.after(layer, 2))
                for k in range(8):
                    project_split(layer, *ROPES[k])
                    if k:
                        rotate(layer, k - 1)
                project_tok(layer, "sv", 0, hT)
                rotate(layer, 7)
                ret_score(layer, 0)
                project_tok(layer, "qa", 0, hT)
                ret_score(layer, 1)
                ret_out(layer, 0)
                project_tok(layer, "qa", 1, hT)
                ret_score(layer, 2)
                ret_out(layer, 1)
                project_tok(layer, "kva", 0, hT)
                ret_score(layer, 3)
                ret_out(layer, 2)
                project_split(layer, "kr", 0, MQK)
                ret_out(layer, 3)
                project_split(layer, "sq", 0)
                rotate(layer, 8)
                for i in range(1, 4):
                    project_split(layer, "sq", i)
                pe.wait_ge(*qk_normed.after(layer, 4))
                turn(layer, [qk[:, t, c * P:c * P + P] for c in range(2) for t in range(NT)], "tqa", 0)
                turn(layer, [qk[:, t, QR:QR + P] for t in range(NT)], "tkv", 0)
                project_split(layer, "sk", 0)
                for i in range(4):
                    project_tok(layer, "rg", i, hT)
                pe.wait_ge(*in_sbuf(layer, "tqa", 0))
                pe.wait_ge(*in_sbuf(layer, "tkv", 0))
                wkv = None
                for h in range(MH):
                    pe.wait_ge(*bank_free(layer, "qb", h))
                    ps = bank_of("qb", h)
                    pe.wait_ge(*loaded(layer, "qb", h // 4))
                    w = tile("qb", h // 4)
                    for c in range(2):
                        o = (c * 4 + h % 4) * MQK
                        last = pe.matmul(ps[0:MQK, 0:SEQ], w[:, o:o + MQK], qanT[:, c, :], start=(c == 0), stop=(c == 1))
                    last.then_inc(*ends("qb", h))
                    pe.wait_ge(*bank_free(layer, "kn", h))
                    ps = bank_of("kn", h)
                    pe.wait_ge(*loaded(layer, "kvb"))
                    w = tile("kvb")
                    pe.matmul(ps[0:NOPE, 0:SEQ], w[:, h * NOPE:h * NOPE + NOPE], kvanT, start=True, stop=True).then_inc(*ends("kn", h))
                    if h:
                        rotate(layer, 9 + h - 1)
                for t in range(NT):
                    pe.wait_ge(*bank_free(layer, "mv", t))
                    ps = bank_of("mv", t)
                    pe.matmul(ps[:, :], kvanT[:, t * P:t * P + P], w[:, 512:1024], start=True, stop=True).then_inc(*ends("mv", t))
                    if t == 0:
                        rotate(layer, 9 + MH - 1)
                turn_y(layer, 0)
                turn_y(layer, 1)
                pe.wait_ge(*in_sbuf(layer, "sk", 0))
                for step in mix_steps():
                    for g, half in gate_halves_at(step):
                        project_half(layer, "gate", g, half)
                    attend(layer, step, range(MIX_UNITS))
                    if step - 1 in END_AT:
                        turn_y(layer, 2 + END_AT[step - 1])
                for br in range(3):
                    at = (0, 4, 0)[br]
                    pe.wait_ge(*in_low.after(layer, br + 1))
                    for cg in range(4):
                        slot, mm = TILES["branch", br * 4 + cg], SPLITS["branch", br * 4 + cg]
                        b = mm % 2
                        for m in range(2):
                            pe.wait_ge(*bank_free(layer, "branch", br, cg, m))
                            ps = bank_of("branch", br, cg, m)
                            if m == 0:
                                pe.wait_ge(*low_first[b].after(layer, mm // 2 + 1))
                            else:
                                pe.wait_ge(*slot_done[slot % SLOTS].after(layer, slot // SLOTS + 1))
                            for c in range(4):
                                w = slice(m * HALF + c * P, m * HALF + c * P + P)
                                for k, (a, h) in enumerate(((hi, h_hi), (hi, h_lo), (lo, h_hi))):
                                    last = pe.matmul(ps[:, 0:SEQ], a[:, b, w], h[:, at + c, :],
                                                     start=(c == 0 and k == 0), stop=(c == 3 and k == 2))
                            last.then_inc(part_used[2 * b + m].sem, 1)
                    if br == 0:
                        turn_y(layer, 5)
                product4(layer, "wo", 8, 4)
                pe.wait_ge(*in_sbuf(layer, "mem", 1, 1))
                for i in range(3):
                    project(layer, "xk", i, memT)
                turn_norm(layer, "x1", 2)
                project(layer, "xk", 3, memT)
                pe.wait_ge(*in_sbuf(layer, "x1", 1, 1))
                for i in range(4):
                    project(layer, "xq", i, hT)
                for step in xa_steps():
                    if step - MIX_UNITS < XH:
                        project_tok(layer, "xv", step - MIX_UNITS, memT)
                    attend(layer, step, range(MIX_UNITS, len(UNITS)))
                    if step - 1 in END_AT and END_AT[step - 1] >= 4:
                        turn_y(layer, 2 + END_AT[step - 1])
                turn_y(layer, 7)
                pe.wait_ge(*in_sbuf(layer, "ty", 7))
                product4(layer, "xo", 4)
                turn_norm(layer, "x2", 3)
                pe.wait_ge(*in_sbuf(layer, "x2", 1, 1))
                for i in range(2):
                    project(layer, "pq", i, hT)
                pe.wait_ge(*h_split.after(layer, 4))
                for i in range(2, 8):
                    project_split(layer, "pq", i)
                pe.wait_ge(*in_sbuf(layer, "pq", 7))
                pe.wait_ge(*loaded(layer, "keys"))
                w = tile("keys")
                for t in range(NT):
                    for pair in range(PH // 2):
                        for p in range(2):
                            pe.wait_ge(*bank_free(layer, "ps", t, pair, p))
                            ps = bank_of("ps", t, pair, p)
                            for k in range(2):
                                h = 2 * pair + k
                                last = pe.matmul(ps[:, k * NK:k * NK + NK], pq[64 * p:64 * p + 64, h, t * P:t * P + P],
                                                 w[64 * p:64 * p + 64, h * NK:h * NK + NK], start=True, stop=True)
                            last.then_inc(*ends("ps", t, pair, p))
                settle(pe)

                def spread_gates(chunk, q, b):
                    step = q + chunk * CHUNK_ROUNDS
                    pe.wait_ge(*cells_gated[b].after(layer, step))
                    pe.wait_ge(*hot_ready[b].after(layer, step + 1))
                    if chunk:
                        pe.wait_ge(*pool_hot_ready[b].after(layer, q + 1))
                    for k in range(BATCH):
                        for n in range(3):
                            last = pe.matmul(bank[b][:, k * CHUNK:k * CHUNK + CHUNK], hot1[:, b, k, :], hot_gate[:, b, n, k, :],
                                             start=(n == 0), stop=(n == 2))
                    last.then_inc(spread[b].sem, 1)

                def pre_activations(r, q=None):
                    for s in range(SLOTS):
                        b = s % 2
                        if q is not None and b == 0:
                            spread_gates(0, q, s // 2)
                        pe.wait_ge(*pre_stored[s].after(layer, r))
                        for half in range(2):
                            if half == 0:
                                pe.wait_ge(*low_first[b].after(layer, r * 2 + s // 2 + (U_PAIRS + 1)))
                            else:
                                pe.wait_ge(*slot_done[s].after(layer, U_ROUND0 + r + 1))
                            for c in range(4 * half, 4 * half + 4):
                                cols = slice(c * P, c * P + P)
                                for k, (a, h) in enumerate(((hi, h_hi), (hi, h_lo), (lo, h_hi))):
                                    last = pe.matmul(bank[4 + s][:, 0:SEQ], a[:, b, cols], h[:, c, :],
                                                     start=(c == 0 and k == 0), stop=(c == DC - 1 and k == 2))
                            last.then_inc(part_used[2 * b + half].sem, 1)

                with pe.Fori(0, TURN_ROUND) as r:
                    pre_activations(r)
                pe.wait_ge(*choice_made.after(layer, 1))
                pe.wait_ge(*in_sbuf(layer, "ps", NT - 1, PH // 2 - 1, 1))
                for a in range(3):
                    for t in range(NT):
                        last = pe.transpose(bank[a][:, t * P:t * P + P], chosen[:, a, t, :], ident)
                    last.then_inc(choice_turned.sem, 1)
                pre_activations(TURN_ROUND)
                with pe.Fori(0, CHUNK_ROUNDS) as q:
                    pre_activations(q + CHUNK_ROUNDS, q)
                for s in range(4):
                    pe.wait_ge(*pre_stored[s].after(layer, U_ROUNDS))

                def down(r, q=None, first=False, final=False):
                    for s in range(SLOTS):
                        b = s % 2
                        if q is not None and b == 0:
                            spread_gates(1, q, s // 2)
                        pe.wait_ge(*w_low[b].after(layer, r * 2 + s // 2 + 1))
                        for half in range(2):
                            if half == 0:
                                pe.wait_ge(*low_first[b].after(layer, r * 2 + s // 2 + (V_PAIRS + 1)))
                            else:
                                pe.wait_ge(*slot_done[s].after(layer, V_ROUND0 + r + 1))
                            for t in range(NT):
                                tok, cols = slice(t * P, t * P + P), slice(half * HALF, half * HALF + HALF)
                                for k, (a, v) in enumerate(((w_hi, hi), (w_hi, lo), (w_lo, hi))):
                                    last = pe.matmul(bank[4 + 2 * t + half][:, :], a[:, b, tok], v[:, b, cols],
                                                     start=(first and s == 0 and k == 0),
                                                     stop=(final and s == SLOTS - 1 and k == 2))
                            last.then_inc(part_used[2 * b + half].sem, 1)

                down(0, 0, first=True)
                with pe.Fori(1, CHUNK_ROUNDS) as r:
                    down(r, r)
                with pe.Fori(CHUNK_ROUNDS, U_ROUNDS - 1) as r:
                    down(r)
                down(U_ROUNDS - 1, final=True)

        @block.scalar
        def _(act):
            def copy_job(layer, dst, src, *name):
                act.wait_ge(*full(layer, *name))
                act.activation(dst, src, ACT.Copy).then_inc(*stores(*name))

            def square_sums(layer, src, junk, order, col, update=None):
                if update:
                    act.preload_act_table(ACT.Sqrt)
                for t in range(NT):
                    if update:
                        act.wait_ge(*in_sbuf(layer, update, 2 * t + 1))
                    act.activation(junk[:, t, :], src[:, t, :], ACT.Square, accum_out=stat[:, col + t:col + t + 1]) \
                        .then_inc(squares.sem, 1)

            def roots(layer, order, col):
                act.wait_ge(*meansq.after(layer, order + 1))
                act.activation(stat[:, col + 4:col + 6], stat[:, col + 2:col + 4], ACT.Sqrt).then_inc(root.sem, 1)

            def part_high(layer, slot, m_pair, b, half):
                part, cols = 2 * b + half, slice(half * HALF, half * HALF + HALF)
                act.wait_ge(*part_used[part].after(layer, m_pair))
                act.activation(hi[:, b, cols], ring[:, slot, cols], ACT.Copy).then_inc(high_ready[part].sem, 1)

            def split_high(layer, *name):
                act.wait_ge(*loaded(layer, *name))
                m = SPLITS[name]
                for half in range(2):
                    part_high(layer, TILES[name] % SLOTS, m // 2, m % 2, half)

            def high_half_after(layer, half, *name):
                later = next(n for n, m in SPLITS.items() if m == SPLITS[name] + 2)
                if half == 0:
                    act.wait_ge(*loaded(layer, *later))
                m = SPLITS[later]
                part_high(layer, TILES[later] % SLOTS, m // 2, m % 2, half)

            def high_after(layer, *name):
                for half in range(2):
                    high_half_after(layer, half, *name)

            def both(name, i, cols=P):
                return bank_of(name, i)[:, 0:NT * P].rearrange("p (t c) -> p t c", t=NT)

            def raw_copy(layer, k):
                name = ROPES[k]
                rows = P if name[0] in ("rq", "rk") else MQK
                if k >= 2:
                    act.wait_ge(*raw_cos.after(layer, k - 1))
                    act.wait_ge(*full(layer, "rot", *ROPES[k - 2]))
                copy_job(layer, raw[0:rows, k % 2, :], bank_of(*name)[0:rows, 0:SEQ], *name)

            def ret_store(layer, h):
                act.wait_ge(*ret_full.after(layer, h + 1))
                act.activation(ytok[:, :, h * P:h * P + P], bank[6 + h % 2][:, 0:2 * P].rearrange("p (t e) -> p t e", t=NT),
                               ACT.Copy).then_inc(ret_stored.sem, 1)

            def yT_store(layer, n):
                copy_job(layer, yT[:, (n // 2 % 3) * 4:(n // 2 % 3) * 4 + 4, (n % 2) * P:(n % 2) * P + P],
                         bank_of("ty", n).rearrange("p (c s) -> p c s", c=4), "ty", n)

            def xa_high(layer, t):
                act.wait_ge(*full(layer, "ty", 6 + t))
                act.activation(h_hi[:, 0:4, t * P:t * P + P], bank_of("ty", 6 + t).rearrange("p (c s) -> p c s", c=4), ACT.Copy) \
                    .then_inc(in_high.sem, 1)

            def soft(layer, step, units):
                if step in units:
                    kind, t, h = UNITS[step]
                    keys = SEQ if kind == "xa" else P * (t + 1)
                    act.wait_ge(*negmax_ready.after(layer, step + 1))
                    if step >= 2:
                        act.wait_ge(*probT_full.after(layer, step - 1))
                    src = bank[4 + (RH + step) % 2][:, 0:keys] if kind == "xa" else sm[:, step % 2, 0:keys]
                    act.activation(prob[:, step % 2, 0:keys], src, ACT.Exp, bias=negmax[:, step:step + 1],
                                   scale=XD ** -0.5 if kind == "xa" else 1.0,
                                   accum_out=sums[:, step:step + 1]).then_inc(prob_ready.sem, 1)
                if step - 1 in units:
                    v = step - 1
                    kind, t, h = UNITS[v]
                    keys = SEQ if kind == "xa" else P * (t + 1)
                    act.wait_ge(*probT_full.after(layer, v + 1))
                    if v >= 2:
                        act.wait_ge(*pv_done.after(layer, v - 1))
                    act.activation(probT[:, v % 2, 0:keys], bank[6][:, 0:keys], ACT.Copy).then_inc(probT_ready.sem, 1)
                if step in END_AT and END_AT[step] < NT:
                    g = END_AT[step]
                    act.wait_ge(*sink_shift.after(layer, g + 1))
                    act.activation(sinkexp[:, g, :], sinkexp[:, g, :], ACT.Exp).then_inc(sink_exp.sem, 1)

            with act.Fori(0, DEPTH) as layer:
                act.preload_act_table(ACT.Sqrt)
                act.wait_ge(x_loaded.sem, 16)
                act.wait_ge(*peer_added.after(layer, 0))
                square_sums(layer, x, xn, 0, 0)
                roots(layer, 0, 0)
                act.wait_ge(*mem_loaded.after(layer, 1))
                square_sums(layer, mem, memT.rearrange("p c s -> p (c s)").rearrange("p (t d) -> p t d", t=NT), 1, 8)
                act.wait_ge(*in_sbuf(layer, "x0", 1, 1))
                act.activation(h_hi[:, :, :], hT[:, :, :], ACT.Copy).then_inc(h_split.sem, 1)
                roots(layer, 1, 8)
                for i in range(4):
                    copy_job(layer, rv[:, :, i * P:i * P + P], both("rv", i), "rv", i)
                    if i < 2:
                        split_high(layer, "rq", i)
                for k in range(8):
                    if k < 6:
                        high_after(layer, *ROPES[k])
                    raw_copy(layer, k)
                copy_job(layer, sv, both("sv", 0), "sv", 0)
                split_high(layer, "kr", 0)
                for i in range(2):
                    copy_job(layer, qk[:, :, i * P:i * P + P], both("qa", i), "qa", i)
                    if i == 0:
                        split_high(layer, "sq", 0)
                ret_store(layer, 0)
                ret_store(layer, 1)
                copy_job(layer, qk[:, :, QR:QR + P], both("kva", 0), "kva", 0)
                act.wait_ge(*in_sbuf(layer, "kva", 0))
                for t in range(NT):
                    for k, cols in enumerate((slice(0, QR), slice(QR, QR + KVR))):
                        act.activation(junk[:, t, cols], qk[:, t, cols], ACT.Square,
                                       accum_out=stat[:, 32 + 2 * k + t:33 + 2 * k + t]).then_inc(qk_sq.sem, 1)
                ret_store(layer, 2)
                high_after(layer, "kr", 0)
                raw_copy(layer, 8)
                ret_store(layer, 3)
                high_after(layer, "sq", 0)
                copy_job(layer, swq[:, 0, :], bank_of("sq", 0)[:, 0:SEQ], "sq", 0)
                act.wait_ge(*qk_ms.after(layer, 2))
                act.activation(stat[:, 40:44], stat[:, 36:40], ACT.Sqrt).then_inc(qk_root.sem, 1)
                for i in range(1, 4):
                    if i < 3:
                        high_after(layer, "sq", i)
                    copy_job(layer, swq[:, i, :], bank_of("sq", i)[:, 0:SEQ], "sq", i)
                act.wait_ge(*ret_ms.after(layer, 1))
                act.activation(stat[:, 56:64], stat[:, 48:56], ACT.Sqrt).then_inc(ret_root.sem, 1)
                for i in range(4):
                    act.wait_ge(*full(layer, "rg", i))
                    if i:
                        act.wait_ge(*in_sbuf(layer, "rg", i - 1))
                    act.activation(sgm, both("rg", i), ACT.Sigmoid).then_inc(gate_sig.sem, 1)
                for h in range(MH):
                    raw_copy(layer, 9 + h)
                    copy_job(layer, mk[0:NOPE, h, :], bank_of("kn", h)[0:NOPE, 0:SEQ], "kn", h)
                for t in range(NT):
                    split_high(layer, "gate", t)
                    copy_job(layer, mv[:, t, :], bank_of("mv", t), "mv", t)
                yT_store(layer, 0)
                yT_store(layer, 1)
                for step in mix_steps():
                    for g, half in gate_halves_at(step):
                        high_half_after(layer, half, "gate", g)
                        if half == 1:
                            copy_job(layer, gates[:, g, :], bank_of("gate", g)[:, 0:SEQ], "gate", g)
                    soft(layer, step, range(MIX_UNITS))
                    if step - 1 in END_AT:
                        yT_store(layer, 2 + END_AT[step - 1])
                    if step >= MIX_UNITS:
                        br = step - MIX_UNITS
                        for g in range(GATES - JOB_BANKS, GATES):
                            act.wait_ge(*in_sbuf(layer, "gate", g))
                        act.wait_ge(*in_sbuf(layer, "ty", 2 * br + 1))
                        act.activation(h_hi[:, 4 * br:4 * br + 4, :], yT[:, 4 * br:4 * br + 4, :], ACT.Copy).then_inc(in_high.sem, 1)
                for br in range(3):
                    for cg in range(4):
                        g = GATE_OF[br] * DC + cg * 2
                        act.activation(gates[:, g:g + 2, :], gates[:, g:g + 2, :], ACT.Sigmoid).then_inc(gates_open.sem, 1)
                        high_after(layer, "branch", br * 4 + cg)
                        if br == 2 and cg == 2:
                            act.wait_ge(*gated.after(layer, 12))
                            act.activation(h_hi[:, 4:8, :], merged[:, 0:4, :], ACT.Copy).then_inc(in_high.sem, 1)
                    if br == 0:
                        yT_store(layer, 5)
                        act.wait_ge(*in_sbuf(layer, "ty", 5))
                        act.wait_ge(*full(layer, "branch", 0, 3, 1))
                        act.activation(h_hi[:, 0:4, :], yT[:, 8:12, :], ACT.Copy).then_inc(in_high.sem, 1)
                act.wait_ge(*gated.after(layer, 16))
                act.activation(h_hi[:, 0:4, :], merged[:, 4:8, :], ACT.Copy).then_inc(in_high.sem, 1)
                for n in range(6):
                    high_after(layer, "wo", n)
                square_sums(layer, x, xn, 2, 16, "wo")
                roots(layer, 2, 16)
                for i in range(4):
                    copy_job(layer, xk[:, i, :], bank_of("xk", i)[:, 0:SEQ], "xk", i)
                act.preload_act_table(ACT.Exp)
                for i in range(4):
                    copy_job(layer, xq[:, i, :], bank_of("xq", i)[:, 0:SEQ], "xq", i)
                for step in xa_steps():
                    i = step - MIX_UNITS
                    if i < XH:
                        copy_job(layer, xv[:, :, i * P:i * P + P], both("xv", i), "xv", i)
                        if i < 2:
                            split_high(layer, "xo", i)
                    soft(layer, step, range(MIX_UNITS, len(UNITS)))
                    if step - 1 in END_AT and END_AT[step - 1] >= 4:
                        xa_high(layer, 0)
                xa_high(layer, 1)
                for n in range(2):
                    high_after(layer, "xo", n)
                square_sums(layer, x, xn, 3, 24, "xo")
                roots(layer, 3, 24)
                act.wait_ge(*in_sbuf(layer, "x2", 1, 1))
                act.activation(h_hi[:, :, :], hT[:, :, :], ACT.Copy).then_inc(h_split.sem, 1)
                def high(r, s):
                    act.wait_ge(*slot_full[s].after(layer, U_ROUND0 + r + 1))
                    for half in range(2):
                        part_high(layer, s, U_PAIRS + r * 2 + s // 2, s % 2, half)

                for i in range(2, 4):
                    split_high(layer, "pq", i)
                for i in range(8):
                    if 2 <= i < 6:
                        high_after(layer, "pq", i)
                    if i >= 6:
                        high(0, i - 6)
                    copy_job(layer, pq[:, i, :], bank_of("pq", i)[:, 0:SEQ], "pq", i)
                for t in range(NT):
                    for pair in range(PH // 2):
                        for p in range(2):
                            j = (t * PH + 2 * pair) * 2 + p
                            copy_job(layer, sc[:, j:j + 3:2, :],
                                     bank_of("ps", t, pair, p)[:, 0:2 * NK].rearrange("p (a n) -> p a n", a=2), "ps", t, pair, p)

                def high_ahead(r, s):
                    high(r + (s + 2) // SLOTS, (s + 2) % SLOTS)

                def u_round(r):
                    for s in range(SLOTS):
                        high_ahead(r, s)
                        act.wait_ge(*part_used[2 * (s % 2) + 1].after(layer, r * 2 + s // 2 + (U_PAIRS + 1)))
                        act.activation(pre[:, bass.ds(r * SLOTS + s, 1), :].squeeze(1), bank[4 + s][:, 0:SEQ], ACT.Gelu) \
                            .then_inc(pre_stored[s].sem, 1)

                def w_part(r, s):
                    b = s % 2
                    act.wait_ge(*part_used[2 * b + 1].after(layer, r * 2 + s // 2 + V_PAIRS))
                    act.activation(w_hi[:, b, :], pre[:, bass.ds(r * SLOTS + s, 1), :].squeeze(1), ACT.Copy).then_inc(w_high[b].sem, 1)

                def v_round(r, opens_chunk=False, final=False):
                    for s in range(SLOTS):
                        if final and s >= 2:
                            break
                        high_ahead(r + U_ROUNDS, s)
                        if opens_chunk and s == 2:
                            for b in range(2):
                                act.wait_ge(*cells_gated[b].after(layer, 2 * CHUNK_ROUNDS))
                        w_part(r + (s + 2) // SLOTS, (s + 2) % SLOTS)

                act.preload_act_table(ACT.Gelu)
                with act.Fori(0, EXP_ROUND) as r:
                    u_round(r)
                act.wait_ge(*best_shift.after(layer, 1))
                act.activation(best, best, ACT.Exp).then_inc(best_exp.sem, 1)
                act.preload_act_table(ACT.Gelu)
                with act.Fori(EXP_ROUND, TURN_ROUND) as r:
                    u_round(r)
                act.wait_ge(*choice_made.after(layer, 1))
                with act.Fori(TURN_ROUND, U_ROUNDS) as r:
                    u_round(r)
                for b in range(2):
                    act.wait_ge(*cells_gated[b].after(layer, CHUNK_ROUNDS))
                w_part(0, 0)
                w_part(0, 1)
                with act.Fori(0, CHUNK_ROUNDS - 1) as r:
                    v_round(r)
                v_round(CHUNK_ROUNDS - 1, opens_chunk=True)
                with act.Fori(CHUNK_ROUNDS, U_ROUNDS - 1) as r:
                    v_round(r)
                v_round(U_ROUNDS - 1, final=True)
            act.preload_act_table(ACT.Sqrt)
            act.wait_ge(*peer_added.after(DEPTH, 0))
            for t in range(NT):
                last = act.activation(xn[:, t, :], x[:, t, :], ACT.Square, accum_out=stat[:, t:t + 1])
            last.then_inc(f_sq.sem, 1)
            act.wait_ge(f_ms.sem, 1)
            act.activation(stat[:, 4:6], stat[:, 2:4], ACT.Sqrt).then_inc(f_root.sem, 1)

        @block.vector
        def _(dve):
            def norm_rows(layer, src, dst, order, col):
                dve.wait_ge(*squares.after(layer, 2 * order + 2))
                dve.tensor_scalar(stat[:, col + 2:col + 4], stat[:, col:col + 2], 1.0 / D, EPS, ALU.mult, ALU.add) \
                    .then_inc(meansq.sem, 1)
                dve.wait_ge(*root.after(layer, order + 1))
                dve.reciprocal(stat[:, col + 6:col + 8], stat[:, col + 4:col + 6]).then_inc(rstd.sem, 1)
                dve.wait_ge(*rstd.after(layer, order + 1))
                for t in range(NT):
                    dve.tensor_scalar(dst[:, t, :], src[:, t, :], stat[:, col + 6 + t:col + 7 + t], None, ALU.mult) \
                        .then_inc(normed.sem, 1)

            def gain_store(layer, name, dst, g):
                for t in range(NT):
                    for half in range(2):
                        dve.wait_ge(*full(layer, name, t, half))
                        ps = bank_of(name, t, half)
                        dve.tensor_tensor(dst[:, 4 * half:4 * half + 4, t * P:t * P + P],
                                                ps.rearrange("p (c s) -> p c s", c=4),
                                                vec[:, g + 4 * half:g + 4 * half + 4].unsqueeze(2).broadcast_to([P, 4, P]),
                                                ALU.mult).then_inc(*stores(name, t, half))

            def rope(layer, k):
                name, b = ROPES[k], k % 2
                wide = name[0] in ("rq", "rk")
                rows = P if wide else MQK
                c, s = (cos, sin) if wide else (cosm, sinm)
                dst = {"rq": lambda i: rq[:, i, :], "rk": lambda i: rk[:, i, :], "kr": lambda i: krr[0:MQK, :],
                       "qb": lambda i: mq[:, i, :]}[name[0]](name[1])
                dve.wait_ge(*in_sbuf(layer, *name))
                dve.tensor_tensor(cosx[0:rows, b, :], raw[0:rows, b, :], c, ALU.mult).then_inc(raw_cos.sem, 1)
                dve.wait_ge(*full(layer, "rot", *name))
                ps = bank_of("rot", *name)
                dve.tensor_tensor(sinx[0:rows, b, :], ps[0:rows, 0:SEQ], s, ALU.mult).then_inc(*stores("rot", *name))
                dve.wait_ge(*raw_cos.after(layer, k + 1))
                dve.wait_ge(*in_sbuf(layer, "rot", *name))
                dve.tensor_tensor(dst, cosx[0:rows, b, :], sinx[0:rows, b, :], ALU.add).then_inc(roped.sem, 1)

            def ret_decay(layer, h):
                dve.wait_ge(*score_full.after(layer, h + 1))
                if h >= 2:
                    dve.wait_ge(*ret_full.after(layer, h - 1))
                ps = bank[4 + h % 2]
                dve.tensor_tensor(retT[:, h % 2, 0:SEQ], ps[:, 0:SEQ], decay[:, h, :], ALU.mult)
                dve.tensor_tensor(retT[:, h % 2, SEQ:SEQ + P], ps[:, SEQ:SEQ + P], decay[:, h, 0:P], ALU.mult) \
                    .then_inc(ret_scores.sem, 1)

            def soft(layer, step, units):
                if step in units:
                    kind, t, h = UNITS[step]
                    keys = SEQ if kind == "xa" else P * (t + 1)
                    ps = bank[4 + (RH + step) % 2]
                    dve.wait_ge(*score_full.after(layer, RH + step + 1))
                    nm = negmax[:, step:step + 1]
                    if kind == "xa":
                        dve.tensor_reduce(rowm[:, step % 2:step % 2 + 1], ps[:, 0:keys], AXX, ALU.max).then_inc(xa_max.sem, 1)
                        dve.wait_ge(*xa_max.after(layer, step - MIX_UNITS + 1))
                        dve.tensor_scalar(nm, rowm[:, step % 2:step % 2 + 1], -(XD ** -0.5), None, ALU.mult) \
                            .then_inc(negmax_ready.sem, 1)
                        return
                    add = bias[:, h, SEQ - keys:SEQ] if kind == "swa" else causal[:, SEQ - keys:SEQ]
                    if step >= 2:
                        dve.wait_ge(*prob_ready.after(layer, step - 1))
                    dve.scalar_tensor_tensor(out=sm[:, step % 2, 0:keys], in0=ps[:, 0:keys],
                                             scalar=(SD if kind == "swa" else MQK) ** -0.5, in1=add,
                                             op0=ALU.mult, op1=ALU.add).then_inc(masked.sem, 1)
                    dve.wait_ge(*masked.after(layer, step + 1))
                    last = dve.tensor_reduce(nm, sm[:, step % 2, 0:keys], AXX, ALU.max, negate=True)
                    if kind == "mla":
                        last.then_inc(negmax_ready.sem, 1)
                        return
                    last.then_inc(rowmax.sem, 1)
                    dve.wait_ge(*rowmax.after(layer, step + 1))
                    dve.tensor_tensor(nm, nm, negsink[:, h:h + 1], ALU.min).then_inc(negmax_ready.sem, 1)

            def end_group(layer, step):
                if step not in END_AT:
                    return
                g = END_AT[step]
                kind, t, v0, v1 = GROUPS[g]
                heads = v1 - v0 + 1
                den = sums[:, v0:v1 + 1]
                if kind == "swa":
                    dve.wait_ge(*negmax_ready.after(layer, v1 + 1))
                    dve.tensor_tensor(sinkexp[:, t, :], negmax[:, v0:v1 + 1], vec[:, SINKS:SINKS + 8], ALU.add) \
                        .then_inc(sink_shift.sem, 1)
                    dve.wait_ge(*prob_ready.after(layer, v1 + 1))
                    dve.wait_ge(*sink_exp.after(layer, t + 1))
                    dve.tensor_tensor(sinkexp[:, t, :], sinkexp[:, t, :], den, ALU.add).then_inc(den_ready.sem, 1)
                    dve.wait_ge(*den_ready.after(layer, t + 1))
                    den = sinkexp[:, t, :]
                dve.wait_ge(*prob_ready.after(layer, v1 + 1))
                dve.reciprocal(rden[:, t, 0:heads], den).then_inc(rden_ready.sem, 1)
                dve.wait_ge(*rden_ready.after(layer, g + 1))
                dve.wait_ge(*pv_done.after(layer, v1 + 1))
                dve.wait_ge(*full(layer, "ty", g))
                dve.tensor_tensor(ytok[:, t, :].rearrange("p (h e) -> p h e", h=heads),
                                  bank[7][:, :].rearrange("p (h e) -> p h e", h=heads),
                                  rden[:, t, 0:heads].unsqueeze(2).broadcast_to([P, heads, 512 // heads]), ALU.mult) \
                    .then_inc(ytok_ready.sem, 1)

            def add_x(layer, name):
                for i in range(4):
                    dve.wait_ge(*full(layer, name, i))
                    ps = bank_of(name, i)
                    xs = x[:, i // 2, (i % 2) * 512:(i % 2) * 512 + 512]
                    dve.tensor_tensor(xs, xs, ps, ALU.add).then_inc(*stores(name, i))

            def in_low_part(layer, n, at, src):
                dve.wait_ge(*in_high.after(layer, n + 1))
                dve.tensor_tensor(h_lo[:, at:at + 4, :], src, h_hi[:, at:at + 4, :].bitcast(F32), ALU.subtract) \
                    .then_inc(in_low.sem, 1)

            def xa_low(layer, t):
                dve.wait_ge(*in_high.after(layer, 5 + t + 1))
                tok = slice(t * P, t * P + P)
                dve.tensor_tensor(h_lo[:, 0:4, tok], bank_of("ty", 6 + t).rearrange("p (c s) -> p c s", c=4),
                                  h_hi[:, 0:4, tok].bitcast(F32), ALU.subtract).then_inc(*stores("ty", 6 + t))

            dve.wait_ge(cst_loaded.sem, 16)
            with dve.Fori(0, DEPTH) as layer:
                norm_rows(layer, x, xn, 0, 0)
                dve.wait_ge(*vec_loaded.after(layer, 1))
                dve.tensor_scalar(negsink, vec[:, SINKS:SINKS + 8], -1.0, None, ALU.mult).then_inc(sink_negated.sem, 1)
                gain_store(layer, "x0", hT, G_MIX)
                dve.wait_ge(*h_split.after(layer, 1))
                dve.tensor_tensor(h_lo[:, :, :], hT[:, :, :], h_hi[:, :, :].bitcast(F32), ALU.subtract).then_inc(h_split.sem, 1)
                norm_rows(layer, mem, mem, 1, 8)
                gain_store(layer, "mem", memT, G_MEM)
                dve.wait_ge(*tab_loaded.after(layer, 1))
                for k in range(8):
                    rope(layer, k)
                for h in range(RH):
                    ret_decay(layer, h)
                rope(layer, 8)
                dve.wait_ge(*roped.after(layer, 9))
                dve.tensor_copy(mk[NOPE:MQK, :, :], krr[NOPE:MQK, :].unsqueeze(1).broadcast_to([ROPE, MH, SEQ])) \
                    .then_inc(kr_spread.sem, 1)
                dve.wait_ge(*qk_sq.after(layer, 4))
                dve.tensor_scalar(stat[:, 36:38], stat[:, 32:34], 1.0 / QR, EPS, ALU.mult, ALU.add).then_inc(qk_ms.sem, 1)
                dve.tensor_scalar(stat[:, 38:40], stat[:, 34:36], 1.0 / KVR, EPS, ALU.mult, ALU.add).then_inc(qk_ms.sem, 1)
                dve.wait_ge(*qk_root.after(layer, 1))
                dve.reciprocal(stat[:, 44:48], stat[:, 40:44]).then_inc(qk_rstd.sem, 1)
                dve.wait_ge(*qk_rstd.after(layer, 1))
                for t in range(NT):
                    for k, cols in enumerate((slice(0, QR), slice(QR, QR + KVR))):
                        dve.tensor_scalar(qk[:, t, cols], qk[:, t, cols], stat[:, 44 + 2 * k + t:45 + 2 * k + t], None,
                                          ALU.mult).then_inc(qk_normed.sem, 1)
                for i in range(2):
                    dve.wait_ge(*loaded(layer, "bias", i))
                    dve.tensor_tensor(bias[:, 4 * i:4 * i + 4, :], tile("bias", i).rearrange("p (h s) -> p h s", h=4),
                                      window.unsqueeze(1).broadcast_to([P, 4, SEQ]), ALU.add) \
                        .then_inc(slot_done[TILES["bias", i] % SLOTS].sem, 1)
                dve.wait_ge(*ret_stored.after(layer, RH))
                ys = ytok.rearrange("p t (h e) -> p t h e", h=RH)
                for t in range(NT):
                    dve.tensor_tensor(rsq[:, t, :], ytok[:, t, :], ytok[:, t, :], ALU.mult).then_inc(ret_sq.sem, 1)
                dve.wait_ge(*ret_sq.after(layer, 2))
                for t in range(NT):
                    dve.tensor_reduce(rsum[:, 4 * t:4 * t + 4], rsq[:, t, :].rearrange("p (h e) -> p h e", h=RH), AXX, ALU.add) \
                        .then_inc(ret_sum.sem, 1)
                dve.wait_ge(*ret_sum.after(layer, 2))
                dve.tensor_scalar(stat[:, 48:56], rsum, 1.0 / P, EPS, ALU.mult, ALU.add).then_inc(ret_ms.sem, 1)
                dve.wait_ge(*ret_root.after(layer, 1))
                dve.reciprocal(rsum, stat[:, 56:64]).then_inc(ret_rstd.sem, 1)
                dve.wait_ge(*ret_rstd.after(layer, 1))
                for t in range(NT):
                    dve.tensor_tensor(ys[:, t], ys[:, t], rsum[:, 4 * t:4 * t + 4].unsqueeze(2).broadcast_to([P, RH, P]),
                                      ALU.mult).then_inc(ret_scaled.sem, 1)
                dve.wait_ge(*full(layer, "tqa", 0))
                ps = bank_of("tqa", 0)
                dve.tensor_tensor(qanT, ps.rearrange("p (c s) -> p c s", c=2),
                                        vec[:, G_Q:G_Q + 2].unsqueeze(2).broadcast_to([P, 2, SEQ]), ALU.mult).then_inc(*stores("tqa", 0))
                dve.wait_ge(*full(layer, "tkv", 0))
                ps = bank_of("tkv", 0)
                dve.tensor_scalar(kvanT, ps[:, 0:SEQ], vec[:, G_KV:G_KV + 1], None, ALU.mult).then_inc(*stores("tkv", 0))
                dve.wait_ge(*full(layer, "sk", 0))
                ps = bank_of("sk", 0)
                for g in range(SKV):
                    for half in range(2):
                        last = dve.tensor_copy(swk[64 * half:64 * half + 64, g, :], ps[64 * g:64 * g + 64, 0:SEQ])
                last.then_inc(*stores("sk", 0))
                for i in range(4):
                    dve.wait_ge(*gate_sig.after(layer, i + 1))
                    ps = bank_of("rg", i)[:, 0:NT * P].rearrange("p (t c) -> p t c", t=NT)
                    dve.tensor_tensor(rgs[:, :, i * P:i * P + P], ps, sgm, ALU.mult).then_inc(*stores("rg", i))
                dve.wait_ge(*in_sbuf(layer, "rg", 3))
                dve.wait_ge(*ret_scaled.after(layer, 2))
                for t in range(NT):
                    dve.tensor_tensor(ytok[:, t, :], ytok[:, t, :], rgs[:, t, :], ALU.mult).then_inc(ytok_ready.sem, 1)
                for h in range(MH):
                    rope(layer, 9 + h)
                for i in range(2):
                    dve.wait_ge(*slot_done[TILES["bias", i] % SLOTS].after(layer, TILES["bias", i] // SLOTS + 1))
                dve.wait_ge(*sink_negated.after(layer, 1))
                for step in mix_steps():
                    soft(layer, step, range(MIX_UNITS))
                    end_group(layer, step)
                    if step >= MIX_UNITS:
                        br = step - MIX_UNITS
                        in_low_part(layer, br, 4 * br, yT[:, 4 * br:4 * br + 4, :])
                for br in range(3):
                    for cg in range(4):
                        for m in range(2):
                            d = cg * 2 + m
                            dve.wait_ge(*full(layer, "branch", br, cg, m))
                            ps = bank_of("branch", br, cg, m)
                            gate = gates[:, GATE_OF[br] * DC + d, :]
                            if m == 0:
                                dve.wait_ge(*gates_open.after(layer, br * 4 + cg + 1))
                            if br == 0:
                                dve.tensor_tensor(merged[:, d, :], ps[:, 0:SEQ], gate, ALU.mult).then_inc(*stores("branch", br, cg, m))
                                continue
                            dve.tensor_tensor(gate, ps[:, 0:SEQ], gate, ALU.mult).then_inc(*stores("branch", br, cg, m))
                            dve.wait_ge(*in_sbuf(layer, "branch", br, cg, m))
                            if br == 1:
                                dve.wait_ge(*in_sbuf(layer, "branch", 0, cg, m))
                            else:
                                dve.wait_ge(*gated.after(layer, d + 1))
                            dve.tensor_tensor(merged[:, d, :], merged[:, d, :], gate, ALU.add).then_inc(gated.sem, 1)
                        if br == 2 and cg == 2:
                            in_low_part(layer, 3, 4, merged[:, 0:4, :])
                    if br == 0:
                        in_low_part(layer, 2, 0, yT[:, 8:12, :])
                in_low_part(layer, 4, 0, merged[:, 4:8, :])
                add_x(layer, "wo")
                norm_rows(layer, x, xn, 2, 16)
                gain_store(layer, "x1", hT, G_XA)
                for step in xa_steps():
                    soft(layer, step, range(MIX_UNITS, len(UNITS)))
                    if END_AT.get(step, 0) >= 4:
                        end_group(layer, step)
                    if END_AT.get(step - 1, 0) >= 4:
                        xa_low(layer, 0)
                xa_low(layer, 1)
                add_x(layer, "xo")
                norm_rows(layer, x, xn, 3, 24)
                gain_store(layer, "x2", hT, G_FFN)
                dve.wait_ge(*h_split.after(layer, 3))
                dve.tensor_tensor(h_lo[:, :, :], hT[:, :, :], h_hi[:, :, :].bitcast(F32), ALU.subtract).then_inc(h_split.sem, 1)

                dve.wait_ge(*in_sbuf(layer, "ps", NT - 1, PH // 2 - 1, 1))
                segs = range(NT * PH * 2)
                settle(dve)
                for j in segs:
                    last = dve.max(top[:, j, 0:8], sc[:, j, :])
                last.then_inc(top1.sem, 1)
                dve.wait_ge(*top1.after(layer, 1))
                settle(dve)
                for j in segs:
                    last = dve.max_index(topi[:, j, 0:8], top[:, j, 0:8], sc[:, j, :])
                last.then_inc(top_idx1.sem, 1)
                dve.wait_ge(*top_idx1.after(layer, 1))
                settle(dve)
                for j in segs:
                    last = dve.match_replace(sc[:, j, :], top[:, j, 0:8], sc[:, j, :], LEAST)
                last.then_inc(top_cut.sem, 1)
                dve.wait_ge(*top_cut.after(layer, 1))
                settle(dve)
                for j in segs:
                    last = dve.max(top[:, j, 8:16], sc[:, j, :])
                last.then_inc(top2.sem, 1)
                dve.wait_ge(*top2.after(layer, 1))
                settle(dve)
                for j in segs:
                    last = dve.max_index(topi[:, j, 8:16], top[:, j, 8:16], sc[:, j, :])
                last.then_inc(top_idx2.sem, 1)
                dve.wait_ge(*top_idx2.after(layer, 1))
                dve.tensor_copy(topf, topi).then_inc(top_float.sem, 1)
                top_v = top.rearrange("p (t h a) k -> p t h a k", t=NT, h=PH)
                for t in range(NT):
                    if t:
                        dve.wait_ge(*best_idx2.after(layer, t))
                    dve.tensor_tensor(cand.rearrange("p h (i j) -> p h i j", i=TOPK),
                                      top_v[:, t, :, 0, :].unsqueeze(3).broadcast_to([P, PH, TOPK, TOPK]),
                                      top_v[:, t, :, 1, :].unsqueeze(2).broadcast_to([P, PH, TOPK, TOPK]), ALU.add) \
                        .then_inc(cand_ready.sem, 1)
                    dve.wait_ge(*cand_ready.after(layer, t + 1))
                    settle(dve)
                    for h in range(PH):
                        last = dve.max(best[:, t * PH + h, 0:8], cand[:, h, :])
                    last.then_inc(best1.sem, 1)
                    dve.wait_ge(*best1.after(layer, t + 1))
                    settle(dve)
                    for h in range(PH):
                        last = dve.max_index(besti[:, t * PH + h, 0:8], best[:, t * PH + h, 0:8], cand[:, h, :])
                    last.then_inc(best_idx1.sem, 1)
                    dve.wait_ge(*best_idx1.after(layer, t + 1))
                    settle(dve)
                    for h in range(PH):
                        last = dve.match_replace(cand[:, h, :], best[:, t * PH + h, 0:8], cand[:, h, :], LEAST)
                    last.then_inc(best_cut.sem, 1)
                    dve.wait_ge(*best_cut.after(layer, t + 1))
                    settle(dve)
                    for h in range(PH):
                        last = dve.max(best[:, t * PH + h, 8:16], cand[:, h, :])
                    last.then_inc(best2.sem, 1)
                    dve.wait_ge(*best2.after(layer, t + 1))
                    settle(dve)
                    for h in range(PH):
                        last = dve.max_index(besti[:, t * PH + h, 8:16], best[:, t * PH + h, 8:16], cand[:, h, :])
                    last.then_inc(best_idx2.sem, 1)
                dve.wait_ge(*best_idx2.after(layer, NT))
                chosen_v = chosen[:, :, :, :].rearrange("p a t (h k) -> p a t h k", h=PH)
                best_v = best.rearrange("p g k -> p (g k)")
                besti_v = besti.rearrange("p g k -> p (g k)")
                dve.tensor_copy(bestmax, best[:, :, 0:1]).then_inc(best_top.sem, 1)
                dve.tensor_scalar(posi[:, 0, :], besti_v, 4, None, ALU.logical_shift_right)
                dve.tensor_scalar(posi[:, 1, :], besti_v, TOPK - 1, None, ALU.bitwise_and).then_inc(pos_split.sem, 1)
                dve.wait_ge(*best_top.after(layer, 1))
                dve.tensor_tensor(best, best, bestmax.broadcast_to([P, NT * PH, TOPK]), ALU.subtract) \
                    .then_inc(best_shift.sem, 1)
                dve.wait_ge(*pos_split.after(layer, 1))
                dve.tensor_copy(posf.rearrange("p a b -> p (a b)"), posi.rearrange("p a b -> p (a b)")).then_inc(pos_float.sem, 1)
                dve.wait_ge(*pos_float.after(layer, 1))
                dve.wait_ge(*top_float.after(layer, 1))
                topf_v = topf.rearrange("p (t h a) k -> p t h a k", t=NT, h=PH)
                oh4 = onehot.rearrange("p (h k) i -> p h k i", h=PH)
                n = 0
                for a in range(2):
                    for t in range(NT):
                        if n:
                            dve.wait_ge(*index_ready.after(layer, n))
                        dve.tensor_tensor(onehot, posf[:, a * NT + t, :].unsqueeze(2).broadcast_to([P, PH * TOPK, TOPK]),
                                          iota[:, 0:TOPK].unsqueeze(1).broadcast_to([P, PH * TOPK, TOPK]), ALU.is_equal) \
                            .then_inc(onehot_ready.sem, 1)
                        dve.wait_ge(*onehot_ready.after(layer, n + 1))
                        dve.tensor_tensor(oh4, oh4, topf_v[:, t, :, a, :].unsqueeze(2).broadcast_to([P, PH, TOPK, TOPK]),
                                          ALU.mult).then_inc(picked.sem, 1)
                        dve.wait_ge(*picked.after(layer, n + 1))
                        dve.tensor_reduce(chosen[:, a, t, :], onehot, AXX, ALU.add).then_inc(index_ready.sem, 1)
                        n += 1
                dve.wait_ge(*best_exp.after(layer, 1))
                dve.tensor_reduce(bestsum, best, AXX, ALU.add).then_inc(best_sum.sem, 1)
                dve.wait_ge(*best_sum.after(layer, 1))
                dve.reciprocal(bestsum, bestsum).then_inc(best_rsum.sem, 1)
                dve.wait_ge(*best_rsum.after(layer, 1))
                dve.wait_ge(*index_ready.after(layer, 2 * NT))
                dve.tensor_tensor(chosen[:, 2, :, :].rearrange("p t (h k) -> p (t h) k", h=PH), best,
                                  bestsum.unsqueeze(2).broadcast_to([P, NT * PH, TOPK]), ALU.mult).then_inc(choice_made.sem, 1)
                for a in range(3):
                    dve.wait_ge(*choice_turned.after(layer, a + 1))
                    dve.tensor_copy(chosenT[:, a, :], bank[a][:, 0:SEQ]).then_inc(choiceT_ready.sem, 1)
                dve.wait_ge(*choiceT_ready.after(layer, 3))

                rest = chosenT[:, 2, :]
                for n in range(3):
                    if n:
                        dve.wait_ge(*gate_rest.after(layer, 2 * n))
                    dve.tensor_copy(gate_parts[n], rest).then_inc(gate_rest.sem, 1)
                    if n < 2:
                        dve.wait_ge(*gate_rest.after(layer, 2 * n + 1))
                        dve.tensor_tensor(rest, rest, gate_parts[n], ALU.subtract).then_inc(gate_rest.sem, 1)
                dve.wait_ge(*gate_rest.after(layer, 5))

                def hots(chunk, q, b):
                    step = q + chunk * CHUNK_ROUNDS
                    toks = bass.ds(q * (2 * BATCH) + b * BATCH, BATCH)

                    def over(src, n):
                        return src[:, toks].unsqueeze(2).broadcast_to([P, BATCH, n])

                    dve.wait_ge(*spread[b].after(layer, step))
                    dve.tensor_tensor(hot2[:, b], iota[:, chunk * CHUNK:chunk * CHUNK + CHUNK].unsqueeze(1)
                                      .broadcast_to([P, BATCH, CHUNK]), over(chosenT[:, 1], CHUNK), ALU.is_equal) \
                        .then_inc(hot2_open[b].sem, 1)
                    dve.tensor_tensor(hot1[:, b], iota.unsqueeze(1).broadcast_to([P, BATCH, P]), over(chosenT[:, 0], P), ALU.is_equal)
                    dve.wait_ge(*hot2_open[b].after(layer, step + 1))
                    for n in range(1 if chunk else 3):
                        last = dve.tensor_tensor(hot_gate[:, b, n], hot2[:, b], over(gate_parts[n], CHUNK), ALU.mult)
                    last.then_inc(hot_ready[b].sem, 1)

                def gate_cells(chunk, q, b):
                    dve.wait_ge(*spread[b].after(layer, q + chunk * CHUNK_ROUNDS + 1))
                    cell = pre[:, chunk * CHUNK:chunk * CHUNK + CHUNK, bass.ds(q * (2 * BATCH) + b * BATCH, BATCH)]
                    dve.tensor_tensor(cell, bank[b][:, :].rearrange("p (k n) -> p n k", k=BATCH), cell, ALU.mult) \
                        .then_inc(cells_gated[b].sem, 1)

                def v_low(r, s):
                    b = s % 2
                    for half in range(2):
                        cols = slice(half * HALF, half * HALF + HALF)
                        dve.wait_ge(*high_ready[2 * b + half].after(layer, r * 2 + s // 2 + (V_PAIRS + 1)))
                        last = dve.tensor_tensor(lo[:, b, cols], ring[:, s, cols], hi[:, b, cols].bitcast(F32), ALU.subtract)
                        if half == 0:
                            last.then_inc(low_first[b].sem, 1)
                        else:
                            last.then_inc(slot_done[s].sem, 1)

                def v_lows_ahead(r, b):
                    for s in (2 * b, 2 * b + 1):
                        v_low(r + (s + 2) // SLOTS, (s + 2) % SLOTS)

                hots(0, 0, 0)
                hots(0, 0, 1)
                for b in range(SLOTS):
                    dve.wait_ge(*pre_stored[b].after(layer, CHUNK_ROUNDS))
                settle(dve)
                with dve.Fori(0, CHUNK_ROUNDS - 1) as q:
                    for b in range(2):
                        gate_cells(0, q, b)
                        hots(0, q + 1, b)
                for b in range(2):
                    gate_cells(0, CHUNK_ROUNDS - 1, b)
                    hots(1, 0, b)
                for b in range(SLOTS):
                    dve.wait_ge(*pre_stored[b].after(layer, U_ROUNDS))
                v_low(0, 0)
                v_low(0, 1)
                with dve.Fori(0, CHUNK_ROUNDS - 1) as q:
                    for b in range(2):
                        gate_cells(1, q, b)
                        hots(1, q + 1, b)
                        v_lows_ahead(q, b)
                for b in range(2):
                    gate_cells(1, CHUNK_ROUNDS - 1, b)
                    v_lows_ahead(CHUNK_ROUNDS - 1, b)
                with dve.Fori(CHUNK_ROUNDS, U_ROUNDS - 1) as r:
                    for b in range(2):
                        v_lows_ahead(r, b)
                v_lows_ahead(U_ROUNDS - 1, 0)
                for b in range(2):
                    dve.wait_ge(*part_used[2 * b + 1].after(layer, ALL_PAIRS))
                for i in range(4):
                    xs = x[:, i // 2, (i % 2) * 512:(i % 2) * 512 + 512]
                    dve.tensor_tensor(xs, xs, bank[4 + i][:, :], ALU.add).then_inc(peer_added.sem, 1)
            dve.wait_ge(f_sq.sem, 1)
            dve.tensor_scalar(stat[:, 2:4], stat[:, 0:2], 1.0 / D, EPS, ALU.mult, ALU.add).then_inc(f_ms.sem, 1)
            dve.wait_ge(f_root.sem, 1)
            dve.reciprocal(stat[:, 6:8], stat[:, 4:6]).then_inc(f_rstd.sem, 1)
            dve.wait_ge(f_rstd.sem, 1)
            for t in range(NT):
                last = dve.tensor_scalar(xn[:, t, :], x[:, t, :], stat[:, 6 + t:7 + t], None, ALU.mult)
            last.then_inc(f_scaled.sem, 1)
            dve.wait_ge(f_scaled.sem, 1)
            dve.wait_ge(gf_loaded.sem, 16)
            dve.tensor_tensor(xn, xn, gfin.unsqueeze(1).broadcast_to([P, NT, D]), ALU.mult).then_inc(f_ready.sem, 1)


def constants():
    cst = np.zeros((P, NCONST), np.float32)
    cst[:, C_ID:C_ID + P] = np.eye(P)
    cst[np.arange(P), C_PERM + (np.arange(P) + P // 2) % P] = 1
    half = ROPE // 2
    swap = np.arange(MQK)
    swap[NOPE:] = NOPE + (np.arange(ROPE) + half) % ROPE
    cst[np.arange(MQK), C_PERM96 + swap] = 1
    cst[:, C_IOTA:C_IOTA + P] = np.arange(P)
    tab = np.zeros((P, NTAB), np.float32)

    def angles(n):
        inv = np.power(np.float32(10000.0), -np.arange(n, dtype=np.float32) / np.float32(n)).astype(np.float32)
        a = inv[:, None] * np.arange(SEQ, dtype=np.float32)[None, :]
        return np.cos(a.astype(np.float32)), np.sin(a.astype(np.float32))

    c, s = angles(P // 2)
    tab[:, T_COS:T_COS + SEQ] = np.concatenate([c, c])
    tab[:, T_SIN:T_SIN + SEQ] = np.concatenate([-s, s])
    c, s = angles(half)
    tab[0:NOPE, T_COSM:T_COSM + SEQ] = 1
    tab[NOPE:MQK, T_COSM:T_COSM + SEQ] = np.concatenate([c, c])
    tab[NOPE:MQK, T_SINM:T_SINM + SEQ] = np.concatenate([-s, s])
    j, i = np.arange(P)[:, None], np.arange(SEQ)[None, :]
    for h in range(RH):
        log_gamma = np.log(1.0 - 2.0 ** (-5.0 - h))
        tab[:, T_DECAY + h * SEQ:T_DECAY + (h + 1) * SEQ] = \
            np.where(i >= j, np.exp(log_gamma * np.maximum(i - j, 0)) * P ** -0.5, 0)
    q, k = np.arange(P)[:, None], np.arange(SEQ)[None, :]
    tab[:, T_CAUSAL:T_CAUSAL + SEQ] = np.where(k <= q + P, 0, NEG)
    rel = q + P - k
    tab[:, T_WINDOW:T_WINDOW + SEQ] = np.where((rel >= 0) & (rel < P), 0, NEG)
    return cst, tab


def buckets():
    rel = np.arange(P)[:, None] + P - np.arange(SEQ)[None, :]
    n = np.maximum(rel, 0)
    exact = 16
    large = exact + (np.log(np.maximum(n, 1) / exact) / np.log(128 / exact) * (32 - exact)).astype(np.int32)
    return np.where(n < exact, n, np.minimum(large, 31)).astype(np.int32)


def lay_out(a):
    L = DEPTH
    mix = np.zeros((L, MIX_TILES, P, D), np.float32)

    def by_columns(w, name, cols=P):
        rows = w.shape[1] // P
        for i in range(w.shape[2] // cols):
            t = w[:, :, i * cols:(i + 1) * cols].reshape(L, rows, P, cols).transpose(0, 2, 1, 3)
            mix[:, TILES[name, i]] = t.reshape(L, P, rows * cols)

    w_in = a["w_in"]
    at = 0
    for name, n in (("rq", 512), ("rk", 512), ("rv", 512), ("rg", 512), ("qa", 256), ("kva", 128), ("kr", 32),
                    ("sq", 512), ("sk", 128), ("sv", 128), ("gate", 3072)):
        w = w_in[:, :, at:at + n]
        at += n
        if name == "kr":
            w = np.concatenate([np.zeros((L, D, NOPE), np.float32), w, np.zeros((L, D, 32), np.float32)], axis=2)
        by_columns(w, name)
    table = a["rel_bias"][buckets()].transpose(2, 0, 1)
    for i in range(2):
        mix[:, TILES["bias", i]] = table[4 * i:4 * i + 4].transpose(1, 0, 2).reshape(P, D)
    qb = a["w_mla_qb"].reshape(L, 2, P, 2, 4 * MQK)
    for i in range(2):
        mix[:, TILES["qb", i], :, 0:8 * MQK] = qb[:, :, :, i].transpose(0, 2, 1, 3).reshape(L, P, 8 * MQK)
    mix[:, TILES["kvb", 0]] = a["w_mla_kvb"].reshape(L, P, MH, 2, 64).transpose(0, 1, 3, 2, 4).reshape(L, P, D)
    for br, name in enumerate(("w_branch_ret", "w_branch_swa", "w_branch_mla")):
        for cg in range(4):
            t = a[name][:, :, cg * 256:(cg + 1) * 256].reshape(L, 4, P, 2, P).transpose(0, 2, 3, 1, 4)
            mix[:, TILES["branch", br * 4 + cg]] = t.reshape(L, P, D)
    mix[:, TILES["wo", 0]:TILES["wo", 0] + 8] = a["w_out"].reshape(L, 8, P, D)
    by_columns(a["w_xkv"][:, :, 0:512], "xk")
    by_columns(a["w_xkv"][:, :, 512:1024], "xv")
    by_columns(a["w_xq"], "xq")
    mix[:, TILES["xo", 0]:TILES["xo", 0] + 4] = a["w_xo"].reshape(L, 4, P, D)
    by_columns(a["w_peer_query"], "pq")
    mix[:, TILES["keys", 0]] = a["peer_sub_keys"].transpose(0, 2, 4, 1, 3).reshape(L, P, D)
    vecs = np.zeros((L, P, NVEC), np.float32)
    for at, name, n in ((G_MIX, "g_mix", 8), (G_XA, "g_xattn", 8), (G_MEM, "g_mem", 8), (G_FFN, "g_ffn", 8),
                        (G_Q, "mla_q_norm", 2), (G_KV, "mla_kv_norm", 1)):
        vecs[:, :, at:at + n] = a[name].reshape(L, n, P).transpose(0, 2, 1)
    vecs[:, :, SINKS:SINKS + 8] = a["swa_sinks"][:, None, :]
    u = a["peer_u"].reshape(L, NK, NK, DC, P).transpose(0, 2, 4, 3, 1)
    v = a["peer_v"].reshape(L, NK, NK, D).transpose(0, 2, 1, 3)
    return {
        "mix_w": mix, "u_t": np.ascontiguousarray(u).reshape(L, NK, P, D), "v_t": np.ascontiguousarray(v), "vecs": vecs,
        "g_final": np.ascontiguousarray(np.broadcast_to(a["g_final"], (P, D))),
        "x_in": np.ascontiguousarray(a["x"].reshape(NT, P, D).transpose(1, 0, 2)),
        "mem_in": np.ascontiguousarray(a["mem"].reshape(NT, P, D).transpose(1, 0, 2)),
    }


def kernel(**inputs):
    import concourse.bacc as bacc
    from concourse.bass_utils import run_bass_kernel_spmd

    arrays = lay_out({k: np.asarray(v) for k, v in inputs.items()})
    arrays["consts"], arrays["tables"] = constants()
    nc = bacc.Bacc("TRN2", target_bir_lowering=False, num_devices=1)
    aps = {n: nc.dram_tensor(n, a.shape, mybir.dt.from_np(a.dtype), kind="ExternalInput").ap() for n, a in arrays.items()}
    out = nc.dram_tensor("out", (P, NT, D), F32, kind="ExternalOutput").ap()
    trunk(nc, **aps, out=out)
    r = run_bass_kernel_spmd(nc, [arrays], core_ids=[0])
    got = r.results[0]["out"]
    return np.ascontiguousarray(got.transpose(1, 0, 2)).reshape(1, SEQ, D)
```
